# Optimizing a Trainium2 kernel written in Bass

```python
import math
import jax, jax.numpy as jnp
from jax import lax
import numpy as np

D_MODEL = 1024
BATCH = 1
SEQ = 1024
DEPTH = 2

CHUNK = 64
N_EVEN = (DEPTH + 1) // 2
N_ODD = DEPTH // 2
RMS_EPS = 1e-6
L2_EPS = 1e-6
F32 = jnp.float32

BRANCH_WIDTH = D_MODEL // 2
MIX_WIDTH = 2 * BRANCH_WIDTH
GDN_HEAD_DIM = 128
GDN_HEADS = BRANCH_WIDTH // GDN_HEAD_DIM
GDN_CONV = 4
SWA_HEAD_DIM = 64
SWA_Q_HEADS = BRANCH_WIDTH // SWA_HEAD_DIM
SWA_KV_HEADS = SWA_Q_HEADS // 4
SWA_KV_WIDTH = SWA_KV_HEADS * SWA_HEAD_DIM
SWA_WINDOW = 128
SWA_WINDOW_CHUNKS = SWA_WINDOW // CHUNK
REL_BUCKETS = 32
REL_MAX_DIST = SWA_WINDOW
S5_GROUP = 16
S5_GROUPS = BRANCH_WIDTH // S5_GROUP
S5_STATE = 64
RWKV_HEAD_DIM = 64
RWKV_HEADS = BRANCH_WIDTH // RWKV_HEAD_DIM
RWKV_DECAY_LORA = 64
RWKV_A_LORA = 64
RWKV_GN_EPS = 64e-5
RWKV_SHIFT_WIDTH = 3 * BRANCH_WIDTH + RWKV_DECAY_LORA + RWKV_A_LORA
EVEN_SIZES = (3 * BRANCH_WIDTH, GDN_HEADS, GDN_HEADS, BRANCH_WIDTH, BRANCH_WIDTH, SWA_KV_WIDTH, SWA_KV_WIDTH, BRANCH_WIDTH)
ODD_SIZES = (BRANCH_WIDTH, BRANCH_WIDTH, RWKV_SHIFT_WIDTH, BRANCH_WIDTH)
EVEN_COLS = sum(EVEN_SIZES)
ODD_COLS = sum(ODD_SIZES)

kernel_name = "hybrid_gdn_swa_s5_rwkv7_encoder"

def split_cols(p, sizes):
    idx = np.cumsum(np.array(sizes))[:-1].tolist()
    return jnp.split(p, idx, axis=-1)

def rms_norm(x, gain):
    xf = x.astype(F32)
    y = xf * lax.rsqrt(jnp.mean(xf * xf, axis=-1, keepdims=True) + RMS_EPS)
    return (y * gain.astype(F32)).astype(x.dtype)

def l2norm(x):
    return x * lax.rsqrt(jnp.sum(x * x, axis=-1, keepdims=True) + L2_EPS)

def causal_depthwise_conv(x, w):
    K, C = w.shape
    return lax.conv_general_dilated(x, w[:, None, :].astype(x.dtype), window_strides=(1,),
                                    padding=[(K - 1, 0)], dimension_numbers=('NWC', 'WIO', 'NWC'),
                                    feature_group_count=C)

def t5_band_buckets():
    i = np.arange(CHUNK)[:, None]
    j = np.arange(SWA_WINDOW_CHUNKS * CHUNK)[None, :]
    rel = j - (SWA_WINDOW_CHUNKS - 1) * CHUNK - i
    half = REL_BUCKETS // 2
    exact = half // 2
    n = np.abs(rel)
    large = exact + (np.log(np.maximum(n, 1) / exact) / np.log(REL_MAX_DIST / exact) * (half - exact)).astype(np.int32)
    large = np.minimum(large, half - 1)
    return ((rel > 0).astype(np.int32) * half + np.where(n < exact, n, large)).astype(np.int32)

def gated_delta_rule(q, k, v, beta_logit, alpha_logit, a_log, dt_bias):
    bsz, T, H, Dh = q.shape
    n_chunks = T // CHUNK
    q = l2norm(q) * (Dh ** -0.5)
    k = l2norm(k)
    beta = jax.nn.sigmoid(beta_logit)
    g = -jnp.exp(a_log) * jax.nn.softplus(alpha_logit + dt_bias)

    def to_chunks(t):
        return t.reshape(bsz, n_chunks, CHUNK, H, -1).transpose(0, 1, 3, 2, 4)

    qc, kc, vc = to_chunks(q), to_chunks(k), to_chunks(v)
    bc = to_chunks(beta[..., None])[..., 0]
    gc = jnp.cumsum(to_chunks(g[..., None])[..., 0], axis=-1)
    pos = jnp.arange(CHUNK)
    causal = pos[:, None] >= pos[None, :]
    strict = pos[:, None] > pos[None, :]
    decay = jnp.exp(jnp.where(causal, gc[..., :, None] - gc[..., None, :], -jnp.inf))
    k_beta = kc * bc[..., None]
    l_mat = jnp.where(strict, jnp.einsum('bnhid,bnhjd->bnhij', k_beta, kc) * decay, 0.0)
    m_mat = jnp.eye(CHUNK, dtype=F32) + l_mat
    rhs = jnp.concatenate([vc * bc[..., None], k_beta * jnp.exp(gc)[..., None]], axis=-1)
    sol = lax.linalg.triangular_solve(m_mat, rhs, left_side=True, lower=True, unit_diagonal=True)
    u_c, w_c = sol[..., :Dh], sol[..., Dh:]
    qk = jnp.einsum('bnhid,bnhjd->bnhij', qc, kc) * decay
    q_g = qc * jnp.exp(gc)[..., None]
    k_tail = kc * jnp.exp(gc[..., -1:] - gc)[..., None]
    g_last = jnp.exp(gc[..., -1])

    def step(S, inp):
        u_i, w_i, qk_i, qg_i, kt_i, gl_i = inp
        v_new = u_i - jnp.einsum('bhcd,bhde->bhce', w_i, S)
        o = jnp.einsum('bhcd,bhde->bhce', qg_i, S) + jnp.einsum('bhij,bhje->bhie', qk_i, v_new)
        S = S * gl_i[..., None, None] + jnp.einsum('bhcd,bhce->bhde', kt_i, v_new)
        return S, o

    xs = tuple(jnp.moveaxis(t, 1, 0) for t in (u_c, w_c, qk, q_g, k_tail, g_last))
    S0 = jnp.zeros((bsz, H, Dh, Dh), F32)
    _, o = lax.scan(step, S0, xs)
    return o.transpose(1, 0, 3, 2, 4).reshape(bsz, T, H, Dh)

def sliding_window_attention(q, k, v, q_gain, k_gain, sinks, band_bias):
    bsz, T, Hq, Dh = q.shape
    Hkv = k.shape[2]
    G = Hq // Hkv
    n_chunks = T // CHUNK
    lookback = SWA_WINDOW_CHUNKS - 1
    q = rms_norm(q.astype(F32), q_gain) * (Dh ** -0.5)
    k = rms_norm(k.astype(F32), k_gain)
    v = v.astype(F32)
    qb = q.reshape(bsz, n_chunks, CHUNK, Hkv, G, Dh)
    kb = k.reshape(bsz, n_chunks, CHUNK, Hkv, Dh)
    vb = v.reshape(bsz, n_chunks, CHUNK, Hkv, Dh)

    def band(t):
        parts = [jnp.pad(t, ((0, 0), (s, 0), (0, 0), (0, 0), (0, 0)))[:, :n_chunks] for s in range(lookback, 0, -1)]
        return jnp.concatenate(parts + [t], axis=2)

    kw, vw = band(kb), band(vb)
    s = jnp.einsum('bnqhgd,bnkhd->bnhgqk', qb, kw) + band_bias.reshape(Hkv, G, CHUNK, SWA_WINDOW_CHUNKS * CHUNK)
    key_block = jnp.arange(SWA_WINDOW_CHUNKS * CHUNK) // CHUNK
    valid = (jnp.arange(n_chunks)[:, None] - (lookback - key_block)[None, :]) >= 0
    s = jnp.where(valid[None, :, None, None, None, :], s, -jnp.inf)
    sink = sinks.astype(F32).reshape(Hkv, G)[None, None, :, :, None, None]
    m = jnp.maximum(jnp.max(s, axis=-1, keepdims=True), sink)
    p = jnp.exp(s - m)
    p = p / (jnp.sum(p, axis=-1, keepdims=True) + jnp.exp(sink - m))
    o = jnp.einsum('bnhgqk,bnkhd->bnqhgd', p, vw)
    return o.reshape(bsz, T, Hq * Dh)

def s5_ssm(u, lam_re, lam_im, log_step, b_re, b_im, c_re, c_im):
    bsz, T, _ = u.shape
    G, P = lam_re.shape
    n_chunks = T // CHUNK
    lam_re, lam_im = lam_re.astype(F32), lam_im.astype(F32)
    b_re, b_im, c_re, c_im = (t.astype(F32) for t in (b_re, b_im, c_re, c_im))
    dt = jnp.exp(log_step.astype(F32))[:, None]
    ar, ai = lam_re * dt, lam_im * dt
    mag = jnp.exp(ar)
    lb_re, lb_im = mag * jnp.cos(ai), mag * jnp.sin(ai)
    den = lam_re * lam_re + lam_im * lam_im
    nr, ni = lb_re - 1.0, lb_im
    f_re = (nr * lam_re + ni * lam_im) / den
    f_im = (ni * lam_re - nr * lam_im) / den
    bb_re = f_re[..., None] * b_re - f_im[..., None] * b_im
    bb_im = f_re[..., None] * b_im + f_im[..., None] * b_re
    tt = jnp.arange(1, CHUNK + 1, dtype=F32)[:, None, None]
    pw_mag = jnp.exp(tt * ar)
    pw_re, pw_im = pw_mag * jnp.cos(tt * ai), pw_mag * jnp.sin(tt * ai)
    a_re = jnp.broadcast_to(lb_re, (bsz, CHUNK, G, P))
    a_im = jnp.broadcast_to(lb_im, (bsz, CHUNK, G, P))

    def combine(e1, e2):
        a1r, a1i, b1r, b1i = e1
        a2r, a2i, b2r, b2i = e2
        return (a2r * a1r - a2i * a1i, a2r * a1i + a2i * a1r,
                a2r * b1r - a2i * b1i + b2r, a2r * b1i + a2i * b1r + b2i)

    def step(h, u_i):
        h_re, h_im = h
        bu_re = jnp.einsum('bcgj,gpj->bcgp', u_i, bb_re)
        bu_im = jnp.einsum('bcgj,gpj->bcgp', u_i, bb_im)
        _, _, s_re, s_im = lax.associative_scan(combine, (a_re, a_im, bu_re, bu_im), axis=1)
        s_re = s_re + pw_re * h_re[:, None] - pw_im * h_im[:, None]
        s_im = s_im + pw_re * h_im[:, None] + pw_im * h_re[:, None]
        y = jnp.einsum('bcgp,gjp->bcgj', s_re, c_re) - jnp.einsum('bcgp,gjp->bcgj', s_im, c_im)
        return (s_re[:, -1], s_im[:, -1]), y

    uc = u.reshape(bsz, n_chunks, CHUNK, G, S5_GROUP).transpose(1, 0, 2, 3, 4)
    h0 = (jnp.zeros((bsz, G, P), F32), jnp.zeros((bsz, G, P), F32))
    _, y = lax.scan(step, h0, uc)
    return y.transpose(1, 0, 2, 3, 4).reshape(bsz, T, G * S5_GROUP)

def rwkv7_time_mix(r, k, v, wd, ad, w0, w2, a0, a2, k_k, k_a, r_k, ln_w, ln_b):
    bsz, T, W = r.shape
    H, Dh = RWKV_HEADS, RWKV_HEAD_DIM
    w = -jax.nn.softplus(-(w0 + jnp.tanh(wd) @ w2)) - 0.5
    decay = jnp.exp(-jnp.exp(w))
    a = jax.nn.sigmoid(a0 + ad @ a2)
    kk = l2norm((k * k_k).reshape(bsz, T, H, Dh))
    k = k * (1.0 + (a - 1.0) * k_a)
    rh, kh, vh, wh, ah = (t.reshape(bsz, T, H, Dh) for t in (r, k, v, decay, a))
    a_vec, b_vec = -kk, kk * ah

    def step(S, inp):
        r_t, w_t, k_t, v_t, a_t, b_t = inp
        sa = jnp.einsum('bhvk,bhk->bhv', S, a_t)
        S = S * w_t[:, :, None, :] + sa[..., None] * b_t[:, :, None, :] + v_t[..., None] * k_t[:, :, None, :]
        return S, jnp.einsum('bhvk,bhk->bhv', S, r_t)

    xs = tuple(jnp.moveaxis(t, 1, 0) for t in (rh, wh, kh, vh, a_vec, b_vec))
    _, y = lax.scan(step, jnp.zeros((bsz, H, Dh, Dh), F32), xs)
    y = jnp.moveaxis(y, 0, 1)
    mu = jnp.mean(y, axis=-1, keepdims=True)
    var = jnp.mean(jnp.square(y - mu), axis=-1, keepdims=True)
    y = ((y - mu) * lax.rsqrt(var + RWKV_GN_EPS)).reshape(bsz, T, W) * ln_w + ln_b
    bonus = jnp.sum(rh * kh * r_k, axis=-1, keepdims=True) * vh
    return y + bonus.reshape(bsz, T, W)

def even_layer(x, norm_g, w_in, conv_w, a_log, dt_bias, out_norm, q_gain, k_gain, sinks, w_out, band_bias):
    bsz, T, _ = x.shape
    p = rms_norm(x, norm_g) @ w_in
    qkv_a, beta_l, alpha_l, z_a, q_b, k_b, v_b, z_b = split_cols(p, EVEN_SIZES)
    qkv_a = jax.nn.silu(causal_depthwise_conv(qkv_a, conv_w)).astype(F32)
    q_a, k_a, v_a = (t.reshape(bsz, T, GDN_HEADS, GDN_HEAD_DIM) for t in jnp.split(qkv_a, 3, axis=-1))
    o_a = gated_delta_rule(q_a, k_a, v_a, beta_l.astype(F32), alpha_l.astype(F32),
                           a_log.astype(F32), dt_bias.astype(F32))
    o_a = rms_norm(o_a, out_norm) * jax.nn.silu(z_a.astype(F32)).reshape(bsz, T, GDN_HEADS, GDN_HEAD_DIM)
    o_b = sliding_window_attention(q_b.reshape(bsz, T, SWA_Q_HEADS, SWA_HEAD_DIM),
                                   k_b.reshape(bsz, T, SWA_KV_HEADS, SWA_HEAD_DIM),
                                   v_b.reshape(bsz, T, SWA_KV_HEADS, SWA_HEAD_DIM),
                                   q_gain, k_gain, sinks, band_bias)
    o_b = o_b * jax.nn.silu(z_b.astype(F32))
    mixed = jnp.concatenate([o_a.reshape(bsz, T, BRANCH_WIDTH), o_b], axis=-1).astype(x.dtype)
    return x + mixed @ w_out

def odd_layer(x, norm_g, w_in, lam_re, lam_im, log_step, b_re, b_im, c_re, c_im, d_skip, w_glu,
              mu, w0, w2, a0, a2, k_k, k_a, r_k, ln_w, ln_b, w_out):
    p = rms_norm(x, norm_g) @ w_in
    u, z_c, feat, z_d = split_cols(p, ODD_SIZES)
    u = u.astype(F32)
    y_c = jax.nn.gelu(s5_ssm(u, lam_re, lam_im, log_step, b_re, b_im, c_re, c_im) + d_skip.astype(F32) * u)
    g_a, g_b = jnp.split(y_c @ w_glu.astype(F32), 2, axis=-1)
    o_c = g_a * jax.nn.sigmoid(g_b) * jax.nn.silu(z_c.astype(F32))
    feat = feat.astype(F32)
    prev = jnp.pad(feat, ((0, 0), (1, 0), (0, 0)))[:, :-1]
    feat = feat + (prev - feat) * mu.astype(F32)
    r, k, v, wd, ad = split_cols(feat, (BRANCH_WIDTH, BRANCH_WIDTH, BRANCH_WIDTH, RWKV_DECAY_LORA, RWKV_A_LORA))
    o_d = rwkv7_time_mix(r, k, v, wd, ad, w0.astype(F32), w2.astype(F32), a0.astype(F32), a2.astype(F32),
                         k_k.astype(F32), k_a.astype(F32), r_k.astype(F32), ln_w.astype(F32), ln_b.astype(F32))
    o_d = o_d * jax.nn.silu(z_d.astype(F32))
    mixed = jnp.concatenate([o_c, o_d], axis=-1).astype(x.dtype)
    return x + mixed @ w_out

def setup_inputs(seed: int = 0) -> dict:
    key = jax.random.key(seed)
    ks = iter(list(jax.random.split(key, 48)))
    nrm = lambda shape, std: std * jax.random.normal(next(ks), shape, F32)
    uni = lambda shape, lo, hi: jax.random.uniform(next(ks), shape, F32, lo, hi)
    NE, NO, W = N_EVEN, N_ODD, BRANCH_WIDTH
    x = nrm((BATCH, SEQ, D_MODEL), 1.0)
    even_norm = 1.0 + nrm((NE, D_MODEL), 0.02)
    even_w_in = nrm((NE, D_MODEL, EVEN_COLS), D_MODEL ** -0.5)
    gdn_conv_w = nrm((NE, GDN_CONV, 3 * W), GDN_CONV ** -0.5)
    gdn_a_log = jnp.log(uni((NE, GDN_HEADS), 1.0, 16.0))
    dt = jnp.exp(uni((NE, GDN_HEADS), math.log(1e-3), math.log(1e-1)))
    gdn_dt_bias = dt + jnp.log(-jnp.expm1(-dt))
    gdn_out_norm = 1.0 + nrm((NE, GDN_HEAD_DIM), 0.02)
    swa_q_norm = 1.0 + nrm((NE, SWA_HEAD_DIM), 0.02)
    swa_k_norm = 1.0 + nrm((NE, SWA_HEAD_DIM), 0.02)
    swa_sinks = nrm((NE, SWA_Q_HEADS), 0.5)
    even_w_out = nrm((NE, MIX_WIDTH, D_MODEL), MIX_WIDTH ** -0.5)
    rel_bias = nrm((REL_BUCKETS, SWA_Q_HEADS), 0.1)
    odd_norm = 1.0 + nrm((NO, D_MODEL), 0.02)
    odd_w_in = nrm((NO, D_MODEL, ODD_COLS), D_MODEL ** -0.5)
    s5_lambda_re = -0.5 + nrm((NO, S5_GROUPS, S5_STATE), 0.01)
    s5_lambda_im = math.pi * jnp.arange(S5_STATE, dtype=F32) + nrm((NO, S5_GROUPS, S5_STATE), 0.01)
    s5_log_step = uni((NO, S5_GROUPS), math.log(1e-3), math.log(1e-1))
    s5_b_re = nrm((NO, S5_GROUPS, S5_STATE, S5_GROUP), (2 * S5_GROUP) ** -0.5)
    s5_b_im = nrm((NO, S5_GROUPS, S5_STATE, S5_GROUP), (2 * S5_GROUP) ** -0.5)
    s5_c_re = nrm((NO, S5_GROUPS, S5_GROUP, S5_STATE), S5_STATE ** -0.5)
    s5_c_im = nrm((NO, S5_GROUPS, S5_GROUP, S5_STATE), S5_STATE ** -0.5)
    s5_d = nrm((NO, W), 1.0)
    s5_w_glu = nrm((NO, W, 2 * W), W ** -0.5)
    rwkv_mu = uni((NO, RWKV_SHIFT_WIDTH), 0.0, 1.0)
    rwkv_w0 = uni((NO, W), -6.0, -1.0)
    rwkv_w2 = nrm((NO, RWKV_DECAY_LORA, W), 0.1)
    rwkv_a0 = nrm((NO, W), 0.1)
    rwkv_a2 = nrm((NO, RWKV_A_LORA, W), RWKV_A_LORA ** -0.5)
    rwkv_k_k = 0.85 + nrm((NO, W), 0.02)
    rwkv_k_a = 1.0 + nrm((NO, W), 0.02)
    rwkv_r_k = nrm((NO, RWKV_HEADS, RWKV_HEAD_DIM), 0.1)
    rwkv_ln_w = 1.0 + nrm((NO, W), 0.02)
    rwkv_ln_b = nrm((NO, W), 0.02)
    odd_w_out = nrm((NO, MIX_WIDTH, D_MODEL), MIX_WIDTH ** -0.5)
    return {"x": x, "even_norm": even_norm, "even_w_in": even_w_in, "gdn_conv_w": gdn_conv_w,
            "gdn_a_log": gdn_a_log, "gdn_dt_bias": gdn_dt_bias, "gdn_out_norm": gdn_out_norm,
            "swa_q_norm": swa_q_norm, "swa_k_norm": swa_k_norm, "swa_sinks": swa_sinks,
            "even_w_out": even_w_out, "rel_bias": rel_bias, "odd_norm": odd_norm, "odd_w_in": odd_w_in,
            "s5_lambda_re": s5_lambda_re, "s5_lambda_im": s5_lambda_im, "s5_log_step": s5_log_step,
            "s5_b_re": s5_b_re, "s5_b_im": s5_b_im, "s5_c_re": s5_c_re, "s5_c_im": s5_c_im,
            "s5_d": s5_d, "s5_w_glu": s5_w_glu, "rwkv_mu": rwkv_mu, "rwkv_w0": rwkv_w0,
            "rwkv_w2": rwkv_w2, "rwkv_a0": rwkv_a0, "rwkv_a2": rwkv_a2, "rwkv_k_k": rwkv_k_k,
            "rwkv_k_a": rwkv_k_a, "rwkv_r_k": rwkv_r_k, "rwkv_ln_w": rwkv_ln_w, "rwkv_ln_b": rwkv_ln_b,
            "odd_w_out": odd_w_out}

def reference(x, even_norm, even_w_in, gdn_conv_w, gdn_a_log, gdn_dt_bias, gdn_out_norm,
              swa_q_norm, swa_k_norm, swa_sinks, even_w_out, rel_bias, odd_norm, odd_w_in,
              s5_lambda_re, s5_lambda_im, s5_log_step, s5_b_re, s5_b_im, s5_c_re, s5_c_im,
              s5_d, s5_w_glu, rwkv_mu, rwkv_w0, rwkv_w2, rwkv_a0, rwkv_a2, rwkv_k_k,
              rwkv_k_a, rwkv_r_k, rwkv_ln_w, rwkv_ln_b, odd_w_out):
    band_bias = jnp.take(rel_bias.astype(F32), jnp.asarray(t5_band_buckets()), axis=0).transpose(2, 0, 1)
    h = x
    for layer in range(DEPTH):
        i = layer // 2
        if layer % 2 == 0:
            h = even_layer(h, even_norm[i], even_w_in[i], gdn_conv_w[i], gdn_a_log[i], gdn_dt_bias[i],
                           gdn_out_norm[i], swa_q_norm[i], swa_k_norm[i], swa_sinks[i], even_w_out[i], band_bias)
        else:
            h = odd_layer(h, odd_norm[i], odd_w_in[i], s5_lambda_re[i], s5_lambda_im[i], s5_log_step[i],
                          s5_b_re[i], s5_b_im[i], s5_c_re[i], s5_c_im[i], s5_d[i], s5_w_glu[i],
                          rwkv_mu[i], rwkv_w0[i], rwkv_w2[i], rwkv_a0[i], rwkv_a2[i], rwkv_k_k[i],
                          rwkv_k_a[i], rwkv_r_k[i], rwkv_ln_w[i], rwkv_ln_b[i], odd_w_out[i])
    return h


_drawn_inputs = setup_inputs


def setup_inputs(seed=0):
    import zlib

    import numpy as np

    out = dict(_drawn_inputs(seed))
    spreads = {}
    factors = {'even_norm': 3.355,
     'gdn_out_norm': 5.818,
     'swa_q_norm': 8.0,
     'swa_k_norm': 8.0,
     'swa_sinks': 8.0,
     'rel_bias': 8.0,
     'odd_norm': 3.556,
     's5_lambda_re': 64.0,
     's5_lambda_im': 39.536,
     's5_log_step': 40.144,
     's5_b_re': 55.312,
     's5_b_im': 56.0,
     's5_c_re': 56.184,
     's5_c_im': 55.024,
     'rwkv_w2': 3.77,
     'rwkv_a0': 4.348,
     'rwkv_k_k': 60.832,
     'rwkv_k_a': 7.141,
     'rwkv_ln_w': 59.304,
     'rwkv_ln_b': 61.472,
     's5_d': 3.719,
     's5_w_glu': 3.221}
    for name, (base, spread) in spreads.items():
        noise = np.random.default_rng([zlib.crc32(name.encode()), seed]).standard_normal(out[name].shape)
        drawn = base * np.exp(spread * noise) if base else spread * noise
        out[name] = __import__('jax').numpy.asarray(drawn.astype(out[name].dtype))
    for name, factor in factors.items():
        out[name] = (out[name] * factor).astype(out[name].dtype)
    return out
```

```python
from contextlib import ExitStack
import math

import numpy as np
import concourse.bass as bass
from concourse import mybir

F32 = mybir.dt.float32
I32 = mybir.dt.int32
ALU = mybir.AluOpType
ACT = mybir.ActivationFunctionType
AX = mybir.AxisListType.X

D, T, P = 1024, 1024, 128
KT = D // P
NT = T // P
W = D // 2
WB = W // P
HG = 4
RMS_EPS, L2_EPS, GN_EPS = 1e-6, 1e-6, 64e-5
EVEN = dict(q=0, k=W, v=2 * W, beta=3 * W, za=3 * W + 2 * HG, qb=4 * W + 2 * HG, kb=5 * W + 2 * HG,
            vb=5 * W + 2 * HG + P, zb=5 * W + 2 * HG + 2 * P)
EVEN_COLS = 6 * W + 2 * HG + 2 * P
ODD = dict(u=0, zc=W, r=2 * W, k=3 * W, v=4 * W, wa=5 * W, zd=5 * W + P)
ODD_COLS = 6 * W + P
NEG = -1.0e30
LEVELS = (1, 2, 4, 8, 16, 32, 64)

C_ID, C_ONE, C_ONE2 = 0, 128, 256
C_UT0 = C_M4 = 384

C_LEV = 896
C_HOT = C_LEV + 128 * len(LEVELS)
C_START = C_HOT + 192
C_ALL = C_START + 1024


def constants():
    c = np.zeros((P, C_ALL), np.float32)
    j, i = np.arange(P)[:, None], np.arange(P)[None, :]
    c[:, C_ID:C_ID + P] = j == i
    c[:, C_ONE:C_ONE + P] = 1
    c[:, C_ONE2:C_ONE2 + P] = j // 64 == i // 64
    for m in range(2):
        c[:, C_M4 + 256 * m:C_M4 + 256 * m + P] = j <= i
        c[:, C_M4 + 256 * m + P:C_M4 + 256 * m + 2 * P] = j < i
    for n, s in enumerate(LEVELS):
        c[:, C_LEV + P * n:C_LEV + P * (n + 1)] = (j // (2 * s) == i // (2 * s)) & (j % (2 * s) < s) & (i % (2 * s) >= s)
    rel = 63 - np.arange(191)
    half, exact = 16, 8
    n = np.abs(rel)
    large = exact + (np.log(np.maximum(n, 1) / exact) / np.log(128 / exact) * (half - exact)).astype(np.int32)
    bucket = (rel > 0) * half + np.where(n < exact, n, np.minimum(large, half - 1))
    c[bucket, C_HOT + np.arange(191)] = 1
    c[:, C_START:] = np.arange(T) % P != 0
    return c


class Core:

    def __init__(self, nc, ctx):
        self.nc, self.ctx = nc, ctx
        self.n_sem = 0
        self.taken = []
        self.output_stored = [nc.alloc_semaphore(name=f"output_stored{i}") for i in range(3)]
        ctx.enter_context(nc.allow_non_contiguous_dma(reason="per-channel vectors"))
        self.sb = ctx.enter_context(nc.sbuf_tensor("arena", [P, 53184], F32))
        self.ps = ctx.enter_context(nc.psum_tensor("banks", [P, 8, 512], F32))

    def sem(self, name):
        handle = self.nc.alloc_semaphore(name=name)
        self.n_sem += 1
        self.taken.append(handle)
        return handle

    def end_part(self):
        with self.nc.Block() as block:
            @block.gpsimd
            def _(pool):
                for handle in self.taken:
                    pool.sem_clear(handle)
        for handle in self.taken:
            self.nc.release_semaphore(handle)
        self.taken = []

    def at(self, col, shape, rows=(0, P)):
        n = int(np.prod(shape))
        v = self.sb[rows[0]:rows[1], col:col + n]
        if len(shape) == 1:
            return v
        names = "abcd"[:len(shape)]
        return v.rearrange(f"p ({' '.join(names)}) -> p {' '.join(names)}", **{x: s for x, s in zip(names[1:], shape[1:])})


A_CST = 0
A_MISC = 3200
A_BIG = 4224
A_F = [20608 + 4096 * i for i in range(7)]
A_T = 49280


class Chain:

    def __init__(self, eng, sem):
        self.eng, self.sem, self.n = eng, sem, 0

    def __call__(self, ins):
        self.n += 1
        ins.then_inc(self.sem, 1)
        self.eng.wait_ge(self.sem, self.n)


def bc(ap, n):
    p, a = ap.shape
    return ap.rearrange("p (a o) -> p a o", o=1).to_broadcast([p, a, n])


def norm_transpose(co, tag, src, gain):
    nc = co.nc
    xt = co.at(A_BIG, (KT, T))
    ring = [co.at(A_F[0] + 1024 * i, (D,)) for i in range(4)]
    junk = co.at(A_T, (D,))
    gn = co.at(A_MISC, (KT,))
    ss, sd, rs = (co.at(A_MISC + 8 + 8 * i, (NT,)) for i in range(3))
    ident = co.at(A_CST + C_ID, (P,))
    loaded = [co.sem(f"{tag}_loaded{i}") for i in range(4)]
    gained, squared, rooted, scaled, turned, placed, dch, ach = (
        co.sem(f"{tag}_{x}") for x in ("gain", "squared", "rooted", "scaled", "turned", "placed", "dch", "ach"))
    with nc.Block() as block:
        @block.sync
        def _(sp):
            sp.dma_start(gn, gain.rearrange("(k p) -> p k", p=P)).then_inc(gained, 16)
            for i in range(NT):
                if i >= 4:
                    sp.wait_ge(turned, 2 * (i - 3))
                sp.dma_start(ring[i % 4], src[i * P:(i + 1) * P, :]).then_inc(loaded[i % 4], 16)

        @block.scalar
        def _(act):
            link = Chain(act, ach)
            for i in range(NT):
                act.wait_ge(loaded[i % 4], 16 * (i // 4 + 1))
                link(nc.scalar.activation(junk, ring[i % 4], ACT.Square, accum_out=ss[:, i:i + 1]))
                act.wait_ge(squared, i + 1)
                nc.scalar.activation(sd[:, i:i + 1], ss[:, i:i + 1], ACT.Sqrt).then_inc(rooted, 1)

        @block.vector
        def _(dve):
            link = Chain(dve, dch)
            dve.wait_ge(gained, 16)
            for i in range(NT):
                dve.wait_ge(ach, i + 1)
                nc.vector.tensor_scalar(ss[:, i:i + 1], ss[:, i:i + 1], 1.0 / D, RMS_EPS, ALU.mult, ALU.add).then_inc(squared, 1)
                dve.wait_ge(rooted, i + 1)
                link(nc.vector.reciprocal(rs[:, i:i + 1], sd[:, i:i + 1]))
                nc.vector.tensor_scalar(ring[i % 4], ring[i % 4], rs[:, i:i + 1], None, ALU.mult).then_inc(scaled, 1)
                for h in range(2):
                    dve.wait_ge(turned, 2 * i + h + 1)
                    bank = (2 * i + h) % 8
                    nc.vector.tensor_tensor(xt[:, 4 * h:4 * h + 4, i * P:(i + 1) * P],
                                            co.ps[:, bank, :].rearrange("p (k t) -> p k t", t=P),
                                            bc(gn[:, 4 * h:4 * h + 4], P), ALU.mult).then_inc(placed, 1)

        @block.tensor
        def _(pe):
            for i in range(NT):
                pe.wait_ge(scaled, i + 1)
                for h in range(2):
                    n = 2 * i + h
                    if n >= 8:
                        pe.wait_ge(placed, n - 7)
                    for k in range(4):
                        last = nc.tensor.transpose(co.ps[:, n % 8, k * P:(k + 1) * P],
                                                   ring[i % 4][:, (4 * h + k) * P:(4 * h + k + 1) * P], ident)
                    last.then_inc(turned, 1)


def project(co, tag, w, blocks, conv_w=None, small=None, mu=None):
    nc = co.nc
    xt = co.at(A_BIG, (KT, T))
    NW = 3
    wr = [co.at(A_BIG + 8192 + 1024 * i, (KT, P)) for i in range(NW)]
    RAW = T + 4
    raw = [co.at(A_BIG + 8192 + 3072 + RAW * i, (RAW,)) for i in range(2)]
    tmp = [co.at(A_T + 1024 * i, (T,)) for i in range(2)]
    cw = co.at(A_MISC + 64, (12, 4))
    mus = co.at(A_MISC + 64, (13,))
    wsmall = co.at(A_MISC + 128, (KT, 8))
    loaded = [co.sem(f"{tag}_w{i}") for i in range(NW)]
    cw_in, small_in, cw_half, multiplied, evacuated, convolved, tanhed, finished, small_done, small_out, pads, dch = (
        co.sem(f"{tag}_{x}") for x in ("cw_in", "small_in", "cw_half", "multiplied", "evacuated", "convolved", "tanhed",
                                       "finished", "small_done", "small_out", "pads", "dch"))
    conv_no, gate_no, post_no = {}, {}, {}
    for n, (_, kind, _) in enumerate(blocks):
        if kind in ("conv", "shift"):
            conv_no[n] = len(conv_no)
        if kind in ("conv", "gate"):
            post_no[n] = len(post_no)
    NB = len(blocks)
    with nc.Block() as block:
        @block.sync
        def _(sp):
            if conv_w is not None:
                for j in range(4):
                    sp.dma_start(cw[:, :, j], conv_w[j, :].rearrange("(b p) -> p b", p=P)).then_inc(cw_in, 16)
            if mu is not None:
                sp.dma_start(mus, mu.rearrange("(b p) -> p b", p=P)).then_inc(cw_in, 16)
            if small is not None:
                sp.dma_start(wsmall[:, :, 0:small[1]], w[:, small[0]:small[0] + small[1]].rearrange("(k p) n -> p k n", p=P)).then_inc(small_in, 16)
            for n, (col, _, _) in enumerate(blocks):
                if n >= NW:
                    sp.wait_ge(multiplied, n - NW + 1)
                sp.dma_start(wr[n % NW], w[:, col:col + P].rearrange("(k p) n -> p k n", p=P)).then_inc(loaded[n % NW], 16)

        @block.tensor
        def _(pe):
            if small is not None:
                pe.wait_ge(small_in, 16)
                for t in range(NT):
                    for k in range(KT):
                        last = nc.tensor.matmul(co.ps[:, 7, t * small[1]:(t + 1) * small[1]], xt[:, k, t * P:(t + 1) * P],
                                                wsmall[:, k, 0:small[1]], start=k == 0, stop=k == KT - 1)
                last.then_inc(small_done, 1)
            for n in range(NB):
                pe.wait_ge(loaded[n % NW], 16 * (n // NW + 1))
                if n >= 2:
                    pe.wait_ge(evacuated, n - 1)
                for h in range(2):
                    for k in range(KT):
                        last = nc.tensor.matmul(co.ps[:, 2 * (n % 2) + h, :], wr[n % NW][:, k, :], xt[:, k, h * 512:(h + 1) * 512],
                                                start=k == 0, stop=k == KT - 1)
                last.then_inc(multiplied, 1)

        @block.scalar
        def _(act):
            if small is not None:
                act.wait_ge(small_done, 1)
                nc.scalar.activation(small[2], co.ps[:, 7, 0:NT * small[1]].rearrange("p (t n) -> p t n", t=NT), ACT.Copy).then_inc(small_out, 1)
            for n, (_, kind, dst) in enumerate(blocks):
                out = raw[conv_no[n] % 2][:, 4:4 + T] if n in conv_no else dst
                if conv_no.get(n, 0) >= 2:
                    act.wait_ge(convolved, conv_no[n] - 1)
                act.wait_ge(multiplied, n + 1)
                nc.scalar.activation(out.rearrange("p (h t) -> p h t", h=2), co.ps[:, 2 * (n % 2):2 * (n % 2) + 2, :], ACT.Copy,
                                     scale=0.5 if kind == "gate" else 1.0).then_inc(evacuated, 1)
                if kind == "conv":
                    act.wait_ge(convolved, conv_no[n] + 1)
                if n in post_no:
                    act.wait_ge(evacuated, n + 1)
                    if post_no[n] >= 2:
                        act.wait_ge(finished, post_no[n] - 1)
                    nc.scalar.activation(tmp[post_no[n] % 2], dst, ACT.Tanh).then_inc(tanhed, 1)

        @block.gpsimd
        def _(pool):
            for r in raw:
                nc.gpsimd.memset(r[:, 0:4], 0.0).then_inc(pads, 1)

        @block.vector
        def _(dve):
            link = Chain(dve, dch)
            dve.wait_ge(pads, 2)
            if mu is not None:
                dve.wait_ge(cw_in, 16)
            if conv_w is not None:
                dve.wait_ge(cw_in, 64)
                nc.vector.tensor_scalar(cw, cw, 0.5, None, ALU.mult).then_inc(cw_half, 1)
                dve.wait_ge(cw_half, 1)
            for n, (_, kind, dst) in enumerate(blocks):
                if kind == "shift":
                    dve.wait_ge(evacuated, n + 1)
                    c = conv_no[n]
                    x = raw[c % 2]
                    link(nc.vector.tensor_tensor(dst, x[:, 3:3 + T], x[:, 4:4 + T], ALU.subtract))
                    nc.vector.scalar_tensor_tensor(dst, dst, mus[:, c:c + 1], x[:, 4:4 + T], ALU.mult, ALU.add).then_inc(convolved, 1)
                if kind == "conv":
                    dve.wait_ge(evacuated, n + 1)
                    c = conv_no[n]
                    x = raw[c % 2]
                    link(nc.vector.tensor_scalar(dst, x[:, 4:4 + T], cw[:, c, 3:4], None, ALU.mult))
                    link(nc.vector.scalar_tensor_tensor(dst, x[:, 3:3 + T], cw[:, c, 2:3], dst, ALU.mult, ALU.add))
                    link(nc.vector.scalar_tensor_tensor(dst, x[:, 2:2 + T], cw[:, c, 1:2], dst, ALU.mult, ALU.add))
                    nc.vector.scalar_tensor_tensor(dst, x[:, 1:1 + T], cw[:, c, 0:1], dst, ALU.mult, ALU.add).then_inc(convolved, 1)
                if n in post_no:
                    dve.wait_ge(tanhed, post_no[n] + 1)
                    nc.vector.scalar_tensor_tensor(dst, tmp[post_no[n] % 2], 1.0, dst, ALU.add, ALU.mult).then_inc(finished, 1)


def norm_blocks(co, tag, items, t0=A_T):
    nc = co.nc
    sq = [co.at(t0 + 1024 * i, (T,)) for i in range(2)]
    squared, summed, rooted, normed, dch = (co.sem(f"{tag}_{x}") for x in ("squared", "summed", "rooted", "normed", "dch"))
    with nc.Block() as block:
        @block.gpsimd
        def _(pool):
            for n, (x, *_) in enumerate(items):
                if n >= 2:
                    pool.wait_ge(normed, n - 1)
                nc.gpsimd.tensor_tensor(sq[n % 2], x, x, ALU.mult).then_inc(squared, 1)

        @block.tensor
        def _(pe):
            for n, (x, group, *_) in enumerate(items):
                pe.wait_ge(squared, n + 1)
                if n >= 4:
                    pe.wait_ge(rooted, n - 3)
                ones = co.at(A_CST + (C_ONE if group == 128 else C_ONE2), (P,))
                for h in range(2):
                    last = nc.tensor.matmul(co.ps[:, 2 * (n % 4) + h, :], ones, sq[n % 2][:, h * 512:(h + 1) * 512], start=True, stop=True)
                last.then_inc(summed, 1)

        @block.scalar
        def _(act):
            for n, (x, group, scale, eps, gain) in enumerate(items):
                act.wait_ge(summed, n + 1)
                nc.scalar.activation(sq[n % 2].rearrange("p (h t) -> p h t", h=2), co.ps[:, 2 * (n % 4):2 * (n % 4) + 2, :], ACT.Sqrt,
                                     bias=co.at(co.eps_at[eps], (1,)), scale=scale).then_inc(rooted, 1)

        @block.vector
        def _(dve):
            link = Chain(dve, dch)
            for n, (x, group, scale, eps, gain) in enumerate(items):
                dve.wait_ge(rooted, n + 1)
                link(nc.vector.reciprocal(sq[n % 2], sq[n % 2]))
                nc.vector.scalar_tensor_tensor(x, x, gain, sq[n % 2], ALU.mult, ALU.mult).then_inc(normed, 1)


def invert(co, tag, store, xv_at, nl_at, yy_at):
    nc = co.nc
    G, NG = 4, 8
    ident = co.at(A_CST + C_ID, (P,))
    xv = [co.at(x, (G, 2, P)) for x in xv_at]
    nl = [co.at(x, (G, P)) for x in nl_at]
    yy = [co.at(x, (G, P)) for x in yy_at]
    L = len(LEVELS)
    steps = L - 1
    masked, first, began, ymade, ycopied, zmade, updated, pch = (
        co.sem(f"{tag}_{x}") for x in ("masked", "first", "began", "ymade", "ycopied", "zmade", "updated", "pch"))
    ident_b = ident.rearrange("p (o t) -> p o t", o=1).to_broadcast([P, G, P])

    def level(n):
        return co.at(A_CST + C_LEV + P * n, (P,)).rearrange("p (o t) -> p o t", o=1).to_broadcast([P, G, P])

    def n_of(g):
        return store[:, G * g:G * g + G, :]

    with nc.Block() as block:
        @block.gpsimd
        def _(pool):
            for q in range(NG // 2):
                for l in range(L):
                    for s in range(2):
                        g = 2 * q + s
                        if l == 1:
                            pool.wait_ge(began, g + 1)
                        elif l > 1:
                            pool.wait_ge(ymade, (q * steps + l - 2) * 2 + s + 1)
                        elif q:
                            pool.wait_ge(ymade, (q - 1) * steps * 2 + (steps - 1) * 2 + s + 1)
                        nc.gpsimd.tensor_tensor(nl[s], n_of(g), level(l), ALU.mult).then_inc(masked, 1)

        @block.tensor
        def _(pe):
            for q in range(NG // 2):
                for s in range(2):
                    g = 2 * q + s
                    pe.wait_ge(masked, q * 2 * L + s + 1)
                    if q:
                        pe.wait_ge(ycopied, (q - 1) * steps * 2 + (steps - 1) * 2 + s + 1)
                    for m in range(G):
                        last = nc.tensor.transpose(co.ps[:, s, m * P:(m + 1) * P], nl[s][:, m, :], ident)
                    last.then_inc(first, 1)
                for l in range(1, L):
                    for s in range(2):
                        n = (q * steps + l - 1) * 2 + s
                        pe.wait_ge(masked, q * 2 * L + 2 * l + s + 1)
                        if l == 1:
                            pe.wait_ge(began, 2 * q + s + 1)
                        else:
                            pe.wait_ge(updated, n - 1)
                        for m in range(G):
                            last = nc.tensor.matmul(co.ps[:, s, m * P:(m + 1) * P], nl[s][:, m, :], xv[s][:, m, 0, :], start=True, stop=True)
                        last.then_inc(ymade, 1)
                    for s in range(2):
                        n = (q * steps + l - 1) * 2 + s
                        pe.wait_ge(ycopied, n + 1)
                        z = co.ps[:, 2 + 2 * s:4 + 2 * s, :].rearrange("p b (m o t) -> p (b m) o t", m=2, o=2)
                        for m in range(G):
                            if l < L - 1:
                                nc.tensor.matmul(z[:, m, 0, :], xv[s][:, m, 1, :], yy[s][:, m, :], start=True, stop=True)
                            last = nc.tensor.matmul(z[:, m, 1, :], yy[s][:, m, :], xv[s][:, m, 1, :], start=True, stop=True)
                        last.then_inc(zmade, 1)

        @block.scalar
        def _(act):
            for q in range(NG // 2):
                for l in range(1, L):
                    for s in range(2):
                        n = (q * steps + l - 1) * 2 + s
                        act.wait_ge(ymade, n + 1)
                        if n >= 2:
                            act.wait_ge(zmade, n - 1)
                        nc.scalar.activation(yy[s], co.ps[:, s, :].rearrange("p (m t) -> p m t", m=G), ACT.Copy).then_inc(ycopied, 1)

        @block.vector
        def _(dve):
            link = Chain(dve, pch)
            for q in range(NG // 2):
                for s in range(2):
                    g = 2 * q + s
                    dve.wait_ge(first, g + 1)
                    if q:
                        dve.wait_ge(updated, 2 * q * steps - 1 + s)
                    nc.vector.tensor_tensor(xv[s][:, :, 0, :], ident_b, co.ps[:, s, :].rearrange("p (m t) -> p m t", m=G), ALU.subtract)
                    dve.wait_ge(masked, q * 2 * L + s + 1)
                    nc.vector.tensor_tensor(xv[s][:, :, 1, :], ident_b, nl[s], ALU.subtract).then_inc(began, 1)
                for l in range(1, L):
                    for s in range(2):
                        n = (q * steps + l - 1) * 2 + s
                        dve.wait_ge(zmade, n + 1)
                        dve.wait_ge(began, 2 * q + s + 1)
                        if n >= 2:
                            dve.wait_ge(updated, n - 1)
                        z = co.ps[:, 2 + 2 * s:4 + 2 * s, :].rearrange("p b (m o t) -> p (b m) o t", m=2, o=2)
                        if l < L - 1:
                            flat = xv[s].rearrange("p m o t -> p (m o t)")
                            nc.vector.tensor_tensor(flat, flat, co.ps[:, 2 + 2 * s:4 + 2 * s, :].rearrange("p b c -> p (b c)"), ALU.subtract).then_inc(updated, 1)
                        else:
                            nc.vector.tensor_tensor(n_of(2 * q + s), xv[s][:, :, 1, :], z[:, :, 1, :], ALU.subtract).then_inc(updated, 1)


def gdn_gates(co, a_log, dt_bias):
    nc = co.nc
    m = A_MISC
    N = NT * HG
    ba = co.at(m + 192, (NT, 2 * HG))
    beta, g, gc, egc, ktl, egl, nbe = (co.at(m + 256 + 32 * i, (N,)) for i in range(7))
    dtb, alog = co.at(m + 480, (HG,)), co.at(m + 484, (HG,))
    t1, t2 = co.at(m + 488, (N,)), co.at(m + 520, (N,))
    v3 = lambda x: x.rearrange("p (t h) -> p t h", h=HG)
    per_head = lambda x: x.rearrange("p (o h) -> p o h", o=1).to_broadcast([P, NT, HG])
    loaded, on_act, on_dve, on_pe, dch = (co.sem(f"gate_{x}") for x in ("loaded", "on_act", "on_dve", "on_pe", "dch"))
    with nc.Block() as block:
        @block.sync
        def _(sp):
            sp.dma_start(dtb, dt_bias.rearrange("(o h) -> o h", o=1).to_broadcast([P, HG])).then_inc(loaded, 16)
            sp.dma_start(alog, a_log.rearrange("(o h) -> o h", o=1).to_broadcast([P, HG])).then_inc(loaded, 16)

        @block.scalar
        def _(act):
            act.wait_ge(loaded, 32)
            nc.scalar.activation(v3(beta), ba[:, :, 0:HG], ACT.Tanh, scale=0.5).then_inc(on_act, 1)
            nc.scalar.activation(alog, alog, ACT.Exp).then_inc(on_act, 1)
            act.wait_ge(on_dve, 1)
            nc.scalar.activation(t2, t1, ACT.Abs).then_inc(on_act, 1)
            act.wait_ge(on_act, 3)
            nc.scalar.activation(t2, t2, ACT.Exp, scale=-1.0).then_inc(on_act, 1)
            act.wait_ge(on_dve, 2)
            nc.scalar.activation(t2, t2, ACT.Ln).then_inc(on_act, 1)
            act.wait_ge(on_dve, 4)
            nc.scalar.activation(egc, gc, ACT.Exp).then_inc(on_act, 1)
            nc.scalar.activation(egl, egl, ACT.Exp).then_inc(on_act, 1)
            nc.scalar.activation(ktl, t1, ACT.Exp).then_inc(on_act, 1)

        @block.vector
        def _(dve):
            link = Chain(dve, dch)
            dve.wait_ge(loaded, 32)
            nc.vector.tensor_tensor(v3(t1), ba[:, :, HG:2 * HG], per_head(dtb), ALU.add).then_inc(on_dve, 1)
            dve.wait_ge(on_act, 4)
            link(nc.vector.tensor_scalar(beta, beta, 0.5, 0.5, ALU.mult, ALU.add))
            nc.vector.tensor_scalar(t2, t2, 1.0, None, ALU.add).then_inc(on_dve, 1)
            dve.wait_ge(on_act, 5)
            dve.wait_ge(on_dve, 2)
            link(nc.vector.scalar_tensor_tensor(g, t1, 0.0, t2, ALU.max, ALU.add))
            nc.vector.scalar_tensor_tensor(v3(g), v3(g), -1.0, per_head(alog), ALU.mult, ALU.mult).then_inc(on_dve, 1)
            dve.wait_ge(on_pe, 2)
            link(nc.vector.tensor_copy(gc, co.ps[:, 0, 0:N]))
            link(nc.vector.tensor_copy(egl, co.ps[:, 1, 0:N]))
            nc.vector.tensor_tensor(t1, egl, gc, ALU.subtract).then_inc(on_dve, 1)
            dve.wait_ge(on_act, 6)
            link(nc.vector.scalar_tensor_tensor(nbe, beta, -1.0, egc, ALU.mult, ALU.mult))

        @block.tensor
        def _(pe):
            pe.wait_ge(on_dve, 3)
            nc.tensor.matmul(co.ps[:, 0, 0:N], co.at(A_CST + C_UT0, (P,)), g, start=True, stop=True).then_inc(on_pe, 1)
            nc.tensor.matmul(co.ps[:, 1, 0:N], co.at(A_CST + C_ONE, (P,)), g, start=True, stop=True).then_inc(on_pe, 1)


def gdn_chunks(co):
    nc = co.nc
    q, k, v = (co.at(A_F[i], (HG, T)) for i in range(3))
    m = A_MISC
    beta, g, gc, egc, ktl = (co.at(m + 256 + 32 * i, (NT * HG,)) for i in range(5))
    n_st, qk_st, kt_st, bv_st = (store_slot(co, i) for i in range(4))
    ident = co.at(A_CST + C_ID, (P,))
    incl = co.at(A_CST + C_UT0, (P,)).rearrange("p (o t) -> p o t", o=1).to_broadcast([P, HG, P])
    strict = co.at(A_CST + C_UT0 + P, (P,)).rearrange("p (o t) -> p o t", o=1).to_broadcast([P, HG, P])
    dt, di, ds, eg, tn = (co.at(A_T + 512 * i, (HG, P)) for i in range(5))
    bank = lambda b: co.ps[:, b, :].rearrange("p (h t) -> p h t", h=HG)
    products, clipped, decayed, grown, masked, qkd, n_made, q_scaled, turned, k_out, v_out, dch = (
        co.sem(f"gdn_{x}") for x in ("products", "clipped", "decayed", "grown", "masked", "qkd", "n_made", "q_scaled", "turned", "k_out", "v_out", "dch"))
    with nc.Block() as block:
        @block.tensor
        def _(pe):
            for c in range(NT):
                ct = slice(c * P, (c + 1) * P)
                if c:
                    pe.wait_ge(clipped, c)
                    pe.wait_ge(grown, c)
                    pe.wait_ge(qkd, c)
                    pe.wait_ge(n_made, c)
                for h in range(HG):
                    s = c * HG + h
                    nc.tensor.matmul(bank(2)[:, h, :], g[:, s:s + 1].to_broadcast([P, P]), co.at(A_CST + C_UT0, (P,)), start=True, stop=True)
                    nc.tensor.matmul(bank(3)[:, h, :], beta[:, s:s + 1].to_broadcast([P, P]), ident, start=True, stop=True)
                    nc.tensor.matmul(bank(0)[:, h, :], k[:, h, ct], k[:, h, ct], start=True, stop=True)
                    last = nc.tensor.matmul(bank(1)[:, h, :], k[:, h, ct], q[:, h, ct], start=True, stop=True)
                last.then_inc(products, 1)
                if c:
                    pe.wait_ge(k_out, c)
                    pe.wait_ge(v_out, c)
                for h in range(HG):
                    nc.tensor.transpose(bank(4)[:, h, :], k[:, h, ct], ident)
                    last = nc.tensor.transpose(bank(5)[:, h, :], v[:, h, ct], ident)
                last.then_inc(turned, 1)

        @block.vector
        def _(dve):
            link = Chain(dve, dch)
            for c in range(NT):
                cs = slice(c * HG, (c + 1) * HG)
                dve.wait_ge(products, c + 1)
                if c:
                    dve.wait_ge(decayed, c)
                for h in range(HG):
                    s = c * HG + h
                    last = nc.vector.tensor_scalar(dt[:, h, :], bank(2)[:, h, :], gc[:, s:s + 1], 0.0, ALU.subtract, ALU.min)
                last.then_inc(clipped, 1)
                dve.wait_ge(turned, c + 1)
                nc.vector.tensor_tensor(kt_st[:, cs, :], bank(4), bc(ktl[:, cs], P), ALU.mult).then_inc(k_out, 1)
                nc.vector.tensor_tensor(bv_st[:, cs, :], bank(5), bc(beta[:, cs], P), ALU.mult).then_inc(v_out, 1)
                dve.wait_ge(masked, 2 * c + 1)
                nc.vector.tensor_tensor(qk_st[:, cs, :], bank(1), di, ALU.mult).then_inc(qkd, 1)
                dve.wait_ge(masked, 2 * c + 2)
                if c:
                    dve.wait_ge(n_made, c)
                link(nc.vector.tensor_tensor(tn, bank(0), ds, ALU.mult))
                nc.vector.tensor_tensor(n_st[:, cs, :], tn, bank(3), ALU.mult).then_inc(n_made, 1)

        @block.scalar
        def _(act):
            for c in range(NT):
                act.wait_ge(clipped, c + 1)
                if c:
                    act.wait_ge(masked, 2 * c)
                nc.scalar.activation(dt2(co), dt, ACT.Exp).then_inc(decayed, 1)
                if c:
                    act.wait_ge(q_scaled, c)
                nc.scalar.activation(eg, bank(2), ACT.Exp).then_inc(grown, 1)

        @block.gpsimd
        def _(pool):
            for c in range(NT):
                ct = slice(c * P, (c + 1) * P)
                pool.wait_ge(decayed, c + 1)
                if c:
                    pool.wait_ge(n_made, c)
                nc.gpsimd.tensor_tensor(di, dt2(co), incl, ALU.mult).then_inc(masked, 1)
                nc.gpsimd.tensor_tensor(ds, dt2(co), strict, ALU.mult).then_inc(masked, 1)
                pool.wait_ge(grown, c + 1)
                pool.wait_ge(products, c + 1)
                nc.gpsimd.tensor_tensor(q[:, :, ct], q[:, :, ct], eg, ALU.mult).then_inc(q_scaled, 1)


def dt2(co):
    return co.at(A_T + 2560, (HG, P))


def store_slot(co, i):
    return co.at(A_BIG, (NT * HG, 4, P))[:, :, i, :]


def gdn_state(co):
    nc = co.nc
    q, k, o = (co.at(A_F[i], (HG, T)) for i in range(3))
    n_st, qk_st, kt_st, bv_st = (store_slot(co, i) for i in range(4))
    egl, nbe = co.at(A_MISC + 256 + 32 * 5, (NT * HG,)), co.at(A_MISC + 256 + 32 * 6, (NT * HG,))
    S, R, VN = (co.at(A_T + 512 * i, (HG, P)) for i in range(3))
    bank = lambda b, pair: co.ps[:, 2 * b + pair, 0:256].rearrange("p (h t) -> p h t", h=2)
    zeroed, ks, resid, vn_made, vn_out, outs, o_out, updated = (
        co.sem(f"gds_{x}") for x in ("zeroed", "ks", "resid", "vn_made", "vn_out", "outs", "o_out", "updated"))
    with nc.Block() as block:
        @block.gpsimd
        def _(pool):
            nc.gpsimd.memset(S, 0.0).then_inc(zeroed, 1)

        @block.tensor
        def _(pe):
            pe.wait_ge(zeroed, 1)
            for c in range(NT):
                ct = slice(c * P, (c + 1) * P)
                for pair in range(2):
                    n = 2 * c + pair
                    if c:
                        pe.wait_ge(updated, 2 * (n - 1))
                    for j in range(2):
                        h = 2 * pair + j
                        last = nc.tensor.matmul(bank(0, pair)[:, j, :], k[:, h, ct], S[:, h, :], start=True, stop=True)
                    last.then_inc(ks, 1)
                for pair in range(2):
                    n = 2 * c + pair
                    pe.wait_ge(resid, 2 * (n + 1))
                    for j in range(2):
                        h = 2 * pair + j
                        last = nc.tensor.matmul(bank(1, pair)[:, j, :], n_st[:, c * HG + h, :], R[:, h, :], start=True, stop=True)
                    last.then_inc(vn_made, 1)
                for pair in range(2):
                    n = 2 * c + pair
                    if c:
                        pe.wait_ge(o_out, n - 1)
                    pe.wait_ge(vn_out, n + 1)
                    for j in range(2):
                        h = 2 * pair + j
                        nc.tensor.matmul(bank(3, pair)[:, j, :], kt_st[:, c * HG + h, :], VN[:, h, :], start=True, stop=True)
                    for j in range(2):
                        h = 2 * pair + j
                        nc.tensor.matmul(bank(2, pair)[:, j, :], S[:, h, :], q[:, h, ct], start=True, stop=False)
                        last = nc.tensor.matmul(bank(2, pair)[:, j, :], VN[:, h, :], qk_st[:, c * HG + h, :], start=False, stop=True)
                    last.then_inc(outs, 1)

        @block.vector
        def _(dve):
            for c in range(NT):
                for pair in range(2):
                    n = 2 * c + pair
                    dve.wait_ge(ks, n + 1)
                    if c:
                        dve.wait_ge(vn_made, n - 1)
                    for j in range(2):
                        h = 2 * pair + j
                        s = c * HG + h
                        nc.vector.scalar_tensor_tensor(R[:, h, :], bank(0, pair)[:, j, :], nbe[:, s:s + 1], bv_st[:, s, :], ALU.mult, ALU.add).then_inc(resid, 1)
                for pair in range(2):
                    n = 2 * c + pair
                    dve.wait_ge(outs, n + 1)
                    for j in range(2):
                        h = 2 * pair + j
                        s = c * HG + h
                        nc.vector.scalar_tensor_tensor(S[:, h, :], S[:, h, :], egl[:, s:s + 1], bank(3, pair)[:, j, :], ALU.mult, ALU.add).then_inc(updated, 1)

        @block.scalar
        def _(act):
            for c in range(NT):
                for pair in range(2):
                    n = 2 * c + pair
                    act.wait_ge(vn_made, n + 1)
                    if c:
                        act.wait_ge(outs, n - 1)
                    nc.scalar.activation(VN[:, 2 * pair:2 * pair + 2, :], bank(1, pair), ACT.Copy).then_inc(vn_out, 1)
                for pair in range(2):
                    act.wait_ge(outs, 2 * c + pair + 1)
                    nc.scalar.activation(o[:, 2 * pair:2 * pair + 2, c * P:(c + 1) * P], bank(2, pair), ACT.Copy).then_inc(o_out, 1)


def swa_prepare(co, rel_bias, sinks):
    nc = co.nc
    qh, kd, vw, bias, bias0 = swa_views(co)
    qb, kb, vbp = co.at(A_F[3], (WB, T)), co.at(A_F[4] + 1088, (T,)), co.at(A_F[4], (T + 64,))
    rb = co.at(A_MISC + 576, (8,), (0, 32))
    sink = co.at(A_MISC + 564, (WB,))
    hot = co.at(A_CST + C_HOT, (192,), (0, 32))
    moved, tabled, padded, hotted, out1, turned, vout = (co.sem(f"swp_{x}") for x in ("moved", "tabled", "padded", "hotted", "out", "turned", "vout"))
    NC = T // 64
    with nc.Block() as block:
        @block.sync
        def _(sp):
            sp.dma_start(rb, rel_bias).then_inc(tabled, 16)
            for h in range(2):
                for b in range(WB):
                    sp.dma_start(qh[:, :, 2 * b + h, :], qb[64 * h:64 * h + 64, b, :].rearrange("p (n t) -> p n t", t=64)).then_inc(moved, 16)
                sp.dma_start(kd[:, h, 64:], kb[64 * h:64 * h + 64, :]).then_inc(moved, 16)
                sp.dma_start(sink[64 * h:64 * h + 64, :], sinks.rearrange("(o b h) -> h o b", o=1, h=2)[h].to_broadcast([64, WB])).then_inc(moved, 16)
            sp.wait_ge(moved, 16 * (2 * WB + 4))

        @block.gpsimd
        def _(pool):
            nc.gpsimd.memset(kd[:, :, 0:64], 0.0).then_inc(padded, 1)
            nc.gpsimd.memset(vbp[:, 0:64], 0.0).then_inc(padded, 1)

        @block.tensor
        def _(pe):
            pe.wait_ge(tabled, 16)
            for j in range(P):
                for h in range(2):
                    last = nc.tensor.matmul(co.ps[64 * h:64 * h + 64, j // 64, (j % 64) * 8:(j % 64) * 8 + 8], hot[:, 127 - j:191 - j],
                                            rb, start=True, stop=True)
            last.then_inc(hotted, 1)
            pe.wait_ge(padded, 2)
            for n in range(NC):
                last = nc.tensor.transpose(co.ps[:, 2 + n // 4, (n % 4) * P:(n % 4 + 1) * P], vbp[:, 64 * n:64 * n + P], co.at(A_CST + C_ID, (P,)))
            last.then_inc(turned, 1)

        @block.scalar
        def _(act):
            act.wait_ge(turned, 1)
            nc.scalar.activation(vw.rearrange("p (b n) d -> p b (n d)", b=4), co.ps[:, 2:6, :], ACT.Copy).then_inc(vout, 1)

        @block.vector
        def _(dve):
            dve.wait_ge(hotted, 1)
            for h in range(2):
                rows = slice(64 * h, 64 * h + 64)
                src = co.ps[rows, 0:2, :].rearrange("p b (j a) -> p (b j) a", a=8)
                for b in range(WB):
                    nc.vector.tensor_copy(bias[rows, b, :], src[:, :, 2 * b + h]).then_inc(out1, 1)
            dve.wait_ge(out1, 8)
            nc.vector.tensor_copy(bias0, bias).then_inc(out1, 1)
            dve.wait_ge(out1, 9)
            nc.vector.memset(bias0[:, :, 0:64], NEG).then_inc(out1, 1)


def swa_views(co):
    qh = co.at(A_BIG, (16, 8, 64), (0, 64))
    kd = co.at(A_BIG + 8192, (2, T + 64), (0, 64))
    vw = co.at(A_BIG + 8192 + 2176, (16, P))
    bias = co.at(A_BIG + 8192 + 2176 + 2048, (WB, P))
    bias0 = co.at(A_BIG + 8192 + 2176 + 2048 + 512, (WB, P))
    return qh, kd, vw, bias, bias0


def swa_attend(co, zb):
    nc = co.nc
    qh, kd, vw, bias, bias0 = swa_views(co)
    sink = co.at(A_MISC + 564, (WB,))
    ident = co.at(A_CST + C_ID, (P,))
    sc = [co.at(A_T + 512 * i, (WB, P)) for i in range(2)]
    pt = [co.at(A_T + 1024 + 512 * i, (WB, P)) for i in range(2)]
    mx = [co.at(A_MISC + 600 + 16 * i, (WB,)) for i in range(2)]
    es = [co.at(A_MISC + 604 + 16 * i, (WB,)) for i in range(2)]
    sm = [co.at(A_MISC + 608 + 16 * i, (WB,)) for i in range(2)]
    NC = T // 64
    scored, shifted, sunk, powered, normed, turned, pt_out, mixed, gated, dch = (
        co.sem(f"swa_{x}") for x in ("scored", "shifted", "sunk", "powered", "normed", "turned", "pt_out", "mixed", "gated", "dch"))
    bank = lambda b: co.ps[:, b, :].rearrange("p (h t) -> p h t", h=WB)
    with nc.Block() as block:
        @block.tensor
        def _(pe):
            def scores(n):
                if n >= 2:
                    pe.wait_ge(shifted, n - 1)
                for b in range(WB):
                    last = nc.tensor.matmul(bank(n % 2)[:, b, :], qh[:, n, 2 * b:2 * b + 2, :].rearrange("p h t -> p (h t)"),
                                            kd[:, b // 2, 64 * n:64 * n + P], start=True, stop=True)
                last.then_inc(scored, 1)

            scores(0)
            for n in range(NC):
                if n + 1 < NC:
                    scores(n + 1)
                pe.wait_ge(normed, n + 1)
                if n >= 2:
                    pe.wait_ge(pt_out, n - 1)
                for b in range(WB):
                    last = nc.tensor.transpose(bank(2 + n % 2)[:, b, :], sc[n % 2][:, b, :], ident)
                last.then_inc(turned, 1)
                pe.wait_ge(pt_out, n + 1)
                if n >= 2:
                    pe.wait_ge(gated, n - 1)
                for b in range(WB):
                    for h in range(2):
                        last = nc.tensor.matmul(co.ps[64 * h:64 * h + 64, 4 + n % 2, 64 * b:64 * b + 64],
                                                vw[:, n, 64 * (b // 2):64 * (b // 2) + 64], pt[n % 2][:, b, 64 * h:64 * h + 64],
                                                start=True, stop=True)
                last.then_inc(mixed, 1)

        @block.vector
        def _(dve):
            link = Chain(dve, dch)
            def gate(n):
                dve.wait_ge(mixed, n + 1)
                z = zb[:, :, 64 * n:64 * n + 64]
                nc.vector.tensor_tensor(z, z, co.ps[:, 4 + n % 2, 0:256].rearrange("p (b t) -> p b t", b=WB), ALU.mult).then_inc(gated, 1)

            def first(n):
                i = n % 2
                dve.wait_ge(scored, n + 1)
                if n >= 2:
                    dve.wait_ge(turned, n - 1)
                link(nc.vector.tensor_tensor(sc[i], bank(i), bias if n else bias0, ALU.add))
                link(nc.vector.tensor_reduce(mx[i], sc[i], AX, ALU.max))
                link(nc.vector.tensor_tensor(mx[i], mx[i], sink, ALU.max))
                link(nc.vector.tensor_tensor(es[i], sink, mx[i], ALU.subtract))
                nc.vector.tensor_tensor(sc[i], sc[i], bc(mx[i], P), ALU.subtract).then_inc(shifted, 1)

            first(0)
            for n in range(NC):
                i = n % 2
                if n + 1 < NC:
                    first(n + 1)
                dve.wait_ge(powered, 2 * n + 2)
                link(nc.vector.tensor_reduce(sm[i], sc[i], AX, ALU.add))
                link(nc.vector.tensor_tensor(sm[i], sm[i], es[i], ALU.add))
                link(nc.vector.reciprocal(sm[i], sm[i]))
                nc.vector.tensor_tensor(sc[i], sc[i], bc(sm[i], P), ALU.mult).then_inc(normed, 1)
                if n:
                    gate(n - 1)
            gate(NC - 1)

        @block.scalar
        def _(act):
            def power(n):
                act.wait_ge(shifted, n + 1)
                nc.scalar.activation(es[n % 2], es[n % 2], ACT.Exp).then_inc(powered, 1)
                nc.scalar.activation(sc[n % 2], sc[n % 2], ACT.Exp).then_inc(powered, 1)

            power(0)
            for n in range(NC):
                if n + 1 < NC:
                    power(n + 1)
                act.wait_ge(turned, n + 1)
                if n >= 2:
                    act.wait_ge(mixed, n - 1)
                nc.scalar.activation(pt[n % 2], bank(2 + n % 2), ACT.Copy).then_inc(pt_out, 1)


def multiply_blocks(co, tag, pairs):
    nc = co.nc
    done = co.sem(f"{tag}_done")
    with nc.Block() as block:
        @block.vector
        def _(dve):
            for n, (out, x) in enumerate(pairs):
                nc.vector.tensor_tensor(out, out, x, ALU.mult).then_inc(done, 1)


def project_out(co, tag, w, mixed, res, dst, stored):
    nc = co.nc
    wo = co.at(A_BIG, (KT, D))
    rr = [co.at(A_BIG + 8192 + 1024 * i, (D,)) for i in range(3)]
    loaded = [co.sem(f"{tag}_w{k}") for k in range(KT)]
    resin = [co.sem(f"{tag}_r{i}") for i in range(3)]
    multiplied, added = co.sem(f"{tag}_multiplied"), co.sem(f"{tag}_added")
    with nc.Block() as block:
        @block.sync
        def _(sp):
            for k in range(KT):
                sp.dma_start(wo[:, k, :], w[k * P:(k + 1) * P, :]).then_inc(loaded[k], 16)
                if k < 3:
                    sp.dma_start(rr[k], res[k * P:(k + 1) * P, :]).then_inc(resin[k], 16)
            for t in range(NT):
                sp.wait_ge(added, t + 1)
                sp.dma_start(dst[t * P:(t + 1) * P, :], rr[t % 3]).then_inc(stored[t % 3], 16)
                if t + 3 < NT:
                    sp.wait_ge(stored[t % 3], 16 * (t // 3 + 1))
                    sp.dma_start(rr[t % 3], res[(t + 3) * P:(t + 4) * P, :]).then_inc(resin[t % 3], 16)
            for i in range(3):
                sp.wait_ge(stored[i], 16 * len(range(i, NT, 3)))

        @block.tensor
        def _(pe):
            for t in range(NT):
                if t >= 4:
                    pe.wait_ge(added, t - 3)
                for h in range(2):
                    for k in range(KT):
                        if t == 0 and h == 0:
                            pe.wait_ge(loaded[k], 16)
                        last = nc.tensor.matmul(co.ps[:, 2 * (t % 4) + h, :], mixed[k][:, t * P:(t + 1) * P], wo[:, k, h * 512:(h + 1) * 512],
                                                start=k == 0, stop=k == KT - 1)
                last.then_inc(multiplied, 1)

        @block.vector
        def _(dve):
            for t in range(NT):
                dve.wait_ge(multiplied, t + 1)
                dve.wait_ge(resin[t % 3], 16 * (t // 3 + 1))
                nc.vector.tensor_tensor(rr[t % 3], rr[t % 3], co.ps[:, 2 * (t % 4):2 * (t % 4) + 2, :].rearrange("p b n -> p (b n)"), ALU.add).then_inc(added, 1)


def start(co, cst):
    nc = co.nc
    loaded, set_ = co.sem("constants"), co.sem("epsilons")
    co.eps_at = {RMS_EPS: A_MISC + 568, GN_EPS: A_MISC + 569, 128 * L2_EPS: A_MISC + 570, 64 * RMS_EPS: A_MISC + 571}
    with nc.Block() as block:
        @block.sync
        def _(sp):
            sp.dma_start(co.at(A_CST, (C_ALL,)), cst).then_inc(loaded, 16)
            sp.wait_ge(loaded, 16)

        @block.gpsimd
        def _(pool):
            for eps, col in co.eps_at.items():
                nc.gpsimd.memset(co.at(col, (1,)), eps).then_inc(set_, 1)


def load_columns(co, tag, pairs):
    nc = co.nc
    loaded = co.sem(f"{tag}_loaded")
    with nc.Block() as block:
        @block.sync
        def _(sp):
            for dst, src in pairs:
                sp.dma_start(dst, src).then_inc(loaded, 16)
            sp.wait_ge(loaded, 16 * len(pairs))


def even_layer(co, a, x, dst):
    q, k, v, qb = ([co.at(A_F[i] + T * b, (T,)) for b in range(WB)] for i in range(4))
    za, zb = ([co.at(A_F[i] + T * b, (T,)) for b in range(WB)] for i in (5, 6))
    kb, vb = co.at(A_F[4] + 1088, (T,)), co.at(A_F[4] + 64, (T,))
    norm_transpose(co, "en", x, a["even_norm"][0])
    blocks = [(EVEN["q"] + P * b, "conv", q[b]) for b in range(WB)]
    blocks += [(EVEN["k"] + P * b, "conv", k[b]) for b in range(WB)]
    blocks += [(EVEN["v"] + P * b, "conv", v[b]) for b in range(WB)]
    blocks += [(EVEN["za"] + P * b, "gate", za[b]) for b in range(WB)]
    blocks += [(EVEN["qb"] + P * b, "plain", qb[b]) for b in range(WB)]
    blocks += [(EVEN["kb"], "plain", kb), (EVEN["vb"], "plain", vb)]
    blocks += [(EVEN["zb"] + P * b, "gate", zb[b]) for b in range(WB)]
    project(co, "ep", a["even_w_in"][0], blocks, conv_w=a["gdn_conv_w"][0],
            small=(EVEN["beta"], 2 * HG, co.at(A_MISC + 192, (NT, 2 * HG))))
    qn, kn, on = (co.at(A_MISC + 560 + i, (1,)) for i in range(3))
    col = lambda ap: ap.rearrange("(p o) -> p o", o=1)
    load_columns(co, "eg", [(qn[0:64], col(a["swa_q_norm"][0])), (qn[64:128], col(a["swa_q_norm"][0])),
                            (kn[0:64], col(a["swa_k_norm"][0])), (kn[64:128], col(a["swa_k_norm"][0])),
                            (on, col(a["gdn_out_norm"][0]))])
    norm_blocks(co, "eq", [(x_, 128, 128.0, 128 * L2_EPS, 1.0) for x_ in q] + [(x_, 128, 1.0, L2_EPS, 1.0) for x_ in k]
                + [(x_, 64, 1.0, 64 * RMS_EPS, qn) for x_ in qb] + [(kb, 64, 1.0 / 64, RMS_EPS, kn)])
    swa_prepare(co, a["rel_bias"], a["swa_sinks"][0])
    swa_attend(co, co.at(A_F[6], (WB, T)))
    gdn_gates(co, a["gdn_a_log"][0], a["gdn_dt_bias"][0])
    gdn_chunks(co)
    invert(co, "gi", store_slot(co, 0), (A_F[3], A_F[3] + 1024), (A_F[3] + 2048, A_F[3] + 2560), (A_F[3] + 3072, A_F[3] + 3584))
    gdn_state(co)
    norm_blocks(co, "eo", [(x_, 128, 1.0 / 128, RMS_EPS, on) for x_ in v])
    multiply_blocks(co, "eo2", list(zip(za, v)))
    project_out(co, "eout", a["even_w_out"][0], za + zb, x, dst, [co.sem(f"eout_stored{i}") for i in range(3)])



SG, SP, SCH, SC8 = 32, 64, 16, 8
NPAIR = SG // 2
TWO_PI = 2 * math.pi
TP1 = 6.28125
TP2 = float(np.float32(np.floor((TWO_PI - TP1) * 2 ** 21) / 2 ** 21))
TP3 = TWO_PI - TP1 - TP2
MAGIC = 12582912.0


def complex_product(nc, link, out, x, y, t):
    tt = nc.vector.tensor_tensor
    link(tt(t[0], x[0], y[0], ALU.mult))
    link(tt(t[1], x[1], y[1], ALU.mult))
    link(tt(out[0], t[0], t[1], ALU.subtract))
    link(tt(t[0], x[0], y[1], ALU.mult))
    link(tt(t[1], x[1], y[0], ALU.mult))
    link(tt(out[1], t[0], t[1], ALU.add))


class S5:

    def __init__(self, co):
        B = A_BIG
        self.us = co.at(B, (SG, P))
        self.toep = co.at(B + 4096, (SG, P))
        self.bpt = [co.at(B + 8192 + 2048 * i, (NPAIR, P)) for i in range(2)]
        self.h = [co.at(B + 12288 + 2048 * i, (NPAIR, P)) for i in range(2)]
        self.rot = [co.at(A_F[0] + 2048 * i, (NPAIR, P)) for i in range(2)]
        self.ck = [co.at(A_F[4] + 1024, (NPAIR, 9, SCH)), co.at(A_T, (NPAIR, 9, SCH))]
        self.bp = [co.at(A_F[4] + 1024, (NPAIR, 8, SCH)), co.at(A_T, (NPAIR, 8, SCH))]
        t = A_T + 2304
        self.pw = [co.at(t + 144 * i, (NPAIR, 9)) for i in range(2)]
        self.pwr = [co.at(t + 288 + 128 * i, (NPAIR, 8)) for i in range(2)]
        self.bb = [co.at(t + 544 + 256 * i, (NPAIR, SCH)) for i in range(2)]
        self.cc = [co.at(t + 1056 + 256 * i, (NPAIR, SCH)) for i in range(2)]
        self.braw = [co.at(B + 12288 + 256 * i, (NPAIR, SCH)) for i in range(2)]
        self.cnat = [co.at(B + 12288 + 512 + 512 * i, (4, 2, SP)) for i in range(2)]
        self.small = lambda i: co.at(A_MISC + 192 + 16 * i, (NPAIR,))
        self.kst = co.at(A_F[0], (SG, P), (0, SCH))


def s5_store_u(co, u, u5):
    nc = co.nc
    u2 = co.at(A_BIG + 4096, (WB, SC8, P))
    turned, stored = co.sem("s5u_turned"), co.sem("s5u_stored")
    with nc.Block() as block:
        @block.vector
        def _(dve):
            for b in range(WB):
                nc.vector.tensor_copy(u2[:, b, :, :], u[:, b, :].rearrange("p (c j) -> p j c", j=SC8)).then_inc(turned, 1)

        @block.sync
        def _(sp):
            for b in range(WB):
                sp.wait_ge(turned, b + 1)
                sp.dma_start(u5[b * P:(b + 1) * P, :, :], u2[:, b, :, :]).then_inc(stored, 16)
            sp.wait_ge(stored, 16 * WB)


def s5_tables(co, a, u5):
    nc = co.nc
    s = S5(co)
    (lre, lim, ls, dt, ar, ai, mag, mag8, sn, cs, lbre, lbim, den, fre, fim, k_, r_, t1, t2, u0, u1, n0, n1) = (s.small(i) for i in range(23))
    loaded, on_act, on_dve, on_pe, taken, dch, uin = (co.sem(f"s5t_{x}") for x in ("loaded", "on_act", "on_dve", "on_pe", "taken", "dch", "uin"))
    q_a = lambda ap: ap.rearrange("(a g) p -> (g p) a", g=2)
    ident = co.at(A_CST + C_ID, (P,))
    with nc.Block() as block:
        @block.sync
        def _(sp):
            sp.dma_start(lre, a["s5_lambda_re"][0].rearrange("(a g) p -> g p a", g=2)).then_inc(loaded, 16)
            sp.dma_start(lim, a["s5_lambda_im"][0].rearrange("(a g) p -> g p a", g=2)).then_inc(loaded, 16)
            for g in range(2):
                sp.dma_start(ls[64 * g:64 * g + 64, :], a["s5_log_step"][0].rearrange("(o a g) -> g o a", o=1, g=2)[g].to_broadcast([64, NPAIR])).then_inc(loaded, 16)
            for i, name in enumerate(("re", "im")):
                sp.dma_start(s.braw[i], a[f"s5_b_{name}"][0].rearrange("(a g) p c -> (g p) a c", g=2)).then_inc(loaded, 16)
                for d in range(2):
                    sp.dma_start(s.cnat[i][:, :, d, :], a[f"s5_c_{name}"][0].rearrange("g c p -> (g c) p").rearrange("(n q) p -> q n p", q=P)).then_inc(loaded, 16)
            sp.wait_ge(on_dve, 6)
            for j in range(SC8):
                sp.dma_start(s.us[16 * j:16 * j + 16, :, :], u5[:, j, :].rearrange("(g c) n -> c g n", c=SCH)).then_inc(uin, 16)
            sp.wait_ge(uin, 16 * SC8)

        @block.scalar
        def _(act):
            act.wait_ge(loaded, 16 * 10)
            nc.scalar.activation(dt, ls, ACT.Exp).then_inc(on_act, 1)
            act.wait_ge(on_dve, 1)
            nc.scalar.activation(mag, ar, ACT.Exp).then_inc(on_act, 1)
            nc.scalar.activation(mag8, ar, ACT.Exp, scale=8.0).then_inc(on_act, 1)
            act.wait_ge(on_dve, 2)
            nc.scalar.activation(sn, r_, ACT.Sin).then_inc(on_act, 1)
            nc.scalar.activation(cs, t1, ACT.Sin).then_inc(on_act, 1)
            for i in range(2):
                for n in range(4):
                    act.wait_ge(on_pe, 2 + 4 * i + n)
                    nc.scalar.activation(s.bpt[i][:, 4 * n:4 * n + 4, :], co.ps[:, 4 + n, :].rearrange("p (a t) -> p a t", a=4), ACT.Copy).then_inc(taken, 1)

        @block.tensor
        def _(pe):
            pe.wait_ge(loaded, 16 * 10)
            for i in range(2):
                for n in range(4):
                    last = nc.tensor.transpose(co.ps[:, i, n * P:(n + 1) * P], s.cnat[i][:, n, :, :].rearrange("p d q -> p (d q)"), ident)
            last.then_inc(on_pe, 1)
            pe.wait_ge(on_dve, 4)
            for i in range(2):
                for n in range(4):
                    if i:
                        pe.wait_ge(taken, n + 1)
                    for m in range(4):
                        last = nc.tensor.transpose(co.ps[:, 4 + n, m * P:(m + 1) * P], s.bp[i][:, 4 * n + m, :, :].rearrange("p j c -> p (j c)"), ident)
                    last.then_inc(on_pe, 1)

        @block.vector
        def _(dve):
            link = Chain(dve, dch)
            tt, ts, stt = nc.vector.tensor_tensor, nc.vector.tensor_scalar, nc.vector.scalar_tensor_tensor
            dve.wait_ge(on_act, 1)
            link(tt(ai, lim, dt, ALU.mult))
            tt(ar, lre, dt, ALU.mult).then_inc(on_dve, 1)
            link(ts(k_, ai, 1.0 / TWO_PI, MAGIC, ALU.mult, ALU.add))
            link(ts(k_, k_, MAGIC, None, ALU.subtract))
            link(stt(r_, k_, -TP1, ai, ALU.mult, ALU.add))
            link(stt(r_, k_, -TP2, r_, ALU.mult, ALU.add))
            link(stt(r_, k_, -TP3, r_, ALU.mult, ALU.add))
            link(ts(r_, r_, 3.1415925, -3.1415925, ALU.min, ALU.max))
            link(ts(t1, r_, -1.0, None, ALU.mult))
            link(tt(t1, t1, r_, ALU.max))
            ts(t1, t1, -1.0, math.pi / 2, ALU.mult, ALU.add).then_inc(on_dve, 1)
            dve.wait_ge(on_pe, 1)
            for i in range(2):
                for g in range(2):
                    link(nc.vector.tensor_copy(s.cc[i][64 * g:64 * g + 64, :, :],
                                               co.ps[64 * g:64 * g + 64, i, :].rearrange("p (a g c) -> p a g c", g=2, c=SCH)[:, :, g, :]))
            dve.wait_ge(on_act, 5)
            link(tt(lbre, mag, cs, ALU.mult))
            link(tt(lbim, mag, sn, ALU.mult))
            link(tt(den, lre, lre, ALU.mult))
            link(tt(t1, lim, lim, ALU.mult))
            link(tt(den, den, t1, ALU.add))
            link(nc.vector.reciprocal(den, den))
            link(ts(n0, lbre, 1.0, None, ALU.subtract))
            link(tt(t1, n0, lre, ALU.mult))
            link(tt(t2, lbim, lim, ALU.mult))
            link(tt(fre, t1, t2, ALU.add))
            link(tt(fre, fre, den, ALU.mult))
            link(tt(t1, lbim, lre, ALU.mult))
            link(tt(t2, n0, lim, ALU.mult))
            link(tt(fim, t1, t2, ALU.subtract))
            link(tt(fim, fim, den, ALU.mult))
            tmp = [co.at(A_BIG + 4096 + 2304 * 0, (NPAIR, SCH)), co.at(A_BIG + 4096 + 256, (NPAIR, SCH))]
            complex_product(nc, link, s.bb, [bc(fre, SCH), bc(fim, SCH)], s.braw, tmp)
            for i, v in enumerate((1.0, 0.0)):
                link(nc.vector.memset(s.pw[i][:, :, 0:1], v))
                link(nc.vector.tensor_copy(s.pw[i][:, :, 1], (lbre, lbim)[i]))
            for m in (1, 2, 4):
                tm = [co.at(A_BIG + 4096 + 64 * i, (NPAIR, m)) for i in range(2)]
                complex_product(nc, link, [x[:, :, m + 1:2 * m + 1] for x in s.pw], [x[:, :, 1:m + 1] for x in s.pw],
                                [x[:, :, m:m + 1].to_broadcast([P, NPAIR, m]) for x in s.pw], tm)
            for i in range(2):
                for j in range(8):
                    link(nc.vector.tensor_copy(s.pwr[i][:, :, j], s.pw[i][:, :, 7 - j]))
            nc.vector.memset(t1, 0.0).then_inc(on_dve, 1)
            wide = lambda x, n: x.rearrange("p a (o c) -> p a o c", o=1).to_broadcast([P, NPAIR, n, SCH])
            deep = lambda x, n: x.rearrange("p a (k o) -> p a k o", o=1).to_broadcast([P, NPAIR, n, SCH])
            tb = [co.at(A_BIG + 4096 + 2048 * i, (NPAIR, 8, SCH)) for i in range(2)]
            complex_product(nc, link, s.bp, [deep(x, 8) for x in s.pwr], [wide(x, 8) for x in s.bb], tb)
            nc.vector.memset(t1, 0.0).then_inc(on_dve, 1)
            dve.wait_ge(on_pe, 9)
            dve.wait_ge(on_dve, 4)
            tc_ = [co.at(A_BIG + 2304 * i, (NPAIR, 9, SCH)) for i in range(2)]
            complex_product(nc, link, s.ck, [deep(x, 9) for x in s.pw], [wide(x, 9) for x in s.cc], tc_)
            ts(s.ck[1], s.ck[1], -1.0, None, ALU.mult).then_inc(on_dve, 1)
            dve.wait_ge(on_dve, 5)
            nc.vector.memset(t1, 0.0).then_inc(on_dve, 1)
            link(nc.vector.tensor_copy(u0, cs))
            link(nc.vector.tensor_copy(u1, sn))
            for _i in range(3):
                complex_product(nc, link, [n0, n1], [u0, u1], [u0, u1], [t1, t2])
                link(nc.vector.tensor_copy(u0, n0))
                link(nc.vector.tensor_copy(u1, n1))


def s5_toeplitz(co):
    nc = co.nc
    s = S5(co)
    made, taken, zeroed, placed = (co.sem(f"s5k_{x}") for x in ("made", "taken", "zeroed", "placed"))
    with nc.Block() as block:
        @block.gpsimd
        def _(pool):
            nc.gpsimd.memset(s.toep, 0.0).then_inc(zeroed, 1)

        @block.tensor
        def _(pe):
            for n in range(4):
                for m in range(4):
                    for g in range(2):
                        a, rows = 4 * n + m, slice(64 * g, 64 * g + 64)
                        for i in range(2):
                            last = nc.tensor.matmul(co.ps[0:SCH, 2 * n + g, m * P:(m + 1) * P], s.bb[i][rows, a, :],
                                                    s.ck[i][rows, a, 0:8, :], start=i == 0, stop=i == 1)
                last.then_inc(made, 1)

        @block.scalar
        def _(act):
            kst = s.kst.rearrange("p (n m g) t -> p n m g t", n=4, g=2)
            for n in range(4):
                act.wait_ge(made, n + 1)
                for g in range(2):
                    nc.scalar.activation(kst[:, n, :, g, :], co.ps[0:SCH, 2 * n + g, :].rearrange("p (m t) -> p m t", m=4), ACT.Copy).then_inc(taken, 1)

        @block.sync
        def _(sp):
            sp.wait_ge(zeroed, 1)
            sp.wait_ge(taken, 8)
            for j in range(SC8):
                sp.dma_start(s.toep[16 * j:16 * j + 16, :, 16 * j:P], s.kst[:, :, 0:P - 16 * j]).then_inc(placed, 16)
            sp.wait_ge(placed, 16 * SC8)


def s5_scan(co, y5):
    nc = co.nc
    s = S5(co)
    mag8, u0, u1, n0, n1, t1, t2 = (s.small(i) for i in (7, 19, 20, 21, 22, 17, 18))
    tmp = [co.at(A_BIG + 8192 + 2048 * i, (NPAIR, P)) for i in range(2)]
    flat = lambda x: x.rearrange("p a c -> p (a c)")
    fed, ready, made, taken, stored, dch = (co.sem(f"s5s_{x}") for x in ("fed", "ready", "made", "taken", "stored", "dch"))
    with nc.Block() as block:
        @block.tensor
        def _(pe):
            for i in range(2):
                for a in range(NPAIR):
                    for g in range(2):
                        last = nc.tensor.matmul(co.ps[64 * g:64 * g + 64, 4 * i + a // 4, (a % 4) * P:(a % 4 + 1) * P],
                                                s.bpt[i][:, a, 64 * g:64 * g + 64], s.us[:, 2 * a + g, :], start=True, stop=True)
            last.then_inc(fed, 1)
            pe.wait_ge(ready, 1)
            for n in range(4):
                for g in range(2):
                    for m in range(4):
                        a, rows = 4 * n + m, slice(64 * g, 64 * g + 64)
                        out = co.ps[:, 2 * n + g, m * P:(m + 1) * P]
                        nc.tensor.matmul(out, s.toep[:, 2 * a + g, :], s.us[:, 2 * a + g, :], start=True, stop=False)
                        for i in range(2):
                            last = nc.tensor.matmul(out[:, 1:P], s.ck[i][rows, a, 1:9, :].rearrange("p k c -> p (k c)"),
                                                    s.h[i][rows, a, 0:P - 1], start=False, stop=i == 1)
                    last.then_inc(made, 1)

        @block.vector
        def _(dve):
            link = Chain(dve, dch)
            tt = nc.vector.tensor_tensor
            for i, v in enumerate((1.0, 0.0)):
                link(nc.vector.memset(s.rot[i][:, :, 0:1], v))
            w, w2 = (u0, u1), (n0, n1)
            for m in (1, 2, 4, 8, 16, 32, 64):
                tm = [co.at(A_BIG + 12288 + 2048 * i, (NPAIR, m)) for i in range(2)]
                complex_product(nc, link, [x[:, :, m:2 * m] for x in s.rot], [x[:, :, 0:m] for x in s.rot], [bc(x, m) for x in w], tm)
                complex_product(nc, link, w2, w, w, [t1, t2])
                w, w2 = w2, w
            dve.wait_ge(fed, 1)
            ps = [co.ps[:, 4 * i:4 * i + 4, :].rearrange("p n c -> p (n c)") for i in range(2)]
            er, ei = flat(s.rot[0]), flat(s.rot[1])
            hr, hi = flat(s.h[0]), flat(s.h[1])
            t0_, t1_ = flat(tmp[0]), flat(tmp[1])
            link(tt(hr, ps[0], er, ALU.mult))
            link(tt(t0_, ps[1], ei, ALU.mult))
            link(tt(hr, hr, t0_, ALU.add))
            link(tt(hi, ps[1], er, ALU.mult))
            link(tt(t0_, ps[0], ei, ALU.mult))
            link(tt(hi, hi, t0_, ALU.subtract))
            link(nc.vector.tensor_copy(tmp[0], bc(mag8, P)))
            link(nc.vector.memset(tmp[0][:, :, 0:1], 0.0))
            link(nc.vector.tensor_tensor_scan(hr, t0_, hr, 0.0, ALU.mult, ALU.add))
            link(nc.vector.tensor_tensor_scan(hi, t0_, hi, 0.0, ALU.mult, ALU.add))
            link(tt(t0_, hr, ei, ALU.mult))
            link(tt(t1_, hi, ei, ALU.mult))
            link(tt(hr, hr, er, ALU.mult))
            link(tt(hi, hi, er, ALU.mult))
            link(tt(hr, hr, t1_, ALU.subtract))
            tt(hi, hi, t0_, ALU.add).then_inc(ready, 1)

        @block.scalar
        def _(act):
            us = s.us.rearrange("p (n m g) t -> p n m g t", n=4, g=2)
            for n in range(4):
                for g in range(2):
                    act.wait_ge(made, 2 * n + g + 1)
                    nc.scalar.activation(us[:, n, :, g, :], co.ps[:, 2 * n + g, :].rearrange("p (m t) -> p m t", m=4), ACT.Copy).then_inc(taken, 1)

        @block.sync
        def _(sp):
            sp.wait_ge(taken, 8)
            for j in range(SC8):
                sp.dma_start(y5[:, j, :].rearrange("(g c) n -> c g n", c=SCH), s.us[16 * j:16 * j + 16, :, :]).then_inc(stored, 16)
            sp.wait_ge(stored, 16 * SC8)


def s5_glu(co, d_skip, w_glu, u5, y5, zc):
    nc = co.nc
    y = co.at(A_BIG, (WB, T))
    u = co.at(A_BIG + 4096, (WB, T))
    wg = co.at(A_BIG + 8192, (WB, 2 * W))
    yc = co.at(A_BIG + 12288, (WB, T))
    tb = co.at(A_F[0], (2, T))
    dcol = co.at(A_MISC + 632, (WB,))
    loaded, wloaded, cubed, tanhed, gelu, made_a, tanh_b, halved, gated, dch = (
        co.sem(f"glu_{x}") for x in ("loaded", "wloaded", "cubed", "tanhed", "gelu", "made", "tanh_b", "halved", "gated", "dch"))
    with nc.Block() as block:
        @block.sync
        def _(sp):
            sp.dma_start(dcol, d_skip.rearrange("(b p) -> p b", p=P)).then_inc(loaded, 16)
            for b in range(WB):
                sp.dma_start(y[:, b, :], y5[b * P:(b + 1) * P, :, :].rearrange("p j c -> p (j c)")).then_inc(loaded, 16)
                sp.dma_start(u[:, b, :], u5[b * P:(b + 1) * P, :, :].rearrange("p j c -> p (j c)")).then_inc(loaded, 16)
            sp.dma_start(wg, w_glu.rearrange("(k p) n -> p k n", p=P)).then_inc(wloaded, 16)

        @block.vector
        def _(dve):
            link = Chain(dve, dch)
            dve.wait_ge(loaded, 16 * (1 + 2 * WB))
            for b in range(WB):
                yb, ub = y[:, b, :], u[:, b, :]
                link(nc.vector.scalar_tensor_tensor(yb, ub, dcol[:, b:b + 1], yb, ALU.mult, ALU.add))
                link(nc.vector.tensor_tensor(ub, yb, yb, ALU.mult))
                link(nc.vector.tensor_scalar(ub, ub, 0.044715, 1.0, ALU.mult, ALU.add))
                nc.vector.tensor_tensor(ub, ub, yb, ALU.mult).then_inc(cubed, 1)
            for b in range(WB):
                dve.wait_ge(tanhed, b + 1)
                nc.vector.scalar_tensor_tensor(yc[:, b, :].rearrange("p (c j) -> p j c", j=SC8), u[:, b, :].rearrange("p (j c) -> p j c", j=SC8), 1.0,
                                               y[:, b, :].rearrange("p (j c) -> p j c", j=SC8), ALU.add, ALU.mult).then_inc(gelu, 1)
            for b in range(WB):
                dve.wait_ge(tanh_b, b + 1)
                link(nc.vector.scalar_tensor_tensor(tb[:, b % 2, :], tb[:, b % 2, :], 1.0, zc[b], ALU.add, ALU.mult))
                a_ = co.ps[:, 4 * (b % 2):4 * (b % 2) + 2, :].rearrange("p h t -> p (h t)")
                nc.vector.scalar_tensor_tensor(zc[b], a_, 0.25, tb[:, b % 2, :], ALU.mult, ALU.mult).then_inc(gated, 1)

        @block.scalar
        def _(act):
            for b in range(WB):
                act.wait_ge(cubed, b + 1)
                nc.scalar.activation(u[:, b, :], u[:, b, :], ACT.Tanh, scale=math.sqrt(2 / math.pi)).then_inc(tanhed, 1)
            for b in range(WB):
                act.wait_ge(made_a, b + 1)
                if b >= 2:
                    act.wait_ge(gated, b - 1)
                nc.scalar.activation(tb[:, b % 2, :], co.ps[:, 4 * (b % 2) + 2:4 * (b % 2) + 4, :].rearrange("p h t -> p (h t)"), ACT.Tanh, scale=0.25).then_inc(tanh_b, 1)

        @block.tensor
        def _(pe):
            pe.wait_ge(wloaded, 16)
            pe.wait_ge(gelu, WB)
            for b in range(WB):
                if b >= 2:
                    pe.wait_ge(gated, b - 1)
                for part in range(2):
                    for h in range(2):
                        for k in range(WB):
                            last = nc.tensor.matmul(co.ps[:, 4 * (b % 2) + 2 * part + h, :], wg[:, k, part * W + b * P:part * W + (b + 1) * P],
                                                    yc[:, k, h * 512:(h + 1) * 512], start=k == 0, stop=k == WB - 1)
                last.then_inc(made_a, 1)


LOGW = -math.exp(-0.5)


class R7:
    def __init__(self, co, half):
        m = A_MISC
        self.b0 = 2 * half
        self.r, self.k, self.v = (co.at(A_F[i] + 2048 * half, (2, T)) for i in (1, 2, 3))
        self.kk, self.b = co.at(A_F[0], (2, T)), co.at(A_F[0] + 2048, (2, T))
        self.bon = co.at(A_F[4] + 1024, (2, T))
        self.wa = co.at(A_F[4], (T,))
        self.cols = {n: co.at(m + 600 + 4 * i, (WB,)) for i, n in enumerate(("w0", "a0", "k_k", "k_a", "omka", "r_k", "ln_w", "ln_b"))}
        self.scale = co.at(m + 640, (2, NT))
        self.lw = [co.at(A_BIG + 2048 + 1024 * i, (T,)) for i in range(2)]
        self.gg = [co.at(A_BIG + 4096 + 1024 * i, (T,)) for i in range(2)]
        self.t = [co.at(A_BIG + 6144 + 1024 * i, (T,)) for i in range(8)]
        self.w2a2 = co.at(A_BIG, (W,))
        self.rk1 = [co.at(A_BIG + 1024 + P * i, (P,)) for i in range(2)]


def r7_start(co, a):
    nc = co.nc
    x = R7(co, 0)
    loaded, done, hd = co.sem("r7_loaded"), co.sem("r7_tanh"), co.sem("r7_halved")
    col = lambda ap: ap.rearrange("(b p) -> p b", p=P)
    with nc.Block() as block:
        @block.sync
        def _(sp):
            for n, src in (("w0", col(a["rwkv_w0"][0])), ("a0", col(a["rwkv_a0"][0])), ("k_k", col(a["rwkv_k_k"][0])), ("k_a", col(a["rwkv_k_a"][0])),
                           ("r_k", a["rwkv_r_k"][0].rearrange("(b h) d -> (h d) b", h=2)), ("ln_w", col(a["rwkv_ln_w"][0])), ("ln_b", col(a["rwkv_ln_b"][0]))):
                sp.dma_start(x.cols[n], src).then_inc(loaded, 16)
            sp.wait_ge(loaded, 16 * 7)

        @block.scalar
        def _(act):
            nc.scalar.activation(x.wa[0:64, :], x.wa[0:64, :], ACT.Tanh).then_inc(done, 1)

        @block.vector
        def _(dve):
            dve.wait_ge(loaded, 16 * 7)
            nc.vector.tensor_scalar(x.cols["w0"], x.cols["w0"], 0.5, None, ALU.mult).then_inc(hd, 1)
            nc.vector.tensor_scalar(x.cols["a0"], x.cols["a0"], 0.5, None, ALU.mult).then_inc(hd, 1)
            nc.vector.tensor_scalar(x.cols["omka"], x.cols["k_a"], -1.0, 1.0, ALU.mult, ALU.add).then_inc(hd, 1)


def r7_features(co, half, w2, a2):
    nc = co.nc
    x = R7(co, half)
    c_ = lambda n, j: x.cols[n][:, x.b0 + j:x.b0 + j + 1]
    loaded, made, tanhed, formed, rk, bonus, bout, dch = (co.sem(f"r7f{half}_{y}") for y in ("loaded", "made", "tanhed", "formed", "rk", "bonus", "bout", "dch"))
    with nc.Block() as block:
        @block.sync
        def _(sp):
            sp.dma_start(x.w2a2[0:64, :], w2).then_inc(loaded, 16)
            sp.dma_start(x.w2a2[64:128, :], a2).then_inc(loaded, 16)

        @block.tensor
        def _(pe):
            pe.wait_ge(loaded, 32)
            for j in range(2):
                cols = slice((x.b0 + j) * P, (x.b0 + j + 1) * P)
                if j:
                    pe.wait_ge(tanhed, 2)
                for h in range(2):
                    for part in range(2):
                        rows = slice(64 * part, 64 * part + 64)
                        last = nc.tensor.matmul(co.ps[:, 2 * part + h, :], x.w2a2[rows, cols], x.wa[rows, h * 512:(h + 1) * 512], start=True, stop=True)
                last.then_inc(made, 1)
            for j in range(2):
                pe.wait_ge(formed, j + 1)
                for h in range(2):
                    last = nc.tensor.matmul(co.ps[:, 4 + 2 * j + h, :], x.rk1[j], x.t[2 + j][:, h * 512:(h + 1) * 512], start=True, stop=True)
                last.then_inc(bonus, 1)

        @block.scalar
        def _(act):
            for j in range(2):
                act.wait_ge(made, j + 1)
                for part, (out, bias) in enumerate(((x.lw[j], "w0"), (x.b[:, j, :], "a0"))):
                    nc.scalar.activation(out, co.ps[:, 2 * part:2 * part + 2, :].rearrange("p h t -> p (h t)"), ACT.Tanh, bias=c_(bias, j), scale=0.5).then_inc(tanhed, 1)

        @block.vector
        def _(dve):
            link = Chain(dve, dch)
            for j in range(2):
                link(nc.vector.tensor_scalar(x.rk1[j], co.at(A_CST + C_ONE2, (P,)), c_("r_k", j), None, ALU.mult))
            for j in range(2):
                link(nc.vector.tensor_scalar(x.kk[:, j, :], x.k[:, j, :], c_("k_k", j), None, ALU.mult))
                dve.wait_ge(tanhed, 2 * j + 2)
                link(nc.vector.tensor_scalar(x.lw[j], x.lw[j], LOGW / 2, LOGW / 2, ALU.mult, ALU.add))
                link(nc.vector.tensor_scalar(x.b[:, j, :], x.b[:, j, :], 0.5, 0.5, ALU.mult, ALU.add))
                link(nc.vector.tensor_scalar(x.t[j], x.b[:, j, :], c_("k_a", j), c_("omka", j), ALU.mult, ALU.add))
                link(nc.vector.tensor_tensor(x.k[:, j, :], x.k[:, j, :], x.t[j], ALU.mult))
                nc.vector.tensor_tensor(x.t[2 + j], x.r[:, j, :], x.k[:, j, :], ALU.mult).then_inc(formed, 1)
            for j in range(2):
                dve.wait_ge(bonus, j + 1)
                nc.vector.tensor_tensor(x.bon[:, j, :], co.ps[:, 4 + 2 * j:6 + 2 * j, :].rearrange("p h t -> p (h t)"), x.v[:, j, :], ALU.mult).then_inc(bout, 1)


def r7_decay(co, half):
    nc = co.nc
    x = R7(co, half)
    summed, centred, shifted, expd, rated, used, sc, scd, dch = (co.sem(f"r7d{half}_{y}") for y in ("summed", "centred", "shifted", "expd", "rated", "used", "sc", "scd", "dch"))
    startm = co.at(A_CST + C_START, (T,))
    v3 = lambda ap: ap.rearrange("p (c t) -> p c t", t=P)
    e = [[x.t[4 * j + i] for i in range(3)] for j in range(2)]
    with nc.Block() as block:
        @block.vector
        def _(dve):
            link = Chain(dve, dch)
            tt = nc.vector.tensor_tensor
            for j in range(2):
                g = v3(x.gg[j])
                link(nc.vector.tensor_tensor_scan(x.gg[j], startm, x.lw[j], 0.0, ALU.mult, ALU.add))
                mid, end = g[:, :, P // 2 - 1], g[:, :, P - 1]
                link(tt(x.scale[:, j, :], end, mid, ALU.subtract))
                tt(x.scale[:, j, 0:NT - 1], x.scale[:, j, 0:NT - 1], g[:, 1:NT, P // 2 - 1], ALU.add).then_inc(sc, 1)
                tt(v3(x.t[4 * j + 3]), g, g[:, :, P // 2 - 1:P // 2].to_broadcast([P, NT, P]), ALU.subtract).then_inc(centred, 1)
            for j in range(2):
                dve.wait_ge(expd, 3 * j + 3)
                tt(x.r[:, j, :], x.r[:, j, :], e[j][0], ALU.mult).then_inc(used, 1)
                tt(x.k[:, j, :], x.k[:, j, :], e[j][1], ALU.mult).then_inc(used, 1)
                dve.wait_ge(rated, j + 1)
                tt(x.b[:, j, :], x.b[:, j, :], e[j][1], ALU.mult).then_inc(used, 1)
                tt(x.kk[:, j, :], x.kk[:, j, :], e[j][2], ALU.mult).then_inc(used, 1)

        @block.gpsimd
        def _(pool):
            for j in range(2):
                nc.gpsimd.tensor_tensor(x.b[:, j, :], x.b[:, j, :], x.kk[:, j, :], ALU.mult).then_inc(rated, 1)
                pool.wait_ge(centred, j + 1)
                nc.gpsimd.tensor_tensor(e[j][2], x.t[4 * j + 3], x.lw[j], ALU.subtract).then_inc(shifted, 1)

        @block.scalar
        def _(act):
            for j in range(2):
                act.wait_ge(centred, j + 1)
                nc.scalar.activation(e[j][0], x.t[4 * j + 3], ACT.Exp).then_inc(expd, 1)
                nc.scalar.activation(e[j][1], x.t[4 * j + 3], ACT.Exp, scale=-1.0).then_inc(expd, 1)
                act.wait_ge(shifted, j + 1)
                nc.scalar.activation(e[j][2], e[j][2], ACT.Exp).then_inc(expd, 1)
                nc.scalar.activation(x.scale[:, j, :], x.scale[:, j, :], ACT.Exp).then_inc(scd, 1)


def r7_pairs(co, half):
    nc = co.nc
    x = R7(co, half)
    store = co.at(A_BIG, (NT * 4, 4, P))
    mask = co.at(A_CST + C_M4, (4, P)).bitcast(I32)
    zeroed, made, kept = (co.sem(f"r7p{half}_{y}") for y in ("zeroed", "made", "kept"))
    with nc.Block() as block:
        @block.gpsimd
        def _(pool):
            for i in range(4):
                nc.gpsimd.memset(store[:, 8 * i + 4:8 * i + 8, :, :], 0.0).then_inc(zeroed, 1)

        @block.tensor
        def _(pe):
            for c in range(NT):
                ct = slice(c * P, (c + 1) * P)
                for h in range(4):
                    n = 4 * c + h
                    j, rows = h // 2, slice(64 * (h % 2), 64 * (h % 2) + 64)
                    if n >= 8:
                        pe.wait_ge(kept, n - 7)
                    for m, key in enumerate((x.b, x.k)):
                        for o, query in enumerate((x.r, x.kk)):
                            last = nc.tensor.matmul(co.ps[:, n % 8, (2 * m + o) * P:(2 * m + o + 1) * P], key[rows, j, ct], query[rows, j, ct], start=True, stop=True)
                    last.then_inc(made, 1)

        @block.vector
        def _(dve):
            link = Chain(dve, co.sem(f"r7p{half}_cleared"))
            for i in range(4):
                link(nc.vector.memset(store[:, 8 * i:8 * i + 4, :, :], 0.0))
            dve.wait_ge(zeroed, 4)
            for n in range(4 * NT):
                dve.wait_ge(made, n + 1)
                nc.vector.copy_predicated(store[:, n, :, :], mask, co.ps[:, n % 8, :].rearrange("p (s t) -> p s t", s=4)).then_inc(kept, 1)


def r7_state(co, half):
    nc = co.nc
    x = R7(co, half)
    store = co.at(A_BIG, (NT * 4, 4, P))
    ident = co.at(A_CST + C_ID, (P,))
    tok = [[co.at(A_T + 384 * (2 * j + i), (3, P)) for i in range(2)] for j in range(2)]
    S = [co.at(A_T + 1536 + P * j, (P,)) for j in range(2)]
    R = [co.at(A_T + 1792 + P * j, (P,)) for j in range(2)]
    SA = [co.at(A_T + 2048 + P * j, (P,)) for j in range(2)]
    zeroed, turned, tok_out, rs, r_out, solved, sa_out, ys, y_out, grown, added, updated = (
        co.sem(f"r7s{half}_{y}") for y in ("zeroed", "turned", "tok_out", "rs", "r_out", "solved", "sa_out", "ys", "y_out", "grown", "added", "updated"))
    bank = lambda b, j: co.ps[:, 2 * b + j, 0:P]
    with nc.Block() as block:
        @block.gpsimd
        def _(pool):
            for j in range(2):
                nc.gpsimd.memset(S[j], 0.0).then_inc(zeroed, 1)

        @block.tensor
        def _(pe):
            pe.wait_ge(zeroed, 2)

            def turn(c):
                for j in range(2):
                    if c:
                        pe.wait_ge(tok_out, 2 * (c - 1) + j + 1)
                    for i, src in enumerate((x.b, x.k, x.v)):
                        last = nc.tensor.transpose(co.ps[:, j, i * P:(i + 1) * P], src[:, j, c * P:(c + 1) * P], ident)
                    last.then_inc(turned, 1)

            turn(0)
            for c in range(NT):
                ct = slice(c * P, (c + 1) * P)
                for j in range(2):
                    n = 2 * c + j
                    if c:
                        pe.wait_ge(updated, 2 * (n - 1))
                    pe.wait_ge(tok_out, n + 1)
                    nc.tensor.matmul(bank(1, j), x.kk[:, j, ct], S[j], start=True, stop=False)
                    for h in range(2):
                        last = nc.tensor.matmul(bank(1, j)[:, 64 * h:64 * h + 64], store[:, 4 * c + 2 * j + h, 3, :],
                                                tok[j][c % 2][:, 2, 64 * h:64 * h + 64], start=False, stop=h == 1)
                    last.then_inc(rs, 1)
                if c + 1 < NT:
                    turn(c + 1)
                for j in range(2):
                    n = 2 * c + j
                    pe.wait_ge(r_out, n + 1)
                    for h in range(2):
                        last = nc.tensor.matmul(bank(2, j)[:, 64 * h:64 * h + 64], store[:, 4 * c + 2 * j + h, 1, :], R[j][:, 64 * h:64 * h + 64], start=True, stop=True)
                    last.then_inc(solved, 1)
                for j in range(2):
                    n = 2 * c + j
                    pe.wait_ge(sa_out, n + 1)
                    nc.tensor.matmul(bank(2, j), tok[j][c % 2][:, 1, :], tok[j][c % 2][:, 2, :], start=True, stop=False)
                    nc.tensor.matmul(bank(2, j), tok[j][c % 2][:, 0, :], SA[j], start=False, stop=True).then_inc(grown, 1)
                    if c:
                        pe.wait_ge(y_out, n - 1)
                    nc.tensor.matmul(bank(3, j), x.r[:, j, ct], S[j], start=True, stop=False)
                    for h in range(2):
                        cols = slice(64 * h, 64 * h + 64)
                        nc.tensor.matmul(bank(3, j)[:, cols], store[:, 4 * c + 2 * j + h, 2, :], tok[j][c % 2][:, 2, cols], start=False, stop=False)
                        last = nc.tensor.matmul(bank(3, j)[:, cols], store[:, 4 * c + 2 * j + h, 0, :], SA[j][:, cols], start=False, stop=h == 1)
                    last.then_inc(ys, 1)

        @block.vector
        def _(dve):
            link = Chain(dve, added)
            for c in range(NT):
                for j in range(2):
                    n = 2 * c + j
                    dve.wait_ge(rs, n + 1)
                    if c:
                        dve.wait_ge(solved, n - 1)
                    nc.vector.tensor_copy(R[j], bank(1, j)).then_inc(r_out, 1)
                for j in range(2):
                    n = 2 * c + j
                    dve.wait_ge(ys, n + 1)
                    for h in range(2):
                        d = slice(64 * h, 64 * h + 64)
                        link(nc.vector.tensor_tensor(S[j][d, d], S[j][d, d], co.ps[d, 4 + j, d], ALU.add))
                        nc.vector.tensor_scalar(S[j][d, d], S[j][d, d], x.scale[d, j, c:c + 1], None, ALU.mult).then_inc(updated, 1)

        @block.scalar
        def _(act):
            def take(c):
                for j in range(2):
                    act.wait_ge(turned, 2 * c + j + 1)
                    if c >= 2:
                        act.wait_ge(ys, 2 * (c - 2) + j + 1)
                    nc.scalar.activation(tok[j][c % 2], co.ps[:, j, 0:3 * P].rearrange("p (i t) -> p i t", i=3), ACT.Copy).then_inc(tok_out, 1)

            take(0)
            for c in range(NT):
                if c + 1 < NT:
                    take(c + 1)
                for j in range(2):
                    n = 2 * c + j
                    act.wait_ge(solved, n + 1)
                    if c:
                        act.wait_ge(ys, n - 1)
                    nc.scalar.activation(SA[j], bank(2, j), ACT.Copy, scale=-1.0).then_inc(sa_out, 1)
                for j in range(2):
                    act.wait_ge(ys, 2 * c + j + 1)
                    nc.scalar.activation(x.kk[:, j, c * P:(c + 1) * P], bank(3, j), ACT.Copy).then_inc(y_out, 1)


def r7_finish(co, half, zd):
    nc = co.nc
    x = R7(co, half)
    y = x.kk.rearrange("p j (g v) -> p (j g) v", v=64)
    sq = co.at(A_BIG, (32, 64))
    yt = [co.at(A_BIG + 2048 + 1024 * j, (T,)) for j in range(2)]
    mean, var, rs = (co.at(A_MISC + 680 + 32 * i, (32,)) for i in range(3))
    ident = co.at(A_CST + C_ID, (P,))
    summed, rooted, normed, turned, mapped, done, dch = (co.sem(f"r7n{half}_{y_}") for y_ in ("summed", "rooted", "normed", "turned", "mapped", "done", "dch"))
    c_ = lambda n, j: x.cols[n][:, x.b0 + j:x.b0 + j + 1]
    with nc.Block() as block:
        @block.vector
        def _(dve):
            link = Chain(dve, dch)
            link(nc.vector.tensor_reduce(mean, y, AX, ALU.add))
            link(nc.vector.tensor_scalar(mean, mean, 1.0 / 64, None, ALU.mult))
            link(nc.vector.tensor_tensor(y, y, bc(mean, 64), ALU.subtract))
            link(nc.vector.tensor_tensor(sq, y, y, ALU.mult))
            nc.vector.tensor_reduce(var, sq, AX, ALU.add).then_inc(summed, 1)
            dve.wait_ge(rooted, 1)
            link(nc.vector.reciprocal(rs, rs))
            nc.vector.tensor_tensor(y, y, bc(rs, 64), ALU.mult).then_inc(normed, 1)
            for j in range(2):
                dve.wait_ge(mapped, j + 1)
                link(nc.vector.tensor_tensor(yt[j], yt[j], x.bon[:, j, :], ALU.add))
                nc.vector.tensor_tensor(zd[x.b0 + j], zd[x.b0 + j], yt[j], ALU.mult).then_inc(done, 1)

        @block.scalar
        def _(act):
            act.wait_ge(summed, 1)
            nc.scalar.activation(rs, var, ACT.Sqrt, bias=co.at(co.eps_at[GN_EPS], (1,)), scale=1.0 / 64).then_inc(rooted, 1)
            for j in range(2):
                act.wait_ge(turned, j + 1)
                nc.scalar.activation(yt[j], co.ps[:, 2 * j:2 * j + 2, :].rearrange("p h t -> p (h t)"), ACT.Identity, bias=c_("ln_b", j), scale=c_("ln_w", j)).then_inc(mapped, 1)

        @block.tensor
        def _(pe):
            pe.wait_ge(normed, 1)
            for j in range(2):
                for c in range(NT):
                    last = nc.tensor.transpose(co.ps[:, 2 * j + c // 4, (c % 4) * P:(c % 4 + 1) * P], x.kk[:, j, c * P:(c + 1) * P], ident)
                last.then_inc(turned, 1)


def odd_layer(co, a, x, dst):
    nc = co.nc
    u5 = nc.dram_tensor("u_by_chunk", (W, SC8, P), F32, kind="Internal").ap()
    y5 = nc.dram_tensor("y_by_chunk", (W, SC8, P), F32, kind="Internal").ap()
    u, r, k, v, zc, zd = ([co.at(A_F[i] + T * b, (T,)) for b in range(WB)] for i in (0, 1, 2, 3, 5, 6))
    norm_transpose(co, "on", x, a["odd_norm"][0])
    blocks = [(ODD["u"] + P * b, "plain", u[b]) for b in range(WB)]
    blocks += [(ODD["zc"] + P * b, "gate", zc[b]) for b in range(WB)]
    blocks += [(ODD[n] + P * b, "shift", y[b]) for n, y in (("r", r), ("k", k), ("v", v)) for b in range(WB)]
    blocks += [(ODD["wa"], "shift", co.at(A_F[4], (T,)))]
    blocks += [(ODD["zd"] + P * b, "gate", zd[b]) for b in range(WB)]
    project(co, "op", a["odd_w_in"][0], blocks, mu=a["rwkv_mu"][0])
    s5_store_u(co, co.at(A_F[0], (WB, T)), u5)
    s5_tables(co, a, u5)
    s5_toeplitz(co)
    s5_scan(co, y5)
    s5_glu(co, a["s5_d"][0], a["s5_w_glu"][0], u5, y5, zc)
    r7_start(co, a)
    for half in range(2):
        f = R7(co, half)
        r7_features(co, half, a["rwkv_w2"][0], a["rwkv_a2"][0])
        norm_blocks(co, f"rn{half}", [(f.kk[:, j, :], 64, 1.0, L2_EPS, 1.0) for j in range(2)])
        r7_decay(co, half)
        r7_pairs(co, half)
        invert(co, f"ri{half}", store_slot(co, 1), (A_T, A_F[4] + 3072), (A_T + 1024, A_T + 1536), (A_T + 2048, A_T + 2560))
        r7_state(co, half)
        r7_finish(co, half, zd)
        if half == 0:
            co.end_part()
    project_out(co, "oout", a["odd_w_out"][0], zc + zd, x, dst, co.output_stored)


INPUTS = ["x", "even_norm", "even_w_in", "gdn_conv_w", "gdn_a_log", "gdn_dt_bias", "gdn_out_norm", "swa_q_norm", "swa_k_norm",
          "swa_sinks", "even_w_out", "rel_bias", "odd_norm", "odd_w_in", "s5_lambda_re", "s5_lambda_im", "s5_log_step",
          "s5_b_re", "s5_b_im", "s5_c_re", "s5_c_im", "s5_d", "s5_w_glu", "rwkv_mu", "rwkv_w0", "rwkv_w2", "rwkv_a0",
          "rwkv_a2", "rwkv_k_k", "rwkv_k_a", "rwkv_r_k", "rwkv_ln_w", "rwkv_ln_b", "odd_w_out"]


def build(nc, a, cst, out):
    with ExitStack() as ctx:
        co = Core(nc, ctx)
        h = nc.dram_tensor("h_between_layers", (T, D), F32, kind="Internal").ap()
        start(co, cst)
        even_layer(co, a, a["x"][0], h)
        co.end_part()
        odd_layer(co, a, h, out[0])


def kernel(**inputs):
    import concourse.bacc as bacc
    from concourse.bass_utils import run_bass_kernel_spmd

    nc = bacc.Bacc("TRN2", target_bir_lowering=False, num_devices=1)
    arrays = {f"in_{n}": np.ascontiguousarray(inputs[n]) for n in INPUTS}
    a = {n: nc.dram_tensor(f"in_{n}", arrays[f"in_{n}"].shape, F32, kind="ExternalInput").ap() for n in INPUTS}
    arrays["constants"] = constants()
    cst = nc.dram_tensor("constants", (P, C_ALL), F32, kind="ExternalInput").ap()
    out = nc.dram_tensor("out", (1, T, D), F32, kind="ExternalOutput").ap()
    build(nc, a, cst, out)
    r = run_bass_kernel_spmd(nc, [arrays], core_ids=[0])
    return r.results[0]["out"]
```

```python
from contextlib import ExitStack
import math

import numpy as np
import concourse.bass as bass
from concourse import mybir

F32 = mybir.dt.float32
F32R = mybir.dt.float32r
I32 = mybir.dt.int32
ALU = mybir.AluOpType
ACT = mybir.ActivationFunctionType
AX = mybir.AxisListType.X

D, T, P = 1024, 1024, 128
KT = D // P
NT = T // P
W = D // 2
WB = W // P
HG = 4
RMS_EPS, L2_EPS, GN_EPS = 1e-6, 1e-6, 64e-5
EVEN = dict(q=0, k=W, v=2 * W, beta=3 * W, za=3 * W + 2 * HG, qb=4 * W + 2 * HG, kb=5 * W + 2 * HG,
            vb=5 * W + 2 * HG + P, zb=5 * W + 2 * HG + 2 * P)
EVEN_COLS = 6 * W + 2 * HG + 2 * P
ODD = dict(u=0, zc=W, r=2 * W, k=3 * W, v=4 * W, wa=5 * W, zd=5 * W + P)
ODD_COLS = 6 * W + P
NEG = -1.0e30
LEVELS = (1, 2, 4, 8, 16, 32, 64)

C_ID, C_ONE, C_ONE2 = 0, 128, 256
C_UT0 = C_M4 = 384

C_LEV = 896
C_HOT = C_LEV + 128 * len(LEVELS)
C_START = C_HOT + 192
C_SUM = C_START + 1024
C_SUM2 = C_SUM + 63
C_PARAM = C_SUM2 + 63
C_ALL = C_PARAM + 6


def constants():
    c = np.zeros((P, C_ALL), np.float32)
    j, i = np.arange(P)[:, None], np.arange(P)[None, :]
    c[:, C_ID:C_ID + P] = j == i
    c[:, C_ONE:C_ONE + P] = 1
    c[:, C_ONE2:C_ONE2 + P] = j // 64 == i // 64
    for m in range(2):
        c[:, C_M4 + 256 * m:C_M4 + 256 * m + P] = j <= i
        c[:, C_M4 + 256 * m + P:C_M4 + 256 * m + 2 * P] = j < i
    for n, s in enumerate(LEVELS):
        c[:, C_LEV + P * n:C_LEV + P * (n + 1)] = (j // (2 * s) == i // (2 * s)) & (j % (2 * s) < s) & (i % (2 * s) >= s)
    rel = np.arange(191) - 127
    half, exact = 16, 8
    n = np.abs(rel)
    large = exact + (np.log(np.maximum(n, 1) / exact) / np.log(128 / exact) * (half - exact)).astype(np.int32)
    bucket = (rel > 0) * half + np.where(n < exact, n, np.minimum(large, half - 1))
    c[bucket, C_HOT + np.arange(191)] = 1
    c[:, C_START:C_START + T] = np.arange(T) % P != 0
    c[:, C_SUM + 31] = 1
    c[:64, C_SUM2 + 31] = 1
    c[64:, C_SUM2 + 32] = 1
    c[:, C_PARAM], c[:, C_PARAM + 1] = 1, 1
    for at, n, scale, eps in ((0, 8, 1, 64 * RMS_EPS), (8, 2, 1 / 64, RMS_EPS), (10, 4, 128, 128 * L2_EPS), (14, 4, 1, L2_EPS)):
        c[at:at + n, C_PARAM], c[at:at + n, C_PARAM + 1] = scale, eps
    c[:, C_PARAM + 2], c[:, C_PARAM + 3] = 1 / 128, RMS_EPS
    c[:, C_PARAM + 4], c[:, C_PARAM + 5] = 1, L2_EPS
    return c


class Core:

    def __init__(self, nc, ctx):
        self.nc, self.ctx = nc, ctx
        self.n_sem = 0
        self.taken = []
        self.output_stored = [nc.alloc_semaphore(name=f"output_stored{i}") for i in range(3)]
        ctx.enter_context(nc.allow_non_contiguous_dma(reason="per-channel vectors"))
        self.base = -(-nc.sbuf_base // 64) * 64
        self.areas = [(lo, hi, nc.alloc_sbuf_tensor_at(name, [P, hi - lo], F32, offset=self.base + 4 * lo))
                      for name, lo, hi in AREAS]
        self.ps = ctx.enter_context(nc.psum_tensor("banks", [P, 8, 512], F32))

    def sem(self, name):
        handle = self.nc.alloc_semaphore(name=name)
        self.n_sem += 1
        self.taken.append(handle)
        return handle

    def end_part(self):
        with self.nc.Block() as block:
            @block.gpsimd
            def _(pool):
                for handle in self.taken:
                    pool.sem_clear(handle)
        for handle in self.taken:
            self.nc.release_semaphore(handle)
        self.taken = []

    def rounded(self, name, col, shape):
        t = self.nc.alloc_sbuf_tensor_at(name, [P, int(np.prod(shape))], F32R, offset=self.base + 4 * col)
        v = t[:, :]
        if len(shape) == 2:
            v = v.rearrange("p (a b) -> p a b", b=shape[1])
        return v

    def at(self, col, shape, rows=(0, P)):
        n = int(np.prod(shape))
        (lo, area), = [(lo, area) for lo, hi, area in self.areas if lo <= col and col + n <= hi]
        v = area[rows[0]:rows[1], col - lo:col - lo + n]
        if len(shape) == 1:
            return v
        names = "abcd"[:len(shape)]
        return v.rearrange(f"p ({' '.join(names)}) -> p {' '.join(names)}", **{x: s for x, s in zip(names[1:], shape[1:])})


A_CST = 0
A_MISC = 3200
A_BIG = 4224
A_F = [20608 + 4096 * i for i in range(7)]
A_T = 49280
AREAS = (("constants", A_CST, A_BIG), ("big", A_BIG, A_F[0]), ("features", A_F[0], A_T), ("temporaries", A_T, 53168))


class Chain:

    def __init__(self, eng, sem):
        self.eng, self.sem, self.n = eng, sem, 0

    def __call__(self, ins):
        self.n += 1
        ins.then_inc(self.sem, 1)
        self.eng.wait_ge(self.sem, self.n)


def bc(ap, n):
    p, a = ap.shape
    return ap.rearrange("p (a o) -> p a o", o=1).to_broadcast([p, a, n])


def three_passes(nc, out, w, x, start, stop):
    nc.tensor.matmul(out, w[0], x[1], start=start, stop=False)
    nc.tensor.matmul(out, w[1], x[0], start=False, stop=False)
    return nc.tensor.matmul(out, w[0], x[0], start=False, stop=stop)


def norm_transpose(co, tag, src, gain, ahead, constants_in=None):
    nc = co.nc
    xh, xl = co.xt
    ring = [co.at(A_F[0] + 1024 * i, (D,)) for i in range(4)]
    junk = co.at(A_T, (D,))
    tmp = [co.at(A_T + 1024 + 512 * i, (4, P)) for i in range(4)]
    gn = co.at(A_MISC, (KT,))
    ss, sd, rs = (co.at(A_MISC + 8 + 8 * i, (NT,)) for i in range(3))
    ident = co.at(A_CST + C_ID, (P,))
    loaded = [co.sem(f"{tag}_loaded{i}") for i in range(4)]
    gained, summed, squared, rooted, inverted, scaled, turned, gained_x, high, low_even, low_odd, one_hot = (
        co.sem(f"{tag}_{x}") for x in ("gain", "summed", "squared", "rooted", "inverted", "scaled", "turned", "gained_x", "high",
                                       "low_even", "low_odd", "one_hot"))
    part = lambda x, n: x[:, 4 * (n % 2):4 * (n % 2) + 4, (n // 2) * P:(n // 2 + 1) * P]
    with nc.Block() as block:
        @block.sync
        def _(sp):
            for i in range(NT):
                if i >= 4:
                    sp.wait_ge(turned, 2 * (i - 3))
                sp.dma_start(ring[i % 4], src[i * P:(i + 1) * P, :]).then_inc(loaded[i % 4], 16)
                if i == 0:
                    sp.dma_start(gn, gain.rearrange("(k p) -> p k", p=P)).then_inc(gained, 16)
            for to, what, sem in ahead:
                sp.dma_start(to, what).then_inc(sem, 16)

        @block.scalar
        def _(act):
            def high_part(n):
                act.wait_ge(gained_x, n + 1)
                nc.scalar.activation(part(xh, n), tmp[n % 4], ACT.Copy).then_inc(high, 1)

            def square(i):
                act.wait_ge(loaded[i % 4], 16 * (i // 4 + 1))
                if i:
                    act.wait_ge(summed, i)
                nc.scalar.activation(junk, ring[i % 4], ACT.Square, accum_out=ss[:, i:i + 1]).then_inc(summed, 1)

            square(0)
            for i in range(NT):
                if i + 1 < NT:
                    square(i + 1)
                act.wait_ge(squared, i + 1)
                nc.scalar.activation(sd[:, i:i + 1], ss[:, i:i + 1], ACT.Sqrt).then_inc(rooted, 1)
                if i:
                    high_part(2 * i - 2)
                    high_part(2 * i - 1)
            high_part(2 * NT - 2)
            high_part(2 * NT - 1)
            if constants_in is not None:
                act.wait_ge(constants_in, 16)
                nc.scalar.activation(co.hot_r, co.at(A_CST + C_ID, (32,)), ACT.Copy).then_inc(one_hot, 1)

        @block.vector
        def _(dve):
            def gained_part(n):
                dve.wait_ge(turned, n + 1)
                if n >= 4:
                    dve.wait_ge((low_even, low_odd)[n % 2], n // 2 - 1)
                nc.vector.tensor_tensor(tmp[n % 4], co.ps[:, n % 8, :].rearrange("p (k t) -> p k t", t=P),
                                        bc(gn[:, 4 * (n % 2):4 * (n % 2) + 4], P), ALU.mult).then_inc(gained_x, 1)

            def low_part(n):
                dve.wait_ge(high, n + 1)
                nc.vector.tensor_tensor(part(xl, n), tmp[n % 4], part(xh, n).bitcast(F32), ALU.subtract).then_inc(low_odd, 1)

            dve.wait_ge(gained, 16)
            for i in range(NT):
                dve.wait_ge(summed, i + 1)
                nc.vector.tensor_scalar(ss[:, i:i + 1], ss[:, i:i + 1], 1.0 / D, RMS_EPS, ALU.mult, ALU.add).then_inc(squared, 1)
                if i:
                    gained_part(2 * i - 2)
                if i >= 2:
                    low_part(2 * i - 3)
                dve.wait_ge(rooted, i + 1)
                nc.vector.reciprocal(rs[:, i:i + 1], sd[:, i:i + 1]).then_inc(inverted, 1)
                dve.wait_ge(inverted, i + 1)
                nc.vector.tensor_scalar(ring[i % 4], ring[i % 4], rs[:, i:i + 1], None, ALU.mult).then_inc(scaled, 1)
                if i:
                    gained_part(2 * i - 1)
            gained_part(2 * NT - 2)
            low_part(2 * NT - 3)
            gained_part(2 * NT - 1)
            low_part(2 * NT - 1)

        @block.gpsimd
        def _(pool):
            for n in range(0, 2 * NT, 2):
                pool.wait_ge(high, n + 1)
                nc.gpsimd.tensor_tensor(part(xl, n), tmp[n % 4], part(xh, n).bitcast(F32), ALU.subtract).then_inc(low_even, 1)

        @block.tensor
        def _(pe):
            if constants_in is not None:
                pe.wait_ge(constants_in, 16)
            for i in range(NT):
                pe.wait_ge(scaled, i + 1)
                for h in range(2):
                    n = 2 * i + h
                    if n >= 8:
                        pe.wait_ge(gained_x, n - 7)
                    for k in range(4):
                        last = nc.tensor.transpose(co.ps[:, n % 8, k * P:(k + 1) * P],
                                                   ring[i % 4][:, (4 * h + k) * P:(4 * h + k + 1) * P], ident)
                    last.then_inc(turned, 1)


def weight_slot(co, n):
    return co.at(A_F[5] + 1024 * (n % 3), (KT, P))


def project_ahead(co, tag, w, blocks, small=None):
    co.weights_in = [co.sem(f"{tag}_w{i}") for i in range(3)]
    co.small_in = co.sem(f"{tag}_small_in")
    loads = [(weight_slot(co, n), w[:, blocks[n][0]:blocks[n][0] + P].rearrange("(k p) n -> p k n", p=P), co.weights_in[n]) for n in range(3)]
    if small is not None:
        loads.insert(0, (co.at(A_MISC + 128, (KT, 8)), w[:, small[0]:small[0] + small[1]].rearrange("(k p) n -> p k n", p=P), co.small_in))
    return loads


def project(co, tag, w, blocks, conv_w=None, small=None, mu=None, also=None):
    nc = co.nc
    xh, xl = co.xt
    NW = 3
    wr = [weight_slot(co, i) for i in range(NW)]
    wh, wl = co.w_parts
    RAW = T + 4
    raw = [co.at(A_T + RAW * i, (RAW,)) for i in range(2)]
    tmp = [co.at(A_F[5] + 7168, (T,)), co.at(A_T + 2 * RAW, (T,))]
    cw = co.at(A_MISC + 64, (12, 4))
    mus = co.at(A_MISC + 64, (13,))
    wsmall = co.at(A_MISC + 128, (KT * 8,))
    sh, sl = co.small_parts
    loaded, small_in = co.weights_in, co.small_in
    narrow = co.at(A_F[4] + 3072, (T,), (0, 8))
    spilled = [co.sem(f"{tag}_spilled{i}") for i in range(2)]
    cw_in, cw_half, high, low, small_high, small_low, multiplied, evacuated, convolved, tanhed, finished, small_done, small_taken, small_turned, small_out, pads, dch = (
        co.sem(f"{tag}_{x}") for x in ("cw_in", "cw_half", "high", "low", "small_high", "small_low", "multiplied", "evacuated", "convolved",
                                       "tanhed", "finished", "small_done", "small_taken", "small_turned", "small_out", "pads", "dch"))
    NB = len(blocks)
    slot_no, conv_no, post_no, gate_no = {}, {}, {}, {}
    for n, (_, kind, _) in enumerate(blocks):
        for kinds, no in ((("conv", "shift", "gate"), slot_no), (("conv", "shift"), conv_no), (("conv", "gate"), post_no), (("gate",), gate_no)):
            if kind in kinds:
                no[n] = len(no)
    by_slot = {c: n for n, c in slot_no.items()}
    spills = {n: 16 * (1 + sum(slot_no[m] % 2 == slot_no[n] % 2 for m in gate_no if m < n)) for n in gate_no}
    with nc.Block() as block:
        @block.sync
        def _(sp):
            for n, (col, _, _) in enumerate(blocks):
                if n >= NW:
                    sp.wait_ge(low, n - NW + 1)
                    sp.dma_start(wr[n % NW], w[:, col:col + P].rearrange("(k p) n -> p k n", p=P)).then_inc(loaded[n % NW], 16)
                if n == 0 and conv_w is not None:
                    for j in range(4):
                        sp.dma_start(cw[:, :, j], conv_w[j, :].rearrange("(b p) -> p b", p=P)).then_inc(cw_in, 16)
                if n == 0 and mu is not None:
                    sp.dma_start(mus, mu.rearrange("(b p) -> p b", p=P)).then_inc(cw_in, 16)
            if also is not None:
                sp.wait_ge(*also)

        @block.tensor
        def _(pe):
            if small is not None:
                pe.wait_ge(small_low, 1)
                for h in range(2):
                    for k in range(KT):
                        last = three_passes(nc, co.ps[0:8, 4 + h, :], (sh[:, k, :], sl[:, k, :]), [x[:, k, h * 512:(h + 1) * 512] for x in (xh, xl)],
                                            k == 0, k == KT - 1)
                last.then_inc(small_done, 1)
            for n in range(NB):
                if n == 1 and small is not None:
                    pe.wait_ge(small_taken, 1)
                    for t in range(NT):
                        last = nc.tensor.transpose(co.ps[:, 6, t * 8:(t + 1) * 8], narrow[:, t * P:(t + 1) * P], co.at(A_CST + C_ID, (8,), (0, 8)))
                    last.then_inc(small_turned, 1)
                pe.wait_ge(low, n + 1)
                if n >= 2:
                    pe.wait_ge(evacuated, n - 1)
                for h in range(2):
                    hs = slice(h * 512, (h + 1) * 512)
                    for k in range(KT):
                        last = three_passes(nc, co.ps[:, 2 * (n % 2) + h, :], (wh[n % 2][:, k, :], wl[n % 2][:, k, :]), (xh[:, k, hs], xl[:, k, hs]),
                                            k == 0, k == KT - 1)
                last.then_inc(multiplied, 1)

        @block.gpsimd
        def _(pool):
            for r in raw:
                nc.gpsimd.memset(r[:, 0:4], 0.0).then_inc(pads, 1)
            if small is not None:
                pool.wait_ge(small_high, 1)
                nc.gpsimd.tensor_tensor(sl.rearrange("p k n -> p (k n)"), wsmall, sh.rearrange("p k n -> p (k n)").bitcast(F32), ALU.subtract).then_inc(small_low, 1)
            for n in range(NB):
                pool.wait_ge(high, n + 1)
                nc.gpsimd.tensor_tensor(wl[n % 2], wr[n % NW], wh[n % 2].bitcast(F32), ALU.subtract).then_inc(low, 1)

        @block.scalar
        def _(act):
            def high_part(n):
                act.wait_ge(loaded[n % NW], 16 * (n // NW + 1))
                if n >= 2:
                    act.wait_ge(multiplied, n - 1)
                nc.scalar.activation(wh[n % 2], wr[n % NW], ACT.Copy).then_inc(high, 1)

            def spill(n):
                act.wait_ge(finished, post_no[n] + 1)
                act.dma_start(blocks[n][2], raw[slot_no[n] % 2][:, 4:4 + T]).then_inc(spilled[slot_no[n] % 2], 16)

            if small is not None:
                act.wait_ge(small_in, 16)
                nc.scalar.activation(sh.rearrange("p k n -> p (k n)"), wsmall, ACT.Copy).then_inc(small_high, 1)
            high_part(0)
            high_part(1)
            if small is not None:
                act.wait_ge(small_done, 1)
                nc.scalar.activation(narrow.rearrange("p (h t) -> p h t", h=2), co.ps[0:8, 4:6, :], ACT.Copy).then_inc(small_taken, 1)
            for n, (_, kind, dst) in enumerate(blocks):
                out = raw[slot_no[n] % 2][:, 4:4 + T] if n in slot_no else dst
                before = by_slot.get(slot_no.get(n, 0) - 2)
                if before in conv_no:
                    act.wait_ge(convolved, conv_no[before] + 1)
                elif before in gate_no:
                    act.wait_ge(spilled[slot_no[before] % 2], spills[before])
                act.wait_ge(multiplied, n + 1)
                nc.scalar.activation(out.rearrange("p (h t) -> p h t", h=2), co.ps[:, 2 * (n % 2):2 * (n % 2) + 2, :], ACT.Copy,
                                     scale=0.5 if kind == "gate" else 1.0).then_inc(evacuated, 1)
                if n + 2 < NB:
                    high_part(n + 2)
                if n - 1 in gate_no:
                    spill(n - 1)
                if n in post_no:
                    if kind == "conv":
                        act.wait_ge(convolved, conv_no[n] + 1)
                    act.wait_ge(evacuated, n + 1)
                    if post_no[n] >= 2:
                        act.wait_ge(finished, post_no[n] - 1)
                    nc.scalar.activation(tmp[post_no[n] % 2], out if kind == "gate" else dst, ACT.Tanh).then_inc(tanhed, 1)
            if NB - 1 in gate_no:
                spill(NB - 1)
            if small is not None:
                act.wait_ge(small_turned, 1)
                nc.scalar.activation(small[2], co.ps[:, 6, 0:NT * 8].rearrange("p (t n) -> p t n", t=NT), ACT.Copy).then_inc(small_out, 1)
            for i in range(2):
                last = max([spills[n] for n in gate_no if slot_no[n] % 2 == i], default=0)
                if last:
                    act.wait_ge(spilled[i], last)

        @block.vector
        def _(dve):
            link = Chain(dve, dch)
            dve.wait_ge(pads, 2)
            if mu is not None:
                dve.wait_ge(cw_in, 16)
            if conv_w is not None:
                dve.wait_ge(cw_in, 64)
                nc.vector.tensor_scalar(cw, cw, 0.5, None, ALU.mult).then_inc(cw_half, 1)
                dve.wait_ge(cw_half, 1)
            for n, (_, kind, dst) in enumerate(blocks):
                if n in slot_no:
                    x = raw[slot_no[n] % 2]
                if kind == "shift":
                    dve.wait_ge(evacuated, n + 1)
                    c = conv_no[n]
                    link(nc.vector.tensor_tensor(dst, x[:, 3:3 + T], x[:, 4:4 + T], ALU.subtract))
                    nc.vector.scalar_tensor_tensor(dst, dst, mus[:, c:c + 1], x[:, 4:4 + T], ALU.mult, ALU.add).then_inc(convolved, 1)
                if kind == "conv":
                    dve.wait_ge(evacuated, n + 1)
                    c = conv_no[n]
                    link(nc.vector.tensor_scalar(dst, x[:, 4:4 + T], cw[:, c, 3:4], None, ALU.mult))
                    link(nc.vector.scalar_tensor_tensor(dst, x[:, 3:3 + T], cw[:, c, 2:3], dst, ALU.mult, ALU.add))
                    link(nc.vector.scalar_tensor_tensor(dst, x[:, 2:2 + T], cw[:, c, 1:2], dst, ALU.mult, ALU.add))
                    nc.vector.scalar_tensor_tensor(dst, x[:, 1:1 + T], cw[:, c, 0:1], dst, ALU.mult, ALU.add).then_inc(convolved, 1)
                if n in post_no:
                    dve.wait_ge(tanhed, post_no[n] + 1)
                    y = x[:, 4:4 + T] if kind == "gate" else dst
                    nc.vector.scalar_tensor_tensor(y, tmp[post_no[n] % 2], 1.0, y, ALU.add, ALU.mult).then_inc(finished, 1)


def norm_blocks(co, tag, items, params, fetch=(), ahead=()):
    nc = co.nc
    R = 32
    sq = [co.at(A_T + 1024 * i, (T,)) for i in range(3)]
    rows = co.at(A_T + 2048, (T,), (0, R))
    high, low = (x[0:R, :] for x in co.row_parts)
    scale, eps = (co.at(A_CST + C_PARAM + 2 * params + i, (1,), (0, R)) for i in range(2))
    first_row = np.cumsum([0] + [P // item[1] for item in items]).tolist()
    hot = co.hot_r[0:R, :]
    pairs = co.pairs_r[0:R, :, :]
    N = len(items)
    paired, squared, summed, rooted, inverted, high_r, low_r, spread, normed, gated, fetched = (co.sem(f"{tag}_{x}") for x in (
        "paired", "squared", "summed", "rooted", "inverted", "high_r", "low_r", "spread", "normed", "gated", "fetched"))
    hs = [slice(512 * h, 512 * h + 512) for h in range(2)]
    gates = [n for n, item in enumerate(items) if item[3] is not None]
    with nc.Block() as block:
        if fetch or ahead:
            @block.sync
            def _(sp):
                for dst, src, sem in ahead:
                    sp.dma_start(dst, src).then_inc(sem, 16)
                for dst, src in fetch:
                    sp.dma_start(dst, src).then_inc(fetched, 16)
                if fetch:
                    sp.wait_ge(fetched, 16 * len(fetch))

        @block.scalar
        def _(act):
            for n, item in enumerate(items):
                if n >= 3:
                    act.wait_ge(summed, n - 2)
                nc.scalar.activation(sq[n % 3], item[0], ACT.Square).then_inc(squared, 1)
            act.wait_ge(summed, N)
            for h in range(2):
                nc.scalar.activation(rows[:, hs[h]], co.ps[0:R, h, :], ACT.Sqrt, bias=eps, scale=scale).then_inc(rooted, 1)
            for h in range(2):
                act.wait_ge(inverted, h + 1)
                nc.scalar.activation(high[:, hs[h]], rows[:, hs[h]], ACT.Copy).then_inc(high_r, 1)

        @block.gpsimd
        def _(pool):
            for n in gates:
                pool.wait_ge(squared, n + 1)
                nc.gpsimd.tensor_tensor(items[n][0], items[n][0], items[n][3], ALU.mult).then_inc(gated, 1)
            for h in range(2):
                pool.wait_ge(high_r, h + 1)
                nc.gpsimd.tensor_tensor(low[:, hs[h]], rows[:, hs[h]], high[:, hs[h]].bitcast(F32), ALU.subtract).then_inc(low_r, 1)

        @block.tensor
        def _(pe):
            for n, item in enumerate(items):
                pe.wait_ge(squared, n + 1)
                at = (C_SUM if item[1] == 128 else C_SUM2) + R - 1 - first_row[n]
                for h in range(2):
                    last = nc.tensor.matmul(co.ps[0:R, h, :], co.at(A_CST + at, (R,)), sq[n % 3][:, hs[h]], start=n == 0, stop=n == N - 1)
                last.then_inc(summed, 1)
            pe.wait_ge(paired, 1)
            pe.wait_ge(low_r, 2)
            for n, item in enumerate(items):
                if n >= 3:
                    pe.wait_ge(normed, n - 2)
                for h in range(2):
                    out = co.ps[:, 2 + 2 * (n % 3) + h, :]
                    r = first_row[n]
                    spreader = pairs[:, r // 2, :] if item[1] == 64 else hot[:, r:r + 1].to_broadcast([R, P])
                    nc.tensor.matmul(out, spreader, low[:, hs[h]], start=True, stop=False)
                    last = nc.tensor.matmul(out, spreader, high[:, hs[h]], start=False, stop=True)
                last.then_inc(spread, 1)

        @block.vector
        def _(dve):
            nc.vector.tensor_copy(co.pairs_r[0:R, :, :].rearrange("p i (m c) -> p (i m) c", c=64), bc(co.at(A_CST + C_ID, (10,), (0, R)), 64)).then_inc(paired, 1)
            for h in range(2):
                dve.wait_ge(rooted, h + 1)
                nc.vector.reciprocal(rows[:, hs[h]], rows[:, hs[h]]).then_inc(inverted, 1)
            for n, (x, group, gain, gate) in enumerate(items):
                dve.wait_ge(spread, n + 1)
                if gate is not None:
                    dve.wait_ge(gated, gates.index(n) + 1)
                v = x.rearrange("p (h t) -> p h t", h=2)
                nc.vector.scalar_tensor_tensor(v, v, gain, co.ps[:, 2 + 2 * (n % 3):4 + 2 * (n % 3), :], ALU.mult, ALU.mult).then_inc(normed, 1)


def invert(co, tag, store, xv_at, nl_at, yy_at):
    nc = co.nc
    G, NG, NS = 4, 8, len(xv_at)
    ident = co.at(A_CST + C_ID, (P,))
    xv = [co.at(x, (G, 2, P)) for x in xv_at]
    nl = [co.at(x, (G, P)) for x in nl_at]
    yy = [co.at(x, (G, P)) for x in yy_at]
    L = len(LEVELS)
    steps = L - 1
    masked, first, began, ymade, ycopied, zmade, updated = (
        co.sem(f"{tag}_{x}") for x in ("masked", "first", "began", "ymade", "ycopied", "zmade", "updated"))
    ident_b = ident.rearrange("p (o t) -> p o t", o=1).to_broadcast([P, G, P])
    level = lambda l: co.at(A_CST + C_LEV + P * l, (P,)).rearrange("p (o t) -> p o t", o=1).to_broadcast([P, G, P])
    n_of = lambda g: store[:, G * g:G * g + G, :]
    ybank = lambda i: co.ps[:, i, :].rearrange("p (m t) -> p m t", m=G)
    zbank = lambda i: co.ps[:, NS + i, :].rearrange("p (m o t) -> p m o t", m=G, o=2)

    def half(view, l, o):
        v = view.rearrange("p (b h s) -> p b h s", h=2, s=LEVELS[l]) if len(view.shape) == 2 else \
            view.rearrange("p m (b h s) -> p m b h s", h=2, s=LEVELS[l])
        return v[:, :, o, :] if len(view.shape) == 2 else v[:, :, :, o, :]

    rounds = [(q, l) for q in range(NG // NS) for l in range(1, L)]
    done = lambda q, l, i: (q * steps + l - 1) * NS + i + 1

    with nc.Block() as block:
        @block.gpsimd
        def _(pool):
            for q in range(NG // NS):
                for l in range(L):
                    for i in range(NS):
                        if l == 1:
                            pool.wait_ge(began, q * NS + i + 1)
                        elif l > 1:
                            pool.wait_ge(ymade, done(q, l - 1, i))
                        elif q:
                            pool.wait_ge(ymade, done(q - 1, L - 1, i))
                        nc.gpsimd.tensor_tensor(nl[i], n_of(q * NS + i), level(l), ALU.mult).then_inc(masked, 1)

        @block.tensor
        def _(pe):
            for q in range(NG // NS):
                for i in range(NS):
                    pe.wait_ge(masked, q * NS * L + i + 1)
                    if q:
                        pe.wait_ge(ycopied, done(q - 1, L - 1, i))
                    for m in range(G):
                        last = nc.tensor.transpose(ybank(i)[:, m, :], nl[i][:, m, :], ident)
                    last.then_inc(first, 1)
                for l in range(1, L):
                    for i in range(NS):
                        pe.wait_ge(masked, q * NS * L + l * NS + i + 1)
                        if l == 1:
                            pe.wait_ge(began, q * NS + i + 1)
                        else:
                            pe.wait_ge(updated, done(q, l - 1, i))
                        for m in range(G):
                            if l < L - 1:
                                last = nc.tensor.matmul(ybank(i)[:, m, :], nl[i][:, m, :], xv[i][:, m, 0, :], start=True, stop=True)
                            else:
                                last = nc.tensor.matmul(ybank(i)[64:P, m, 0:64], nl[i][0:64, m, 64:P], xv[i][0:64, m, 0, 0:64], start=True, stop=True)
                        last.then_inc(ymade, 1)
                    for i in range(NS):
                        pe.wait_ge(ycopied, done(q, l, i))
                        for m in range(G):
                            if l < L - 1:
                                nc.tensor.matmul(zbank(i)[:, m, 0, :], xv[i][:, m, 1, :], half(yy[i][:, m, :], l, 0), start=True, stop=True)
                                last = nc.tensor.matmul(zbank(i)[:, m, 1, :], yy[i][:, m, :], half(xv[i][:, m, 1, :], l, 1), start=True, stop=True)
                            else:
                                last = nc.tensor.matmul(zbank(i)[0:64, m, 1, :], yy[i][64:P, m, 0:64], xv[i][64:P, m, 1, 64:P], start=True, stop=True)
                        last.then_inc(zmade, 1)

        @block.scalar
        def _(act):
            for q, l in rounds:
                for i in range(NS):
                    act.wait_ge(ymade, done(q, l, i))
                    if l > 1 or q:
                        act.wait_ge(zmade, done(q, l, i) - NS)
                    if l < L - 1:
                        nc.scalar.activation(yy[i], ybank(i), ACT.Copy).then_inc(ycopied, 1)
                    else:
                        nc.scalar.activation(yy[i][64:P, :, 0:64], ybank(i)[64:P, :, 0:64], ACT.Copy).then_inc(ycopied, 1)

        @block.vector
        def _(dve):
            for q in range(NG // NS):
                for i in range(NS):
                    dve.wait_ge(first, q * NS + i + 1)
                    if q:
                        dve.wait_ge(updated, done(q - 1, L - 1, i))
                    nc.vector.tensor_tensor(xv[i][:, :, 0, :], ident_b, ybank(i), ALU.subtract)
                    nc.vector.tensor_tensor(xv[i][:, :, 1, :], ident_b, nl[i], ALU.subtract).then_inc(began, 1)
                for l in range(1, L):
                    for i in range(NS):
                        dve.wait_ge(zmade, done(q, l, i))
                        z = lambda o: zbank(i)[:, :, o, :].rearrange("p m (b s) -> p m b s", s=LEVELS[l])
                        if l < L - 1:
                            for o in range(2):
                                part = half(xv[i][:, :, o, :], l, o)
                                last = nc.vector.tensor_tensor(part, part, z(o), ALU.subtract)
                        else:
                            v, to = xv[i][:, :, 1, :], n_of(q * NS + i)
                            nc.vector.tensor_copy(to[:, :, 0:64], v[:, :, 0:64])
                            nc.vector.tensor_copy(to[64:P, :, 64:P], v[64:P, :, 64:P])
                            last = nc.vector.tensor_scalar(to[0:64, :, 64:P], zbank(i)[0:64, :, 1, :], -1.0, None, ALU.mult)
                        last.then_inc(updated, 1)


def gdn_gates(co, a_log, dt_bias):
    nc = co.nc
    m = A_MISC
    N = NT * HG
    ba = co.at(m + 192, (NT, 2 * HG))
    beta, g, gc, egc, ktl, egl, nbe = (co.at(m + 256 + 32 * i, (N,)) for i in range(7))
    dtb, alog = co.at(m + 480, (HG,)), co.at(m + 484, (HG,))
    t1, t2 = co.at(m + 488, (N,)), co.at(m + 520, (N,))
    v3 = lambda x: x.rearrange("p (t h) -> p t h", h=HG)
    per_head = lambda x: x.rearrange("p (o h) -> p o h", o=1).to_broadcast([P, NT, HG])
    loaded, on_act, on_dve, on_pe, dch = (co.sem(f"gate_{x}") for x in ("loaded", "on_act", "on_dve", "on_pe", "dch"))
    with nc.Block() as block:
        @block.sync
        def _(sp):
            sp.dma_start(dtb, dt_bias.rearrange("(o h) -> o h", o=1).to_broadcast([P, HG])).then_inc(loaded, 16)
            sp.dma_start(alog, a_log.rearrange("(o h) -> o h", o=1).to_broadcast([P, HG])).then_inc(loaded, 16)

        @block.scalar
        def _(act):
            act.wait_ge(loaded, 32)
            nc.scalar.activation(v3(beta), ba[:, :, 0:HG], ACT.Tanh, scale=0.5).then_inc(on_act, 1)
            nc.scalar.activation(alog, alog, ACT.Exp).then_inc(on_act, 1)
            act.wait_ge(on_dve, 1)
            nc.scalar.activation(t2, t1, ACT.Abs).then_inc(on_act, 1)
            act.wait_ge(on_act, 3)
            nc.scalar.activation(t2, t2, ACT.Exp, scale=-1.0).then_inc(on_act, 1)
            act.wait_ge(on_dve, 2)
            nc.scalar.activation(t2, t2, ACT.Ln).then_inc(on_act, 1)
            act.wait_ge(on_dve, 4)
            nc.scalar.activation(egc, gc, ACT.Exp).then_inc(on_act, 1)
            nc.scalar.activation(egl, egl, ACT.Exp).then_inc(on_act, 1)
            nc.scalar.activation(ktl, t1, ACT.Exp).then_inc(on_act, 1)

        @block.vector
        def _(dve):
            link = Chain(dve, dch)
            dve.wait_ge(loaded, 32)
            nc.vector.tensor_tensor(v3(t1), ba[:, :, HG:2 * HG], per_head(dtb), ALU.add).then_inc(on_dve, 1)
            dve.wait_ge(on_act, 4)
            link(nc.vector.tensor_scalar(beta, beta, 0.5, 0.5, ALU.mult, ALU.add))
            nc.vector.tensor_scalar(t2, t2, 1.0, None, ALU.add).then_inc(on_dve, 1)
            dve.wait_ge(on_act, 5)
            dve.wait_ge(on_dve, 2)
            link(nc.vector.scalar_tensor_tensor(g, t1, 0.0, t2, ALU.max, ALU.add))
            nc.vector.scalar_tensor_tensor(v3(g), v3(g), -1.0, per_head(alog), ALU.mult, ALU.mult).then_inc(on_dve, 1)
            dve.wait_ge(on_pe, 2)
            link(nc.vector.tensor_copy(gc, co.ps[:, 0, 0:N]))
            link(nc.vector.tensor_copy(egl, co.ps[:, 1, 0:N]))
            nc.vector.tensor_tensor(t1, egl, gc, ALU.subtract).then_inc(on_dve, 1)
            dve.wait_ge(on_act, 6)
            link(nc.vector.scalar_tensor_tensor(nbe, beta, -1.0, egc, ALU.mult, ALU.mult))

        @block.tensor
        def _(pe):
            pe.wait_ge(on_dve, 3)
            nc.tensor.matmul(co.ps[:, 0, 0:N], co.at(A_CST + C_UT0, (P,)), g, start=True, stop=True).then_inc(on_pe, 1)
            nc.tensor.matmul(co.ps[:, 1, 0:N], co.at(A_CST + C_ONE, (P,)), g, start=True, stop=True).then_inc(on_pe, 1)


def gdn_chunks(co):
    nc = co.nc
    q, k, v = (co.at(A_F[i], (HG, T)) for i in range(3))
    m = A_MISC
    beta, g, gc, egc, ktl = (co.at(m + 256 + 32 * i, (NT * HG,)) for i in range(5))
    n_st, qk_st, kt_st, bv_st = (store_slot(co, i) for i in range(4))
    ident = co.at(A_CST + C_ID, (P,))
    incl = co.at(A_CST + C_UT0, (P,)).rearrange("p (o t) -> p o t", o=1).to_broadcast([P, HG, P])
    strict = co.at(A_CST + C_UT0 + P, (P,)).rearrange("p (o t) -> p o t", o=1).to_broadcast([P, HG, P])
    dt, di, ds, eg, tn = (co.at(A_T + 512 * i, (HG, P)) for i in range(5))
    bank = lambda b: co.ps[:, b, :].rearrange("p (h t) -> p h t", h=HG)
    gbank = lambda c: bank(2 if c % 2 == 0 else 6)
    cumulated, products, clipped, decayed, grown, masked, qkd, n_made, q_scaled, turned, k_out, v_out, dch = (
        co.sem(f"gdn_{x}") for x in ("cumulated", "products", "clipped", "decayed", "grown", "masked", "qkd", "n_made", "q_scaled", "turned", "k_out", "v_out", "dch"))
    with nc.Block() as block:
        @block.tensor
        def _(pe):
            def decays_and_turns(c):
                ct = slice(c * P, (c + 1) * P)
                if c >= 2:
                    pe.wait_ge(clipped, c - 1)
                    pe.wait_ge(grown, c - 1)
                for h in range(HG):
                    s = c * HG + h
                    last = nc.tensor.matmul(gbank(c)[:, h, :], g[:, s:s + 1].to_broadcast([P, P]), co.at(A_CST + C_UT0, (P,)), start=True, stop=True)
                last.then_inc(cumulated, 1)
                if c:
                    pe.wait_ge(k_out, c)
                    pe.wait_ge(v_out, c)
                for h in range(HG):
                    nc.tensor.transpose(bank(4)[:, h, :], k[:, h, ct], ident)
                    last = nc.tensor.transpose(bank(5)[:, h, :], v[:, h, ct], ident)
                last.then_inc(turned, 1)

            decays_and_turns(0)
            for c in range(NT):
                ct = slice(c * P, (c + 1) * P)
                if c:
                    pe.wait_ge(qkd, c)
                    pe.wait_ge(n_made, c)
                for h in range(HG):
                    s = c * HG + h
                    nc.tensor.matmul(bank(1)[:, h, :], k[:, h, ct], q[:, h, ct], start=True, stop=True)
                    nc.tensor.matmul(bank(0)[:, h, :], k[:, h, ct], k[:, h, ct], start=True, stop=True)
                    last = nc.tensor.matmul(bank(3)[:, h, :], beta[:, s:s + 1].to_broadcast([P, P]), ident, start=True, stop=True)
                last.then_inc(products, 1)
                if c + 1 < NT:
                    decays_and_turns(c + 1)

        @block.vector
        def _(dve):
            link = Chain(dve, dch)
            def clip_and_turn(c):
                cs = slice(c * HG, (c + 1) * HG)
                dve.wait_ge(cumulated, c + 1)
                if c:
                    dve.wait_ge(decayed, c)
                for h in range(HG):
                    s = c * HG + h
                    last = nc.vector.tensor_scalar(dt[:, h, :], gbank(c)[:, h, :], gc[:, s:s + 1], 0.0, ALU.subtract, ALU.min)
                last.then_inc(clipped, 1)
                dve.wait_ge(turned, c + 1)
                nc.vector.tensor_tensor(kt_st[:, cs, :], bank(4), bc(ktl[:, cs], P), ALU.mult).then_inc(k_out, 1)
                nc.vector.tensor_tensor(bv_st[:, cs, :], bank(5), bc(beta[:, cs], P), ALU.mult).then_inc(v_out, 1)

            clip_and_turn(0)
            for c in range(NT):
                cs = slice(c * HG, (c + 1) * HG)
                dve.wait_ge(products, c + 1)
                dve.wait_ge(masked, 2 * c + 1)
                nc.vector.tensor_tensor(qk_st[:, cs, :], bank(1), di, ALU.mult).then_inc(qkd, 1)
                dve.wait_ge(masked, 2 * c + 2)
                if c:
                    dve.wait_ge(n_made, c)
                link(nc.vector.tensor_tensor(tn, bank(0), ds, ALU.mult))
                nc.vector.tensor_tensor(n_st[:, cs, :], tn, bank(3), ALU.mult).then_inc(n_made, 1)
                if c + 1 < NT:
                    clip_and_turn(c + 1)

        @block.scalar
        def _(act):
            for c in range(NT):
                act.wait_ge(clipped, c + 1)
                if c:
                    act.wait_ge(masked, 2 * c)
                nc.scalar.activation(dt2(co), dt, ACT.Exp).then_inc(decayed, 1)
                if c:
                    act.wait_ge(q_scaled, c)
                nc.scalar.activation(eg, gbank(c), ACT.Exp).then_inc(grown, 1)

        @block.gpsimd
        def _(pool):
            for c in range(NT):
                ct = slice(c * P, (c + 1) * P)
                pool.wait_ge(decayed, c + 1)
                if c:
                    pool.wait_ge(n_made, c)
                nc.gpsimd.tensor_tensor(di, dt2(co), incl, ALU.mult).then_inc(masked, 1)
                nc.gpsimd.tensor_tensor(ds, dt2(co), strict, ALU.mult).then_inc(masked, 1)
                pool.wait_ge(grown, c + 1)
                pool.wait_ge(products, c + 1)
                nc.gpsimd.tensor_tensor(q[:, :, ct], q[:, :, ct], eg, ALU.mult).then_inc(q_scaled, 1)


def dt2(co):
    return co.at(A_T + 2560, (HG, P))


def store_slot(co, i):
    return co.at(A_BIG, (NT * HG, 4, P))[:, :, i, :]


def gdn_state(co):
    nc = co.nc
    q, k, o = (co.at(A_F[i], (HG, T)) for i in range(3))
    n_st, qk_st, kt_st, bv_st = (store_slot(co, i) for i in range(4))
    egl, nbe = co.at(A_MISC + 256 + 32 * 5, (NT * HG,)), co.at(A_MISC + 256 + 32 * 6, (NT * HG,))
    S, R, VN = (co.at(A_T + 512 * i, (HG, P)) for i in range(3))
    bank = lambda b, pair: co.ps[:, 2 * b + pair, 0:256].rearrange("p (h t) -> p h t", h=2)
    zeroed, ks, resid, vn_made, vn_out, outs, o_out, updated = (
        co.sem(f"gds_{x}") for x in ("zeroed", "ks", "resid", "vn_made", "vn_out", "outs", "o_out", "updated"))
    with nc.Block() as block:
        @block.gpsimd
        def _(pool):
            nc.gpsimd.memset(S, 0.0).then_inc(zeroed, 1)

        @block.tensor
        def _(pe):
            pe.wait_ge(zeroed, 1)
            for c in range(NT):
                ct = slice(c * P, (c + 1) * P)
                for pair in range(2):
                    n = 2 * c + pair
                    if c:
                        pe.wait_ge(updated, 2 * (n - 1))
                    for j in range(2):
                        h = 2 * pair + j
                        last = nc.tensor.matmul(bank(0, pair)[:, j, :], k[:, h, ct], S[:, h, :], start=True, stop=True)
                    last.then_inc(ks, 1)
                for pair in range(2):
                    n = 2 * c + pair
                    pe.wait_ge(resid, 2 * (n + 1))
                    for j in range(2):
                        h = 2 * pair + j
                        last = nc.tensor.matmul(bank(1, pair)[:, j, :], n_st[:, c * HG + h, :], R[:, h, :], start=True, stop=True)
                    last.then_inc(vn_made, 1)
                for pair in range(2):
                    n = 2 * c + pair
                    if c:
                        pe.wait_ge(o_out, n - 1)
                    pe.wait_ge(vn_out, n + 1)
                    for j in range(2):
                        h = 2 * pair + j
                        nc.tensor.matmul(bank(3, pair)[:, j, :], kt_st[:, c * HG + h, :], VN[:, h, :], start=True, stop=True)
                    for j in range(2):
                        h = 2 * pair + j
                        nc.tensor.matmul(bank(2, pair)[:, j, :], S[:, h, :], q[:, h, ct], start=True, stop=False)
                        last = nc.tensor.matmul(bank(2, pair)[:, j, :], VN[:, h, :], qk_st[:, c * HG + h, :], start=False, stop=True)
                    last.then_inc(outs, 1)

        @block.vector
        def _(dve):
            for c in range(NT):
                for pair in range(2):
                    n = 2 * c + pair
                    dve.wait_ge(ks, n + 1)
                    if c:
                        dve.wait_ge(vn_made, n - 1)
                    for j in range(2):
                        h = 2 * pair + j
                        s = c * HG + h
                        nc.vector.scalar_tensor_tensor(R[:, h, :], bank(0, pair)[:, j, :], nbe[:, s:s + 1], bv_st[:, s, :], ALU.mult, ALU.add).then_inc(resid, 1)
                for pair in range(2):
                    n = 2 * c + pair
                    dve.wait_ge(outs, n + 1)
                    for j in range(2):
                        h = 2 * pair + j
                        s = c * HG + h
                        nc.vector.scalar_tensor_tensor(S[:, h, :], S[:, h, :], egl[:, s:s + 1], bank(3, pair)[:, j, :], ALU.mult, ALU.add).then_inc(updated, 1)

        @block.scalar
        def _(act):
            for c in range(NT):
                for pair in range(2):
                    n = 2 * c + pair
                    act.wait_ge(vn_made, n + 1)
                    if c:
                        act.wait_ge(outs, n - 1)
                    nc.scalar.activation(VN[:, 2 * pair:2 * pair + 2, :], bank(1, pair), ACT.Copy).then_inc(vn_out, 1)
                for pair in range(2):
                    act.wait_ge(outs, 2 * c + pair + 1)
                    nc.scalar.activation(o[:, 2 * pair:2 * pair + 2, c * P:(c + 1) * P], bank(2, pair), ACT.Copy).then_inc(o_out, 1)


def swa_prepare(co, rel_bias, sinks):
    nc = co.nc
    qh, kd, vw, bias, bias0 = swa_views(co)
    qb, kb, vbp = co.at(A_F[3], (WB, T)), co.at(A_F[4] + 1088, (T,)), co.at(A_F[4], (T + 64,))
    rb = co.at(A_MISC + 576, (8,), (0, 32))
    sink = co.at(A_MISC + 564, (WB,))
    hot = co.at(A_CST + C_HOT, (192,), (0, 32))
    heads = 2 * WB
    table = co.at(A_T, (192,), (0, heads))
    skew = nc.dram_tensor("bias_by_query", (heads, 64 * 192), F32, kind="Internal").ap()
    moved, tabled, padded, hotted, out1, turned, vout, tabulated, skewed, biased = (co.sem(f"swp_{x}") for x in (
        "moved", "tabled", "padded", "hotted", "out", "turned", "vout", "tabulated", "skewed", "biased"))
    NC = T // 64

    def move(eng, blocks):
        for b in blocks:
            for h in range(2):
                eng.dma_start(qh[:, :, 2 * b + h, :], qb[64 * h:64 * h + 64, b, :].rearrange("p (n t) -> p n t", t=64)).then_inc(moved, 16)

    with nc.Block() as block:
        @block.sync
        def _(sp):
            sp.dma_start(rb, rel_bias).then_inc(tabled, 16)
            for h in range(2):
                sp.dma_start(kd[:, h, 64:], kb[64 * h:64 * h + 64, :]).then_inc(moved, 16)
            sp.wait_ge(tabulated, 1)
            sp.dma_start(skew.rearrange("a (q x) -> a q x", x=192), table.rearrange("a (o x) -> a o x", o=1).to_broadcast([heads, 64, 192])).then_inc(skewed, 16)
            move(sp, (0, 1))
            sp.wait_ge(skewed, 16)
            for h in range(2):
                slid = skew.rearrange("(b h) z -> h b z", h=2)[h][:, 63:63 + 64 * 191].rearrange("b (q x) -> q b x", x=191)
                sp.dma_start(bias[64 * h:64 * h + 64, :, :], slid[:, :, 0:P]).then_inc(biased, 16)
            sp.wait_ge(moved, 16 * (2 * WB + 4))

        @block.gpsimd
        def _(pool):
            nc.gpsimd.memset(kd[:, :, 0:64], 0.0).then_inc(padded, 1)
            nc.gpsimd.memset(vbp[:, 0:64], 0.0).then_inc(padded, 1)

        @block.tensor
        def _(pe):
            pe.wait_ge(tabled, 16)
            last = nc.tensor.matmul(co.ps[0:heads, 0, 0:192], rb, hot, start=True, stop=True)
            last.then_inc(hotted, 1)
            pe.wait_ge(padded, 2)
            for n in range(NC):
                last = nc.tensor.transpose(co.ps[:, 2 + n // 4, (n % 4) * P:(n % 4 + 1) * P], vbp[:, 64 * n:64 * n + P], co.at(A_CST + C_ID, (P,)))
            last.then_inc(turned, 1)

        @block.scalar
        def _(act):
            move(act, (2, 3))
            for h in range(2):
                act.dma_start(sink[64 * h:64 * h + 64, :], sinks.rearrange("(o b h) -> h o b", o=1, h=2)[h].to_broadcast([64, WB])).then_inc(moved, 16)
            act.wait_ge(turned, 1)
            nc.scalar.activation(vw.rearrange("p (b n) d -> p b (n d)", b=4), co.ps[:, 2:6, :], ACT.Copy).then_inc(vout, 1)

        @block.vector
        def _(dve):
            dve.wait_ge(hotted, 1)
            nc.vector.tensor_copy(table, co.ps[0:heads, 0, 0:192]).then_inc(tabulated, 1)
            dve.wait_ge(biased, 32)
            nc.vector.memset(bias0[:, :, 0:64], NEG)
            nc.vector.tensor_copy(bias0[:, :, 64:P], bias[:, :, 64:P]).then_inc(out1, 1)


def swa_views(co):
    qh = co.at(A_BIG, (16, 8, 64), (0, 64))
    kd = co.at(A_BIG + 8192, (2, T + 64), (0, 64))
    vw = co.at(A_BIG + 8192 + 2176, (16, P))
    bias = co.at(A_BIG + 8192 + 2176 + 2048, (WB, P))
    bias0 = co.at(A_BIG + 8192 + 2176 + 2048 + 512, (WB, P))
    return qh, kd, vw, bias, bias0


def swa_attend(co, zb):
    nc = co.nc
    qh, kd, vw, bias, bias0 = swa_views(co)
    sink = co.at(A_MISC + 564, (WB,))
    ident = co.at(A_CST + C_ID, (P,))
    C = 2
    sc = [co.at(A_T + 1024 * i, (C * WB, P)) for i in range(3)]
    pt = [co.at(A_BIG + 13440 + 1024 * i, (C * WB, P)) for i in range(2)]
    mx, es, sm = ([co.at(A_MISC + 600 + 32 * i + 8 * j, (C * WB,)) for i in range(3)] for j in range(3))
    steps = T // 64 // C
    scored, maxed, inverted, shifted, powered, normed, turned, pt_out, mixed, gated, dch = (
        co.sem(f"swa_{x}") for x in ("scored", "maxed", "inverted", "shifted", "powered", "normed", "turned", "pt_out", "mixed", "gated", "dch"))
    banks = lambda b: co.ps[:, b:b + C, :].rearrange("p c (h t) -> p (c h) t", h=WB)
    of_chunks = lambda v: v.rearrange("p (c h) -> p c h", c=C)
    sink_c = sink.rearrange("p (o h) -> p o h", o=1).to_broadcast([P, C, WB])
    with nc.Block() as block:
        @block.tensor
        def _(pe):
            def scores(n):
                if n >= 2:
                    pe.wait_ge(shifted, n - 1)
                for c in range(C):
                    for b in range(WB):
                        m = C * n + c
                        last = nc.tensor.matmul(banks(C * (n % 2))[:, WB * c + b, :], qh[:, m, 2 * b:2 * b + 2, :].rearrange("p h t -> p (h t)"),
                                                kd[:, b // 2, 64 * m:64 * m + P], start=True, stop=True)
                last.then_inc(scored, 1)

            scores(0)
            scores(1)
            for n in range(steps):
                if n + 2 < steps:
                    scores(n + 2)
                pe.wait_ge(normed, n + 1)
                for c in range(C):
                    if n:
                        pe.wait_ge(pt_out, C * (n - 1) + c + 1)
                    for m in range(WB * c, WB * c + WB):
                        last = nc.tensor.transpose(banks(4)[:, m, :], sc[n % 3][:, m, :], ident)
                    last.then_inc(turned, 1)
                if n >= 2:
                    pe.wait_ge(gated, n - 1)
                for c in range(C):
                    pe.wait_ge(pt_out, C * n + c + 1)
                    for g in range(2):
                        for h in range(2):
                            at = 64 * (WB * c + 2 * g)
                            last = nc.tensor.matmul(co.ps[64 * h:64 * h + 64, 6 + n % 2, at:at + P].rearrange("p (b t) -> p b t", b=2),
                                                    vw[:, C * n + c, 64 * g:64 * g + 64], pt[n % 2][:, WB * c + 2 * g:WB * c + 2 * g + 2, 64 * h:64 * h + 64],
                                                    start=True, stop=True)
                last.then_inc(mixed, 1)

        @block.vector
        def _(dve):
            link = Chain(dve, dch)

            def gate(n):
                dve.wait_ge(mixed, n + 1)
                z = zb[:, :, C * 64 * n:C * 64 * (n + 1)].rearrange("p b (c t) -> p b c t", c=C)
                nc.vector.tensor_tensor(z, z, co.ps[:, 6 + n % 2, :].rearrange("p (c b t) -> p b c t", b=WB, c=C), ALU.mult).then_inc(gated, 1)

            def first(n):
                i = n % 3
                dve.wait_ge(scored, n + 1)
                if n >= 3:
                    dve.wait_ge(turned, C * (n - 2))
                if n == 0:
                    link(nc.vector.tensor_tensor(sc[i][:, 0:WB, :], banks(0)[:, 0:WB, :], bias0, ALU.add))
                    link(nc.vector.tensor_tensor(sc[i][:, WB:2 * WB, :], banks(0)[:, WB:2 * WB, :], bias, ALU.add))
                else:
                    link(nc.vector.tensor_tensor(sc[i].rearrange("p (c h) t -> p c (h t)", c=C), co.ps[:, C * (n % 2):C * (n % 2) + C, :],
                                                 bias.rearrange("p (o h) t -> p o (h t)", o=1).to_broadcast([P, C, WB * P]), ALU.add))
                link(nc.vector.tensor_reduce(mx[i], sc[i], AX, ALU.max))
                link(nc.vector.tensor_tensor(of_chunks(mx[i]), of_chunks(mx[i]), sink_c, ALU.max))
                nc.vector.tensor_tensor(of_chunks(es[i]), sink_c, of_chunks(mx[i]), ALU.subtract).then_inc(maxed, 1)

            first(0)
            for n in range(steps):
                i = n % 3
                if n + 1 < steps:
                    first(n + 1)
                dve.wait_ge(powered, 2 * n + 2)
                link(nc.vector.tensor_reduce(sm[i], sc[i], AX, ALU.add))
                link(nc.vector.tensor_tensor(sm[i], sm[i], es[i], ALU.add))
                nc.vector.reciprocal(sm[i], sm[i]).then_inc(inverted, 1)
                if n:
                    gate(n - 1)
            gate(steps - 1)

        @block.gpsimd
        def _(pool):
            def shift(n):
                pool.wait_ge(maxed, n + 1)
                nc.gpsimd.tensor_tensor(sc[n % 3], sc[n % 3], bc(mx[n % 3], P), ALU.subtract).then_inc(shifted, 1)

            shift(0)
            for n in range(steps):
                if n + 1 < steps:
                    shift(n + 1)
                pool.wait_ge(inverted, n + 1)
                nc.gpsimd.tensor_tensor(sc[n % 3], sc[n % 3], bc(sm[n % 3], P), ALU.mult).then_inc(normed, 1)

        @block.scalar
        def _(act):
            def power(n):
                act.wait_ge(shifted, n + 1)
                nc.scalar.activation(es[n % 3], es[n % 3], ACT.Exp).then_inc(powered, 1)
                nc.scalar.activation(sc[n % 3], sc[n % 3], ACT.Exp).then_inc(powered, 1)

            power(0)
            for n in range(steps):
                if n + 1 < steps:
                    power(n + 1)
                if n >= 2:
                    act.wait_ge(mixed, n - 1)
                for c in range(C):
                    act.wait_ge(turned, C * n + c + 1)
                    nc.scalar.activation(pt[n % 2][:, WB * c:WB * c + WB, :], banks(4)[:, WB * c:WB * c + WB, :], ACT.Copy).then_inc(pt_out, 1)


def project_out(co, tag, w, mixed, hi_at, lo_at, res, dst, stored, ahead=None):
    nc = co.nc
    mh, ml = ([co.rounded(f"{tag}_{n}{k}", at[k], (T,)) for k in range(KT)] for n, at in (("mh", hi_at), ("ml", lo_at)))
    wh, wl = co.xt
    wr = [co.at(A_F[4] + 1024 * i, (D,)) for i in range(3)]
    rr = [co.at(A_T + 1024 * i, (D,)) for i in range(3)]
    loaded = ahead or [co.sem(f"{tag}_w{i}") for i in range(3)]
    resin = [co.sem(f"{tag}_r{i}") for i in range(3)]
    high_w, high_m, low_w, low_m, multiplied, added = (co.sem(f"{tag}_{x}") for x in ("high_w", "high_m", "low_w", "low_m", "multiplied", "added"))
    with nc.Block() as block:
        @block.sync
        def _(sp):
            for k in range(KT):
                if k >= 3:
                    sp.wait_ge(low_w, k - 2)
                if k >= 3 or ahead is None:
                    sp.dma_start(wr[k % 3], w[k * P:(k + 1) * P, :]).then_inc(loaded[k % 3], 16)
                if k < 3:
                    sp.dma_start(rr[k], res[k * P:(k + 1) * P, :]).then_inc(resin[k], 16)
            for t in range(NT):
                sp.wait_ge(added, t + 1)
                sp.dma_start(dst[t * P:(t + 1) * P, :], rr[t % 3]).then_inc(stored[t % 3], 16)
                if t + 3 < NT:
                    sp.wait_ge(stored[t % 3], 16 * (t // 3 + 1))
                    sp.dma_start(rr[t % 3], res[(t + 3) * P:(t + 4) * P, :]).then_inc(resin[t % 3], 16)
            for i in range(3):
                sp.wait_ge(stored[i], 16 * len(range(i, NT, 3)))

        @block.scalar
        def _(act):
            for k in range(KT):
                nc.scalar.activation(mh[k], mixed[k], ACT.Copy).then_inc(high_m, 1)
                act.wait_ge(loaded[k % 3], 16 * (k // 3 + 1))
                nc.scalar.activation(wh[:, k, :], wr[k % 3], ACT.Copy).then_inc(high_w, 1)

        @block.gpsimd
        def _(pool):
            for k in range(KT):
                pool.wait_ge(high_m, k + 1)
                nc.gpsimd.tensor_tensor(ml[k], mixed[k], mh[k].bitcast(F32), ALU.subtract).then_inc(low_m, 1)

        @block.tensor
        def _(pe):
            for g in range(NT // 4):
                for k in range(KT):
                    if g == 0:
                        pe.wait_ge(low_m, k + 1)
                        pe.wait_ge(low_w, k + 1)
                    for i in range(4):
                        if g and k == 0:
                            pe.wait_ge(added, i + 1)
                        ts_ = slice((4 * g + i) * P, (4 * g + i + 1) * P)
                        for h in range(2):
                            hs = slice(h * 512, (h + 1) * 512)
                            last = three_passes(nc, co.ps[:, 2 * i + h, :], (mh[k][:, ts_], ml[k][:, ts_]), (wh[:, k, hs], wl[:, k, hs]), k == 0, k == KT - 1)
                        if k == KT - 1:
                            last.then_inc(multiplied, 1)

        @block.vector
        def _(dve):
            for k in range(KT):
                dve.wait_ge(high_w, k + 1)
                nc.vector.tensor_tensor(wl[:, k, :], wr[k % 3], wh[:, k, :].bitcast(F32), ALU.subtract).then_inc(low_w, 1)
            for t in range(NT):
                dve.wait_ge(multiplied, t + 1)
                dve.wait_ge(resin[t % 3], 16 * (t // 3 + 1))
                nc.vector.tensor_tensor(rr[t % 3], rr[t % 3], co.ps[:, 2 * (t % 4):2 * (t % 4) + 2, :].rearrange("p b n -> p (b n)"), ALU.add).then_inc(added, 1)


def start(co, cst):
    nc = co.nc
    co.constants_in, set_ = co.sem("constants"), co.sem("epsilons")
    co.xt = [co.rounded(f"xt_{n}", A_BIG + 8192 * i, (KT, T)) for i, n in enumerate(("hi", "lo"))]
    co.w_parts = [[co.rounded(f"w_{n}{i}", A_F[5] + 3072 + 2048 * m + 1024 * i, (KT, P)) for i in range(2)] for m, n in enumerate(("hi", "lo"))]
    co.small_parts = [co.rounded(f"wsmall_{n}", A_MISC + 704 + 64 * i, (KT, 8)) for i, n in enumerate(("hi", "lo"))]
    co.row_parts = [co.rounded(f"rows_{n}", A_T + 1024 * i, (T,)) for i, n in enumerate(("hi", "lo"))]
    co.hot_r = co.rounded("one_hot", A_MISC + 832, (32,))
    co.pairs_r = co.rounded("pairs", A_T + 3072, (5, P))
    co.eps_at = {RMS_EPS: A_MISC + 568, GN_EPS: A_MISC + 569, 128 * L2_EPS: A_MISC + 570, 64 * RMS_EPS: A_MISC + 571}
    with nc.Block() as block:
        @block.sync
        def _(sp):
            sp.dma_start(co.at(A_CST, (C_ALL,)), cst).then_inc(co.constants_in, 16)

        @block.gpsimd
        def _(pool):
            for eps, col in co.eps_at.items():
                nc.gpsimd.memset(co.at(col, (1,)), eps).then_inc(set_, 1)


def even_layer(co, a, x, dst):
    nc = co.nc
    q, k, v, qb = ([co.at(A_F[i] + T * b, (T,)) for b in range(WB)] for i in range(4))
    za, zb = ([co.at(A_F[i] + T * b, (T,)) for b in range(WB)] for i in (5, 6))
    kb, vb = co.at(A_F[4] + 1088, (T,)), co.at(A_F[4] + 64, (T,))
    blocks = [(EVEN["q"] + P * b, "conv", q[b]) for b in range(WB)]
    blocks += [(EVEN["k"] + P * b, "conv", k[b]) for b in range(WB)]
    blocks += [(EVEN["v"] + P * b, "conv", v[b]) for b in range(WB)]
    zg = nc.dram_tensor("even_gates", (2 * WB, P, T), F32, kind="Internal").ap()
    blocks += [(EVEN["za"] + P * b, "gate", zg[b]) for b in range(WB)]
    blocks += [(EVEN["qb"] + P * b, "plain", qb[b]) for b in range(WB)]
    blocks += [(EVEN["kb"], "plain", kb), (EVEN["vb"], "plain", vb)]
    blocks += [(EVEN["zb"] + P * b, "gate", zg[WB + b]) for b in range(WB)]
    small = (EVEN["beta"], 2 * HG, co.at(A_MISC + 192, (NT, 2 * HG)))
    qn, kn, on = (co.at(A_MISC + 560 + i, (1,)) for i in range(3))
    col = lambda ap: ap.rearrange("(p o) -> p o", o=1)
    gains_in = co.sem("gains_in")
    gains = [(qn[0:64], col(a["swa_q_norm"][0]), gains_in), (qn[64:128], col(a["swa_q_norm"][0]), gains_in),
             (kn[0:64], col(a["swa_k_norm"][0]), gains_in), (kn[64:128], col(a["swa_k_norm"][0]), gains_in),
             (on, col(a["gdn_out_norm"][0]), gains_in)]
    norm_transpose(co, "en", x, a["even_norm"][0], project_ahead(co, "ep", a["even_w_in"][0], blocks, small) + gains, constants_in=co.constants_in)
    project(co, "ep", a["even_w_in"][0], blocks, conv_w=a["gdn_conv_w"][0], small=small, also=(gains_in, 16 * len(gains)))
    norm_blocks(co, "eq", [(x_, 64, qn, None) for x_ in qb] + [(kb, 64, kn, None)] + [(x_, 128, 1.0, None) for x_ in q + k], 0,
                fetch=[(zb[b], zg[WB + b]) for b in range(WB)] + [(za[b], zg[b]) for b in range(WB)])
    swa_prepare(co, a["rel_bias"], a["swa_sinks"][0])
    swa_attend(co, co.at(A_F[6], (WB, T)))
    gdn_gates(co, a["gdn_a_log"][0], a["gdn_dt_bias"][0])
    gdn_chunks(co)
    invert(co, "gi", store_slot(co, 0), [A_F[3] + 1024 * i for i in range(4)], [A_F[4] + 512 * i for i in range(4)], [A_F[4] + 2048 + 512 * i for i in range(4)])
    gdn_state(co)
    w_in = [co.sem(f"eout_w{k}") for k in range(3)]
    norm_blocks(co, "eo", [(x_, 128, on, za_) for x_, za_ in zip(v, za)], 1,
                ahead=[(co.at(A_F[4] + 1024 * k, (D,)), a["even_w_out"][0][k * P:(k + 1) * P, :], sem) for k, sem in enumerate(w_in)])
    project_out(co, "eout", a["even_w_out"][0], v + zb,
                [A_F[0] + 1024 * k for k in range(KT)], [A_F[2] + 1024 * k for k in range(KT)], x, dst, [co.sem(f"eout_stored{i}") for i in range(3)], ahead=w_in)



SG, SP, SCH, SC8 = 32, 64, 16, 8
NPAIR = SG // 2
TWO_PI = 2 * math.pi
TP1 = 6.28125
TP2 = float(np.float32(np.floor((TWO_PI - TP1) * 2 ** 21) / 2 ** 21))
TP3 = TWO_PI - TP1 - TP2
MAGIC = 12582912.0


def complex_product(nc, link, out, x, y, t):
    tt = nc.vector.tensor_tensor
    link(tt(t[0], x[0], y[0], ALU.mult))
    link(tt(t[1], x[1], y[1], ALU.mult))
    link(tt(out[0], t[0], t[1], ALU.subtract))
    link(tt(t[0], x[0], y[1], ALU.mult))
    link(tt(t[1], x[1], y[0], ALU.mult))
    link(tt(out[1], t[0], t[1], ALU.add))


class S5:

    def __init__(self, co):
        B = A_BIG
        self.us = co.at(B, (SG, P))
        self.toep = co.at(B + 4096, (SG, P))
        self.bpt = [co.at(B + 8192 + 2048 * i, (NPAIR, P)) for i in range(2)]
        self.h = [co.at(B + 12288 + 2048 * i, (NPAIR, P)) for i in range(2)]
        self.rot = [co.at(A_F[6] + 2048 * i, (NPAIR, P)) for i in range(2)]
        self.ck = [co.at(A_F[4] + 1024, (NPAIR, 9, SCH)), co.at(A_T, (NPAIR, 9, SCH))]
        self.bp = [co.at(A_F[4] + 1024, (NPAIR, 8, SCH)), co.at(A_T, (NPAIR, 8, SCH))]
        t = A_T + 2304
        self.pw = [co.at(t + 144 * i, (NPAIR, 9)) for i in range(2)]
        self.pwr = [co.at(t + 288 + 128 * i, (NPAIR, 8)) for i in range(2)]
        self.bb = [co.at(t + 544 + 256 * i, (NPAIR, SCH)) for i in range(2)]
        self.cc = [co.at(t + 1056 + 256 * i, (NPAIR, SCH)) for i in range(2)]
        self.braw = [co.at(B + 12288 + 256 * i, (NPAIR, SCH)) for i in range(2)]
        self.cnat = [co.at(B + 12288 + 512 + 512 * i, (4, 2, SP)) for i in range(2)]
        self.small = lambda i: co.at(A_MISC + 192 + 16 * i, (NPAIR,))
        self.kst = co.at(A_F[0], (SG, P), (0, SCH))


def s5_store_u(co, u, u5):
    nc = co.nc
    u2 = co.at(A_BIG + 4096, (WB, SC8, P))
    turned, stored = co.sem("s5u_turned"), co.sem("s5u_stored")
    with nc.Block() as block:
        @block.vector
        def _(dve):
            for b in range(WB):
                nc.vector.tensor_copy(u2[:, b, :, :], u[:, b, :].rearrange("p (c j) -> p j c", j=SC8)).then_inc(turned, 1)

        @block.sync
        def _(sp):
            for b in range(WB):
                sp.wait_ge(turned, b + 1)
                sp.dma_start(u5[b * P:(b + 1) * P, :, :], u2[:, b, :, :]).then_inc(stored, 16)
            sp.wait_ge(stored, 16 * WB)


def s5_tables(co, a, u5, fetch):
    nc = co.nc
    s = S5(co)
    (lre, lim, ls, dt, ar, ai, mag, mag8, sn, cs, lbre, lbim, den, fre, fim, k_, r_, t1, t2, u0, u1, n0, n1) = (s.small(i) for i in range(23))
    loaded, b_in, c_in, on_act, on_dve, on_pe, taken, dch, uin, fetched = (co.sem(f"s5t_{x}") for x in ("loaded", "b_in", "c_in", "on_act", "on_dve", "on_pe", "taken", "dch", "uin", "fetched"))
    q_a = lambda ap: ap.rearrange("(a g) p -> (g p) a", g=2)
    ident = co.at(A_CST + C_ID, (P,))
    co.s5_u_in = uin
    with nc.Block() as block:
        @block.sync
        def _(sp):
            sp.dma_start(lre, a["s5_lambda_re"][0].rearrange("(a g) p -> g p a", g=2)).then_inc(loaded, 16)
            sp.dma_start(lim, a["s5_lambda_im"][0].rearrange("(a g) p -> g p a", g=2)).then_inc(loaded, 16)
            for g in range(2):
                sp.dma_start(ls[64 * g:64 * g + 64, :], a["s5_log_step"][0].rearrange("(o a g) -> g o a", o=1, g=2)[g].to_broadcast([64, NPAIR])).then_inc(loaded, 16)
            for dst, src in fetch:
                sp.dma_start(dst, src).then_inc(fetched, 16)
            sp.wait_ge(on_dve, 6)
            for j in range(SC8):
                sp.dma_start(s.us[16 * j:16 * j + 16, :, :], u5[:, j, :].rearrange("(g c) n -> c g n", c=SCH)).then_inc(co.s5_u_in, 16)
            sp.wait_ge(fetched, 16 * len(fetch))

        @block.scalar
        def _(act):
            for i, name in enumerate(("re", "im")):
                act.dma_start(s.braw[i], a[f"s5_b_{name}"][0].rearrange("(a g) p c -> (g p) a c", g=2)).then_inc(b_in, 16)
            for i, name in enumerate(("re", "im")):
                for d in range(2):
                    act.dma_start(s.cnat[i][:, :, d, :], a[f"s5_c_{name}"][0].rearrange("g c p -> (g c) p").rearrange("(n q) p -> q n p", q=P)).then_inc(c_in, 16)
            act.wait_ge(loaded, 16 * 4)
            nc.scalar.activation(dt, ls, ACT.Exp).then_inc(on_act, 1)
            act.wait_ge(on_dve, 1)
            nc.scalar.activation(mag, ar, ACT.Exp).then_inc(on_act, 1)
            nc.scalar.activation(mag8, ar, ACT.Exp, scale=8.0).then_inc(on_act, 1)
            act.wait_ge(on_dve, 2)
            nc.scalar.activation(sn, r_, ACT.Sin).then_inc(on_act, 1)
            nc.scalar.activation(cs, t1, ACT.Sin).then_inc(on_act, 1)
            for i in range(2):
                for n in range(4):
                    act.wait_ge(on_pe, 2 + 4 * i + n)
                    nc.scalar.activation(s.bpt[i][:, 4 * n:4 * n + 4, :], co.ps[:, 4 + n, :].rearrange("p (a t) -> p a t", a=4), ACT.Copy).then_inc(taken, 1)

        @block.tensor
        def _(pe):
            pe.wait_ge(c_in, 16 * 4)
            for i in range(2):
                for n in range(4):
                    last = nc.tensor.transpose(co.ps[:, i, n * P:(n + 1) * P], s.cnat[i][:, n, :, :].rearrange("p d q -> p (d q)"), ident)
            last.then_inc(on_pe, 1)
            pe.wait_ge(on_dve, 4)
            for i in range(2):
                for n in range(4):
                    if i:
                        pe.wait_ge(taken, n + 1)
                    for m in range(4):
                        last = nc.tensor.transpose(co.ps[:, 4 + n, m * P:(m + 1) * P], s.bp[i][:, 4 * n + m, :, :].rearrange("p j c -> p (j c)"), ident)
                    last.then_inc(on_pe, 1)

        @block.vector
        def _(dve):
            link = Chain(dve, dch)
            tt, ts, stt = nc.vector.tensor_tensor, nc.vector.tensor_scalar, nc.vector.scalar_tensor_tensor
            dve.wait_ge(on_act, 1)
            link(tt(ai, lim, dt, ALU.mult))
            tt(ar, lre, dt, ALU.mult).then_inc(on_dve, 1)
            link(ts(k_, ai, 1.0 / TWO_PI, MAGIC, ALU.mult, ALU.add))
            link(ts(k_, k_, MAGIC, None, ALU.subtract))
            link(stt(r_, k_, -TP1, ai, ALU.mult, ALU.add))
            link(stt(r_, k_, -TP2, r_, ALU.mult, ALU.add))
            link(stt(r_, k_, -TP3, r_, ALU.mult, ALU.add))
            link(ts(r_, r_, 3.1415925, -3.1415925, ALU.min, ALU.max))
            link(ts(t1, r_, -1.0, None, ALU.mult))
            link(tt(t1, t1, r_, ALU.max))
            ts(t1, t1, -1.0, math.pi / 2, ALU.mult, ALU.add).then_inc(on_dve, 1)
            dve.wait_ge(on_pe, 1)
            for i in range(2):
                for g in range(2):
                    link(nc.vector.tensor_copy(s.cc[i][64 * g:64 * g + 64, :, :],
                                               co.ps[64 * g:64 * g + 64, i, :].rearrange("p (a g c) -> p a g c", g=2, c=SCH)[:, :, g, :]))
            dve.wait_ge(on_act, 5)
            link(tt(lbre, mag, cs, ALU.mult))
            link(tt(lbim, mag, sn, ALU.mult))
            link(tt(den, lre, lre, ALU.mult))
            link(tt(t1, lim, lim, ALU.mult))
            link(tt(den, den, t1, ALU.add))
            link(nc.vector.reciprocal(den, den))
            link(ts(n0, lbre, 1.0, None, ALU.subtract))
            link(tt(t1, n0, lre, ALU.mult))
            link(tt(t2, lbim, lim, ALU.mult))
            link(tt(fre, t1, t2, ALU.add))
            link(tt(fre, fre, den, ALU.mult))
            link(tt(t1, lbim, lre, ALU.mult))
            link(tt(t2, n0, lim, ALU.mult))
            link(tt(fim, t1, t2, ALU.subtract))
            link(tt(fim, fim, den, ALU.mult))
            tmp = [co.at(A_BIG + 4096 + 2304 * 0, (NPAIR, SCH)), co.at(A_BIG + 4096 + 256, (NPAIR, SCH))]
            dve.wait_ge(b_in, 32)
            complex_product(nc, link, s.bb, [bc(fre, SCH), bc(fim, SCH)], s.braw, tmp)
            for i, v in enumerate((1.0, 0.0)):
                link(nc.vector.memset(s.pw[i][:, :, 0:1], v))
                link(nc.vector.tensor_copy(s.pw[i][:, :, 1], (lbre, lbim)[i]))
            for m in (1, 2, 4):
                tm = [co.at(A_BIG + 4096 + 64 * i, (NPAIR, m)) for i in range(2)]
                complex_product(nc, link, [x[:, :, m + 1:2 * m + 1] for x in s.pw], [x[:, :, 1:m + 1] for x in s.pw],
                                [x[:, :, m:m + 1].to_broadcast([P, NPAIR, m]) for x in s.pw], tm)
            for i in range(2):
                for j in range(8):
                    link(nc.vector.tensor_copy(s.pwr[i][:, :, j], s.pw[i][:, :, 7 - j]))
            nc.vector.memset(t1, 0.0).then_inc(on_dve, 1)
            wide = lambda x, n: x.rearrange("p a (o c) -> p a o c", o=1).to_broadcast([P, NPAIR, n, SCH])
            deep = lambda x, n: x.rearrange("p a (k o) -> p a k o", o=1).to_broadcast([P, NPAIR, n, SCH])
            tb = [co.at(A_BIG + 4096 + 2048 * i, (NPAIR, 8, SCH)) for i in range(2)]
            complex_product(nc, link, s.bp, [deep(x, 8) for x in s.pwr], [wide(x, 8) for x in s.bb], tb)
            nc.vector.memset(t1, 0.0).then_inc(on_dve, 1)
            dve.wait_ge(on_pe, 9)
            dve.wait_ge(on_dve, 4)
            tc_ = [co.at(A_BIG + 2304 * i, (NPAIR, 9, SCH)) for i in range(2)]
            complex_product(nc, link, s.ck, [deep(x, 9) for x in s.pw], [wide(x, 9) for x in s.cc], tc_)
            ts(s.ck[1], s.ck[1], -1.0, None, ALU.mult).then_inc(on_dve, 1)
            dve.wait_ge(on_dve, 5)
            nc.vector.memset(t1, 0.0).then_inc(on_dve, 1)
            link(nc.vector.tensor_copy(u0, cs))
            link(nc.vector.tensor_copy(u1, sn))
            for _i in range(3):
                complex_product(nc, link, [n0, n1], [u0, u1], [u0, u1], [t1, t2])
                link(nc.vector.tensor_copy(u0, n0))
                link(nc.vector.tensor_copy(u1, n1))


def s5_toeplitz(co):
    nc = co.nc
    s = S5(co)
    made, taken, zeroed, placed, dch = (co.sem(f"s5k_{x}") for x in ("made", "taken", "zeroed", "placed", "dch"))
    u0, u1, n0, n1, t1, t2 = (s.small(i) for i in (19, 20, 21, 22, 17, 18))
    co.s5_placed = placed
    with nc.Block() as block:
        @block.vector
        def _(dve):
            link = Chain(dve, dch)
            for i, v in enumerate((1.0, 0.0)):
                link(nc.vector.memset(s.rot[i][:, :, 0:1], v))
            w, w2 = (u0, u1), (n0, n1)
            for m in (1, 2, 4, 8, 16, 32, 64):
                tm = [co.at(A_BIG + 12288 + 2048 * i, (NPAIR, m)) for i in range(2)]
                complex_product(nc, link, [x[:, :, m:2 * m] for x in s.rot], [x[:, :, 0:m] for x in s.rot], [bc(x, m) for x in w], tm)
                complex_product(nc, link, w2, w, w, [t1, t2])
                w, w2 = w2, w

        @block.gpsimd
        def _(pool):
            nc.gpsimd.memset(s.toep, 0.0).then_inc(zeroed, 1)

        @block.tensor
        def _(pe):
            for n in range(4):
                for m in range(4):
                    for g in range(2):
                        a, rows = 4 * n + m, slice(64 * g, 64 * g + 64)
                        for i in range(2):
                            last = nc.tensor.matmul(co.ps[0:SCH, 2 * n + g, m * P:(m + 1) * P], s.bb[i][rows, a, :],
                                                    s.ck[i][rows, a, 0:8, :], start=i == 0, stop=i == 1)
                last.then_inc(made, 1)

        @block.scalar
        def _(act):
            kst = s.kst.rearrange("p (n m g) t -> p n m g t", n=4, g=2)
            for n in range(4):
                act.wait_ge(made, n + 1)
                for g in range(2):
                    nc.scalar.activation(kst[:, n, :, g, :], co.ps[0:SCH, 2 * n + g, :].rearrange("p (m t) -> p m t", m=4), ACT.Copy).then_inc(taken, 1)

        @block.sync
        def _(sp):
            sp.wait_ge(zeroed, 1)
            sp.wait_ge(taken, 8)
            for j in range(SC8):
                sp.dma_start(s.toep[16 * j:16 * j + 16, :, 16 * j:P], s.kst[:, :, 0:P - 16 * j]).then_inc(placed, 16)


def s5_scan(co, y5):
    nc = co.nc
    s = S5(co)
    mag8 = s.small(7)
    decay_all = co.at(A_F[0], (4, 4, P))
    tmp = [co.at(A_F[0] + 2048 + 512 * i, (4 * P,)) for i in range(2)]
    fed, ready, made, taken, stored, dch = (co.sem(f"s5s_{x}") for x in ("fed", "ready", "made", "taken", "stored", "dch"))
    with nc.Block() as block:
        @block.tensor
        def _(pe):
            pe.wait_ge(co.s5_u_in, 16 * SC8)
            for n in range(4):
                for i in range(2):
                    for m in range(4):
                        for g in range(2):
                            a = 4 * n + m
                            last = nc.tensor.matmul(co.ps[64 * g:64 * g + 64, 4 * i + n, m * P:(m + 1) * P],
                                                    s.bpt[i][:, a, 64 * g:64 * g + 64], s.us[:, 2 * a + g, :], start=True, stop=True)
                last.then_inc(fed, 1)
            pe.wait_ge(co.s5_placed, 16 * SC8)
            for n in range(4):
                pe.wait_ge(ready, n + 1)
                for g in range(2):
                    for m in range(4):
                        a, rows = 4 * n + m, slice(64 * g, 64 * g + 64)
                        out = co.ps[:, 4 * g + n, m * P:(m + 1) * P]
                        nc.tensor.matmul(out, s.toep[:, 2 * a + g, :], s.us[:, 2 * a + g, :], start=True, stop=False)
                        for i in range(2):
                            last = nc.tensor.matmul(out[:, 1:P], s.ck[i][rows, a, 1:9, :].rearrange("p k c -> p (k c)"),
                                                    s.h[i][rows, a, 0:P - 1], start=False, stop=i == 1)
                    last.then_inc(made, 1)

        @block.vector
        def _(dve):
            link = Chain(dve, dch)
            tt = nc.vector.tensor_tensor
            dve.wait_ge(co.s5_placed, 16 * SC8)
            link(nc.vector.tensor_copy(decay_all, mag8.rearrange("p (n m o) -> p n m o", n=4, o=1).to_broadcast([P, 4, 4, P])))
            link(nc.vector.memset(decay_all[:, :, :, 0:1], 0.0))
            t0, t1 = tmp
            for n in range(4):
                flat = lambda x: x[:, 4 * n:4 * n + 4, :].rearrange("p a c -> p (a c)")
                er, ei, hr, hi = flat(s.rot[0]), flat(s.rot[1]), flat(s.h[0]), flat(s.h[1])
                re, im = co.ps[:, n, :], co.ps[:, 4 + n, :]
                d = decay_all[:, n, :, :].rearrange("p m c -> p (m c)")
                dve.wait_ge(fed, n + 1)
                if n:
                    dve.wait_ge(ready, n)
                tt(hr, re, er, ALU.mult), tt(t0, im, ei, ALU.mult)
                tt(hi, im, er, ALU.mult), link(tt(t1, re, ei, ALU.mult))
                tt(hr, hr, t0, ALU.add), link(tt(hi, hi, t1, ALU.subtract))
                nc.vector.tensor_tensor_scan(hr, d, hr, 0.0, ALU.mult, ALU.add)
                link(nc.vector.tensor_tensor_scan(hi, d, hi, 0.0, ALU.mult, ALU.add))
                tt(t0, hr, ei, ALU.mult), link(tt(t1, hi, ei, ALU.mult))
                tt(hr, hr, er, ALU.mult), link(tt(hi, hi, er, ALU.mult))
                tt(hr, hr, t1, ALU.subtract), tt(hi, hi, t0, ALU.add).then_inc(ready, 1)

        @block.scalar
        def _(act):
            us = s.us.rearrange("p (n m g) t -> p n m g t", n=4, g=2)
            for n in range(4):
                for g in range(2):
                    act.wait_ge(made, 2 * n + g + 1)
                    nc.scalar.activation(us[:, n, :, g, :], co.ps[:, 4 * g + n, :].rearrange("p (m t) -> p m t", m=4), ACT.Copy).then_inc(taken, 1)

        @block.sync
        def _(sp):
            sp.wait_ge(taken, 8)
            for j in range(SC8):
                sp.dma_start(y5[:, j, :].rearrange("(g c) n -> c g n", c=SCH), s.us[16 * j:16 * j + 16, :, :]).then_inc(stored, 16)
            sp.wait_ge(stored, 16 * SC8)


def s5_glu(co, d_skip, w_glu, u5, y5, zc):
    nc = co.nc
    y = co.at(A_BIG, (WB, T))
    u = co.at(A_BIG + 4096, (WB, T))
    wg = co.at(A_BIG + 8192, (WB, 2 * W))
    yc = co.at(A_BIG + 12288, (WB, T))
    tb = co.at(A_F[0], (2, T))
    dcol = co.at(A_MISC + 632, (WB,))
    loaded, cubed, tanhed, gelu, made_a, tanh_b, gated, dch = (
        co.sem(f"glu_{x}") for x in ("loaded", "cubed", "tanhed", "gelu", "made", "tanh_b", "gated", "dch"))
    block_loaded, wloaded = ([co.sem(f"glu_{n}{b}") for b in range(WB)] for n in ("loaded", "wloaded"))
    with nc.Block() as block:
        @block.sync
        def _(sp):
            sp.dma_start(dcol, d_skip.rearrange("(b p) -> p b", p=P)).then_inc(loaded, 16)
            for b in range(WB):
                sp.dma_start(y[:, b, :], y5[b * P:(b + 1) * P, :, :].rearrange("p j c -> p (j c)")).then_inc(block_loaded[b], 16)
                sp.dma_start(u[:, b, :], u5[b * P:(b + 1) * P, :, :].rearrange("p j c -> p (j c)")).then_inc(block_loaded[b], 16)
            for k in range(WB):
                sp.dma_start(wg[:, k, :], w_glu[k * P:(k + 1) * P, :]).then_inc(wloaded[k], 16)

        @block.vector
        def _(dve):
            link = Chain(dve, dch)
            dve.wait_ge(loaded, 16)

            def gelu_of(b):
                dve.wait_ge(tanhed, b + 1)
                nc.vector.scalar_tensor_tensor(yc[:, b, :].rearrange("p (c j) -> p j c", j=SC8), u[:, b, :].rearrange("p (j c) -> p j c", j=SC8), 1.0,
                                               y[:, b, :].rearrange("p (j c) -> p j c", j=SC8), ALU.add, ALU.mult).then_inc(gelu, 1)

            for b in range(WB):
                dve.wait_ge(block_loaded[b], 32)
                yb, ub = y[:, b, :], u[:, b, :]
                link(nc.vector.scalar_tensor_tensor(yb, ub, dcol[:, b:b + 1], yb, ALU.mult, ALU.add))
                link(nc.vector.tensor_tensor(ub, yb, yb, ALU.mult))
                link(nc.vector.tensor_scalar(ub, ub, 0.044715, 1.0, ALU.mult, ALU.add))
                nc.vector.tensor_tensor(ub, ub, yb, ALU.mult).then_inc(cubed, 1)
                if b:
                    gelu_of(b - 1)
            gelu_of(WB - 1)
            for b in range(WB):
                dve.wait_ge(tanh_b, b + 1)
                link(nc.vector.scalar_tensor_tensor(tb[:, b % 2, :], tb[:, b % 2, :], 1.0, zc[b], ALU.add, ALU.mult))
                a_ = co.ps[:, 4 * (b % 2):4 * (b % 2) + 2, :].rearrange("p h t -> p (h t)")
                nc.vector.scalar_tensor_tensor(zc[b], a_, 0.25, tb[:, b % 2, :], ALU.mult, ALU.mult).then_inc(gated, 1)

        @block.scalar
        def _(act):
            for b in range(WB):
                act.wait_ge(cubed, b + 1)
                nc.scalar.activation(u[:, b, :], u[:, b, :], ACT.Tanh, scale=math.sqrt(2 / math.pi)).then_inc(tanhed, 1)
            for b in range(WB):
                act.wait_ge(made_a, b + 1)
                if b >= 2:
                    act.wait_ge(gated, b - 1)
                nc.scalar.activation(tb[:, b % 2, :], co.ps[:, 4 * (b % 2) + 2:4 * (b % 2) + 4, :].rearrange("p h t -> p (h t)"), ACT.Tanh, scale=0.25).then_inc(tanh_b, 1)

        @block.tensor
        def _(pe):
            for q in range(WB // 2):
                for k in range(WB):
                    pe.wait_ge(wloaded[k], 16)
                    pe.wait_ge(gelu, k + 1)
                    for b in (2 * q, 2 * q + 1):
                        if q and k == 0:
                            pe.wait_ge(gated, b - 1)
                        for part in range(2):
                            for h in range(2):
                                last = nc.tensor.matmul(co.ps[:, 4 * (b % 2) + 2 * part + h, :], wg[:, k, part * W + b * P:part * W + (b + 1) * P],
                                                        yc[:, k, h * 512:(h + 1) * 512], start=k == 0, stop=k == WB - 1)
                        if k == WB - 1:
                            last.then_inc(made_a, 1)


LOGW = -math.exp(-0.5)


class R7:
    def __init__(self, co, half):
        m = A_MISC
        self.b0 = 2 * half
        self.r, self.k, self.v = (co.at(A_F[i] + 2048 * half, (2, T)) for i in (1, 2, 3))
        self.kk, self.b = co.at(A_F[0], (2, T)), co.at(A_F[0] + 2048, (2, T))
        self.zd = co.at(A_F[6], (2, T))
        self.bon = co.at(A_F[4] + 1024, (2, T))
        self.wa = co.at(A_F[4], (T,))
        self.cols = {n: co.at(m + 600 + 4 * i, (WB,)) for i, n in enumerate(("w0", "a0", "k_k", "k_a", "omka", "r_k", "ln_w", "ln_b"))}
        self.scale = co.at(m + 640, (2, NT))
        self.lw = [co.at(A_BIG + 2048 + 1024 * i, (T,)) for i in range(2)]
        self.gg = [co.at(A_BIG + 4096 + 1024 * i, (T,)) for i in range(2)]
        self.t = [co.at(A_BIG + 6144 + 1024 * i, (T,)) for i in range(8)]
        self.w2a2 = co.at(A_BIG + 14336, (W,))
        self.rk1 = [co.at(A_BIG + 15360 + P * i, (P,)) for i in range(2)]


def r7_start(co, a):
    nc = co.nc
    x = R7(co, 0)
    rates_in = co.sem("r7_rates_in")
    loaded, done, hd = co.sem("r7_loaded"), co.sem("r7_tanh"), co.sem("r7_halved")
    col = lambda ap: ap.rearrange("(b p) -> p b", p=P)
    with nc.Block() as block:
        @block.sync
        def _(sp):
            for n, src in (("w0", col(a["rwkv_w0"][0])), ("a0", col(a["rwkv_a0"][0])), ("k_k", col(a["rwkv_k_k"][0])), ("k_a", col(a["rwkv_k_a"][0])),
                           ("r_k", a["rwkv_r_k"][0].rearrange("(b h) d -> (h d) b", h=2)), ("ln_w", col(a["rwkv_ln_w"][0])), ("ln_b", col(a["rwkv_ln_b"][0]))):
                sp.dma_start(x.cols[n], src).then_inc(loaded, 16)
            sp.wait_ge(loaded, 16 * 7)
            sp.wait_ge(rates_in, 32)

        @block.scalar
        def _(act):
            act.dma_start(x.w2a2[0:64, :], a["rwkv_w2"][0]).then_inc(rates_in, 16)
            act.dma_start(x.w2a2[64:128, :], a["rwkv_a2"][0]).then_inc(rates_in, 16)
            nc.scalar.activation(x.wa[0:64, :], x.wa[0:64, :], ACT.Tanh).then_inc(done, 1)

        @block.vector
        def _(dve):
            dve.wait_ge(loaded, 16 * 7)
            nc.vector.tensor_scalar(x.cols["w0"], x.cols["w0"], 0.5, None, ALU.mult).then_inc(hd, 1)
            nc.vector.tensor_scalar(x.cols["a0"], x.cols["a0"], 0.5, None, ALU.mult).then_inc(hd, 1)
            nc.vector.tensor_scalar(x.cols["omka"], x.cols["k_a"], -1.0, 1.0, ALU.mult, ALU.add).then_inc(hd, 1)


def r7_features(co, half):
    nc = co.nc
    x = R7(co, half)
    c_ = lambda n, j: x.cols[n][:, x.b0 + j:x.b0 + j + 1]
    made, tanhed, formed, rk, bonus, bout, dch = (co.sem(f"r7f{half}_{y}") for y in ("made", "tanhed", "formed", "rk", "bonus", "bout", "dch"))
    with nc.Block() as block:
        @block.tensor
        def _(pe):
            for j in range(2):
                cols = slice((x.b0 + j) * P, (x.b0 + j + 1) * P)
                for h in range(2):
                    for part in range(2):
                        rows = slice(64 * part, 64 * part + 64)
                        last = nc.tensor.matmul(co.ps[:, 4 * j + 2 * part + h, :], x.w2a2[rows, cols], x.wa[rows, h * 512:(h + 1) * 512], start=True, stop=True)
                last.then_inc(made, 1)
            for j in range(2):
                pe.wait_ge(formed, j + 1)
                for h in range(2):
                    last = nc.tensor.matmul(co.ps[:, 4 * j + h, :], x.rk1[j], x.t[2 + j][:, h * 512:(h + 1) * 512], start=True, stop=True)
                last.then_inc(bonus, 1)

        @block.scalar
        def _(act):
            for j in range(2):
                act.wait_ge(made, j + 1)
                for part, (out, bias) in enumerate(((x.lw[j], "w0"), (x.b[:, j, :], "a0"))):
                    nc.scalar.activation(out, co.ps[:, 4 * j + 2 * part:4 * j + 2 * part + 2, :].rearrange("p h t -> p (h t)"), ACT.Tanh, bias=c_(bias, j), scale=0.5).then_inc(tanhed, 1)

        @block.vector
        def _(dve):
            link = Chain(dve, dch)
            for j in range(2):
                link(nc.vector.tensor_scalar(x.rk1[j], co.at(A_CST + C_ONE2, (P,)), c_("r_k", j), None, ALU.mult))
            for j in range(2):
                link(nc.vector.tensor_scalar(x.kk[:, j, :], x.k[:, j, :], c_("k_k", j), None, ALU.mult))
                dve.wait_ge(tanhed, 2 * j + 2)
                link(nc.vector.tensor_scalar(x.lw[j], x.lw[j], LOGW / 2, LOGW / 2, ALU.mult, ALU.add))
                link(nc.vector.tensor_scalar(x.b[:, j, :], x.b[:, j, :], 0.5, 0.5, ALU.mult, ALU.add))
                link(nc.vector.tensor_scalar(x.t[j], x.b[:, j, :], c_("k_a", j), c_("omka", j), ALU.mult, ALU.add))
                link(nc.vector.tensor_tensor(x.k[:, j, :], x.k[:, j, :], x.t[j], ALU.mult))
                nc.vector.tensor_tensor(x.t[2 + j], x.r[:, j, :], x.k[:, j, :], ALU.mult).then_inc(formed, 1)
            for j in range(2):
                dve.wait_ge(bonus, j + 1)
                nc.vector.tensor_tensor(x.bon[:, j, :], co.ps[:, 4 * j:4 * j + 2, :].rearrange("p h t -> p (h t)"), x.v[:, j, :], ALU.mult).then_inc(bout, 1)


def r7_decay(co, half):
    nc = co.nc
    x = R7(co, half)
    summed, centred, shifted, expd, rated, used, sc, scd, dch = (co.sem(f"r7d{half}_{y}") for y in ("summed", "centred", "shifted", "expd", "rated", "used", "sc", "scd", "dch"))
    startm = co.at(A_CST + C_START, (T,))
    v3 = lambda ap: ap.rearrange("p (c t) -> p c t", t=P)
    e = [[x.t[4 * j + i] for i in range(3)] for j in range(2)]
    with nc.Block() as block:
        @block.vector
        def _(dve):
            link = Chain(dve, dch)
            tt = nc.vector.tensor_tensor
            for j in range(2):
                g = v3(x.gg[j])
                link(nc.vector.tensor_tensor_scan(x.gg[j], startm, x.lw[j], 0.0, ALU.mult, ALU.add))
                mid, end = g[:, :, P // 2 - 1], g[:, :, P - 1]
                link(tt(x.scale[:, j, :], end, mid, ALU.subtract))
                tt(x.scale[:, j, 0:NT - 1], x.scale[:, j, 0:NT - 1], g[:, 1:NT, P // 2 - 1], ALU.add).then_inc(sc, 1)
                tt(v3(x.t[4 * j + 3]), g, g[:, :, P // 2 - 1:P // 2].to_broadcast([P, NT, P]), ALU.subtract).then_inc(centred, 1)
            for j in range(2):
                dve.wait_ge(expd, 3 * j + 3)
                tt(x.r[:, j, :], x.r[:, j, :], e[j][0], ALU.mult).then_inc(used, 1)
                tt(x.k[:, j, :], x.k[:, j, :], e[j][1], ALU.mult).then_inc(used, 1)
                dve.wait_ge(rated, j + 1)
                tt(x.b[:, j, :], x.b[:, j, :], e[j][1], ALU.mult).then_inc(used, 1)
                tt(x.kk[:, j, :], x.kk[:, j, :], e[j][2], ALU.mult).then_inc(used, 1)

        @block.gpsimd
        def _(pool):
            for j in range(2):
                nc.gpsimd.tensor_tensor(x.b[:, j, :], x.b[:, j, :], x.kk[:, j, :], ALU.mult).then_inc(rated, 1)
                pool.wait_ge(centred, j + 1)
                nc.gpsimd.tensor_tensor(e[j][2], x.t[4 * j + 3], x.lw[j], ALU.subtract).then_inc(shifted, 1)

        @block.scalar
        def _(act):
            for j in range(2):
                act.wait_ge(centred, j + 1)
                nc.scalar.activation(e[j][0], x.t[4 * j + 3], ACT.Exp).then_inc(expd, 1)
                nc.scalar.activation(e[j][1], x.t[4 * j + 3], ACT.Exp, scale=-1.0).then_inc(expd, 1)
                act.wait_ge(shifted, j + 1)
                nc.scalar.activation(e[j][2], e[j][2], ACT.Exp).then_inc(expd, 1)
                nc.scalar.activation(x.scale[:, j, :], x.scale[:, j, :], ACT.Exp).then_inc(scd, 1)


def r7_pairs(co, half):
    nc = co.nc
    x = R7(co, half)
    store = co.at(A_BIG, (NT * 4, 4, P))
    mask = co.at(A_CST + C_M4, (4, P)).bitcast(I32)
    zeroed, made, kept = (co.sem(f"r7p{half}_{y}") for y in ("zeroed", "made", "kept"))
    with nc.Block() as block:
        @block.gpsimd
        def _(pool):
            for i in range(4):
                nc.gpsimd.memset(store[:, 8 * i + 4:8 * i + 8, :, :], 0.0).then_inc(zeroed, 1)

        @block.tensor
        def _(pe):
            for c in range(NT):
                ct = slice(c * P, (c + 1) * P)
                for h in range(4):
                    n = 4 * c + h
                    j, rows = h // 2, slice(64 * (h % 2), 64 * (h % 2) + 64)
                    if n >= 8:
                        pe.wait_ge(kept, n - 7)
                    for m, key in enumerate((x.b, x.k)):
                        for o, query in enumerate((x.r, x.kk)):
                            last = nc.tensor.matmul(co.ps[:, n % 8, (2 * m + o) * P:(2 * m + o + 1) * P], key[rows, j, ct], query[rows, j, ct], start=True, stop=True)
                    last.then_inc(made, 1)

        @block.vector
        def _(dve):
            link = Chain(dve, co.sem(f"r7p{half}_cleared"))
            for i in range(4):
                link(nc.vector.memset(store[:, 8 * i:8 * i + 4, :, :], 0.0))
            dve.wait_ge(zeroed, 4)
            for n in range(4 * NT):
                dve.wait_ge(made, n + 1)
                nc.vector.copy_predicated(store[:, n, :, :], mask, co.ps[:, n % 8, :].rearrange("p (s t) -> p s t", s=4)).then_inc(kept, 1)


def r7_state(co, half, gates):
    nc = co.nc
    x = R7(co, half)
    store = co.at(A_BIG, (NT * 4, 4, P))
    ident = co.at(A_CST + C_ID, (P,))
    tok = [[co.at(A_T + 384 * (2 * j + i), (3, P)) for i in range(2)] for j in range(2)]
    S = [co.at(A_T + 1536 + P * j, (P,)) for j in range(2)]
    R = [co.at(A_T + 1792 + P * j, (P,)) for j in range(2)]
    SA = [co.at(A_T + 2048 + P * j, (P,)) for j in range(2)]
    zeroed, turned, tok_out, rs, r_out, solved, sa_out, ys, y_out, grown, added, updated = (
        co.sem(f"r7s{half}_{y}") for y in ("zeroed", "turned", "tok_out", "rs", "r_out", "solved", "sa_out", "ys", "y_out", "grown", "added", "updated"))
    bank = lambda b, j: co.ps[:, 2 * b + j, 0:P]
    gates_in = co.sem(f"r7s{half}_gates_in")
    with nc.Block() as block:
        @block.sync
        def _(sp):
            for j in range(2):
                sp.dma_start(x.zd[:, j, :], gates[WB + x.b0 + j]).then_inc(gates_in, 16)
            sp.wait_ge(gates_in, 32)

        @block.gpsimd
        def _(pool):
            for j in range(2):
                nc.gpsimd.memset(S[j], 0.0).then_inc(zeroed, 1)

        @block.tensor
        def _(pe):
            pe.wait_ge(zeroed, 2)

            def turn(c):
                for j in range(2):
                    if c:
                        pe.wait_ge(tok_out, 2 * (c - 1) + j + 1)
                    for i, src in enumerate((x.b, x.k, x.v)):
                        last = nc.tensor.transpose(co.ps[:, j, i * P:(i + 1) * P], src[:, j, c * P:(c + 1) * P], ident)
                    last.then_inc(turned, 1)

            turn(0)
            for c in range(NT):
                ct = slice(c * P, (c + 1) * P)
                for j in range(2):
                    n = 2 * c + j
                    if c:
                        pe.wait_ge(updated, 2 * (n - 1))
                    pe.wait_ge(tok_out, n + 1)
                    nc.tensor.matmul(bank(1, j), x.kk[:, j, ct], S[j], start=True, stop=False)
                    for h in range(2):
                        last = nc.tensor.matmul(bank(1, j)[:, 64 * h:64 * h + 64], store[:, 4 * c + 2 * j + h, 3, :],
                                                tok[j][c % 2][:, 2, 64 * h:64 * h + 64], start=False, stop=h == 1)
                    last.then_inc(rs, 1)
                if c + 1 < NT:
                    turn(c + 1)
                for j in range(2):
                    n = 2 * c + j
                    pe.wait_ge(r_out, n + 1)
                    for h in range(2):
                        last = nc.tensor.matmul(bank(2, j)[:, 64 * h:64 * h + 64], store[:, 4 * c + 2 * j + h, 1, :], R[j][:, 64 * h:64 * h + 64], start=True, stop=True)
                    last.then_inc(solved, 1)
                for j in range(2):
                    if c:
                        pe.wait_ge(y_out, 2 * (c - 1) + j + 1)
                    nc.tensor.matmul(bank(3, j), x.r[:, j, ct], S[j], start=True, stop=False)
                    for h in range(2):
                        cols = slice(64 * h, 64 * h + 64)
                        nc.tensor.matmul(bank(3, j)[:, cols], store[:, 4 * c + 2 * j + h, 2, :], tok[j][c % 2][:, 2, cols], start=False, stop=False)
                for j in range(2):
                    pe.wait_ge(sa_out, 2 * c + j + 1)
                    nc.tensor.matmul(bank(2, j), tok[j][c % 2][:, 1, :], tok[j][c % 2][:, 2, :], start=True, stop=False)
                    nc.tensor.matmul(bank(2, j), tok[j][c % 2][:, 0, :], SA[j], start=False, stop=True).then_inc(grown, 1)
                for j in range(2):
                    for h in range(2):
                        cols = slice(64 * h, 64 * h + 64)
                        last = nc.tensor.matmul(bank(3, j)[:, cols], store[:, 4 * c + 2 * j + h, 0, :], SA[j][:, cols], start=False, stop=h == 1)
                    last.then_inc(ys, 1)

        @block.vector
        def _(dve):
            link = Chain(dve, added)
            for c in range(NT):
                for j in range(2):
                    n = 2 * c + j
                    dve.wait_ge(rs, n + 1)
                    if c:
                        dve.wait_ge(solved, n - 1)
                    nc.vector.tensor_copy(R[j], bank(1, j)).then_inc(r_out, 1)
                for j in range(2):
                    n = 2 * c + j
                    dve.wait_ge(grown, n + 1)
                    for h in range(2):
                        d = slice(64 * h, 64 * h + 64)
                        link(nc.vector.tensor_tensor(S[j][d, d], S[j][d, d], co.ps[d, 4 + j, d], ALU.add))
                        nc.vector.tensor_scalar(S[j][d, d], S[j][d, d], x.scale[d, j, c:c + 1], None, ALU.mult).then_inc(updated, 1)

        @block.scalar
        def _(act):
            def take(c):
                for j in range(2):
                    act.wait_ge(turned, 2 * c + j + 1)
                    if c >= 2:
                        act.wait_ge(ys, 2 * (c - 2) + j + 1)
                    nc.scalar.activation(tok[j][c % 2], co.ps[:, j, 0:3 * P].rearrange("p (i t) -> p i t", i=3), ACT.Copy).then_inc(tok_out, 1)

            take(0)
            for c in range(NT):
                if c + 1 < NT:
                    take(c + 1)
                for j in range(2):
                    n = 2 * c + j
                    act.wait_ge(solved, n + 1)
                    if c:
                        act.wait_ge(ys, n - 1)
                    nc.scalar.activation(SA[j], bank(2, j), ACT.Copy, scale=-1.0).then_inc(sa_out, 1)
                for j in range(2):
                    act.wait_ge(ys, 2 * c + j + 1)
                    nc.scalar.activation(x.kk[:, j, c * P:(c + 1) * P], bank(3, j), ACT.Copy).then_inc(y_out, 1)


def r7_finish(co, half, ahead=()):
    nc = co.nc
    x = R7(co, half)
    y = x.kk.rearrange("p j (g v) -> p (j g) v", v=64)
    sq = co.at(A_BIG, (32, 64))
    yt = [co.at(A_BIG + 2048 + 1024 * j, (T,)) for j in range(2)]
    mean, var, rs = (co.at(A_MISC + 680 + 32 * i, (32,)) for i in range(3))
    ident = co.at(A_CST + C_ID, (P,))
    summed, rooted, normed, turned, mapped, done, dch = (co.sem(f"r7n{half}_{y_}") for y_ in ("summed", "rooted", "normed", "turned", "mapped", "done", "dch"))
    c_ = lambda n, j: x.cols[n][:, x.b0 + j:x.b0 + j + 1]
    loaded = co.sem(f"r7n{half}_loaded")
    with nc.Block() as block:
        if ahead:
            @block.sync
            def _(sp):
                for dst, src in ahead:
                    sp.dma_start(dst, src).then_inc(loaded, 16)
                sp.wait_ge(loaded, 16 * len(ahead))

        @block.vector
        def _(dve):
            link = Chain(dve, dch)
            link(nc.vector.tensor_reduce(mean, y, AX, ALU.add))
            link(nc.vector.tensor_scalar(mean, mean, 1.0 / 64, None, ALU.mult))
            link(nc.vector.tensor_tensor(y, y, bc(mean, 64), ALU.subtract))
            link(nc.vector.tensor_tensor(sq, y, y, ALU.mult))
            nc.vector.tensor_reduce(var, sq, AX, ALU.add).then_inc(summed, 1)
            dve.wait_ge(rooted, 1)
            link(nc.vector.reciprocal(rs, rs))
            nc.vector.tensor_tensor(y, y, bc(rs, 64), ALU.mult).then_inc(normed, 1)
            for j in range(2):
                dve.wait_ge(mapped, j + 1)
                link(nc.vector.tensor_tensor(yt[j], yt[j], x.bon[:, j, :], ALU.add))
                nc.vector.tensor_tensor(x.r[:, j, :], x.zd[:, j, :], yt[j], ALU.mult).then_inc(done, 1)

        @block.scalar
        def _(act):
            act.wait_ge(summed, 1)
            nc.scalar.activation(rs, var, ACT.Sqrt, bias=co.at(co.eps_at[GN_EPS], (1,)), scale=1.0 / 64).then_inc(rooted, 1)
            for j in range(2):
                act.wait_ge(turned, j + 1)
                nc.scalar.activation(yt[j], co.ps[:, 2 * j:2 * j + 2, :].rearrange("p h t -> p (h t)"), ACT.Identity, bias=c_("ln_b", j), scale=c_("ln_w", j)).then_inc(mapped, 1)

        @block.tensor
        def _(pe):
            pe.wait_ge(normed, 1)
            for j in range(2):
                for c in range(NT):
                    last = nc.tensor.transpose(co.ps[:, 2 * j + c // 4, (c % 4) * P:(c % 4 + 1) * P], x.kk[:, j, c * P:(c + 1) * P], ident)
                last.then_inc(turned, 1)


def odd_layer(co, a, x, dst):
    nc = co.nc
    u5 = nc.dram_tensor("u_by_chunk", (W, SC8, P), F32, kind="Internal").ap()
    y5 = nc.dram_tensor("y_by_chunk", (W, SC8, P), F32, kind="Internal").ap()
    u, r, k, v, zc = ([co.at(A_F[i] + T * b, (T,)) for b in range(WB)] for i in (0, 1, 2, 3, 5))
    blocks = [(ODD["u"] + P * b, "plain", u[b]) for b in range(WB)]
    zg = nc.dram_tensor("odd_gates", (2 * WB, P, T), F32, kind="Internal").ap()
    blocks += [(ODD["zc"] + P * b, "gate", zg[b]) for b in range(WB)]
    blocks += [(ODD[n] + P * b, "shift", y[b]) for n, y in (("r", r), ("k", k), ("v", v)) for b in range(WB)]
    blocks += [(ODD["wa"], "shift", co.at(A_F[4], (T,)))]
    blocks += [(ODD["zd"] + P * b, "gate", zg[WB + b]) for b in range(WB)]
    norm_transpose(co, "on", x, a["odd_norm"][0], project_ahead(co, "op", a["odd_w_in"][0], blocks))
    project(co, "op", a["odd_w_in"][0], blocks, mu=a["rwkv_mu"][0])
    s5_store_u(co, co.at(A_F[0], (WB, T)), u5)
    s5_tables(co, a, u5, fetch=[(zc[b], zg[b]) for b in range(WB)])
    s5_toeplitz(co)
    s5_scan(co, y5)
    s5_glu(co, a["s5_d"][0], a["s5_w_glu"][0], u5, y5, zc)
    r7_start(co, a)
    for half in range(2):
        f = R7(co, half)
        rates = [(f.w2a2[64 * i:64 * i + 64, :], a[n][0]) for i, n in enumerate(("rwkv_w2", "rwkv_a2"))]
        r7_features(co, half)
        norm_blocks(co, f"rn{half}", [(f.kk[:, j, :], 64, 1.0, None) for j in range(2)], 2)
        r7_decay(co, half)
        r7_pairs(co, half)
        invert(co, f"ri{half}", store_slot(co, 1), [A_F[6] + 1024 * i for i in range(3)] + [A_F[4] + 3072],
               [A_F[6] + 3072, A_F[6] + 3584, A_T, A_T + 512], [A_T + 1024 + 512 * i for i in range(4)])
        r7_state(co, half, zg)
        r7_finish(co, half, rates if half == 0 else ())
        if half == 0:
            co.end_part()
    project_out(co, "oout", a["odd_w_out"][0], zc + r,
                [A_F[2] + 1024 * k for k in range(KT)], [A_F[0] + 1024 * k for k in range(4)] + [A_F[6] + 1024 * k for k in range(4)], x, dst, co.output_stored)


INPUTS = ["x", "even_norm", "even_w_in", "gdn_conv_w", "gdn_a_log", "gdn_dt_bias", "gdn_out_norm", "swa_q_norm", "swa_k_norm",
          "swa_sinks", "even_w_out", "rel_bias", "odd_norm", "odd_w_in", "s5_lambda_re", "s5_lambda_im", "s5_log_step",
          "s5_b_re", "s5_b_im", "s5_c_re", "s5_c_im", "s5_d", "s5_w_glu", "rwkv_mu", "rwkv_w0", "rwkv_w2", "rwkv_a0",
          "rwkv_a2", "rwkv_k_k", "rwkv_k_a", "rwkv_r_k", "rwkv_ln_w", "rwkv_ln_b", "odd_w_out"]


def build(nc, a, cst, out):
    with ExitStack() as ctx:
        co = Core(nc, ctx)
        h = nc.dram_tensor("h_between_layers", (T, D), F32, kind="Internal").ap()
        start(co, cst)
        even_layer(co, a, a["x"][0], h)
        co.end_part()
        odd_layer(co, a, h, out[0])


def kernel(**inputs):
    import concourse.bacc as bacc
    from concourse.bass_utils import run_bass_kernel_spmd

    nc = bacc.Bacc("TRN2", target_bir_lowering=False, num_devices=1)
    arrays = {f"in_{n}": np.ascontiguousarray(inputs[n]) for n in INPUTS}
    a = {n: nc.dram_tensor(f"in_{n}", arrays[f"in_{n}"].shape, F32, kind="ExternalInput").ap() for n in INPUTS}
    arrays["constants"] = constants()
    cst = nc.dram_tensor("constants", (P, C_ALL), F32, kind="ExternalInput").ap()
    out = nc.dram_tensor("out", (1, T, D), F32, kind="ExternalOutput").ap()
    build(nc, a, cst, out)
    r = run_bass_kernel_spmd(nc, [arrays], core_ids=[0])
    return r.results[0]["out"]
```
